# Optimizing a Trainium2 kernel written in Bass

```python
import math
import jax, jax.numpy as jnp
from jax import lax
import numpy as np

D_MODEL = 1024
BATCH = 1
SEQ = 512
DEPTH = 2

A_HEADS = 8
A_KV_HEADS = 2
A_HEAD_DIM = 64
A_REP = A_HEADS // A_KV_HEADS
A_WIDTH = A_HEADS * A_HEAD_DIM
WINDOW = 128
BLOCK = 128
REL_BUCKETS = 32
REL_MAX_DIST = 128
B_HEADS = 8
Q_LORA = 256
KV_LORA = 128
NOPE_DIM = 64
ROPE_DIM = 32
B_QK_DIM = NOPE_DIM + ROPE_DIM
B_V_DIM = 64
B_WIDTH = B_HEADS * B_V_DIM
ROPE_THETA = 10000.0
IN_SIZES = (A_HEADS * A_HEAD_DIM, A_KV_HEADS * A_HEAD_DIM, A_KV_HEADS * A_HEAD_DIM,
            Q_LORA, KV_LORA, ROPE_DIM, 2 * D_MODEL)
IN_COLS = sum(IN_SIZES)
N_GROUPS = 4
EXPERTS_PER_GROUP = 8
N_EXPERTS = N_GROUPS * EXPERTS_PER_GROUP
TOP_K = 2
D_EXPERT = 256
MOE_BLOCK = 128
EPS = 1e-6

kernel_name = "hybrid_swa_mla_hier_moe"

def rmsnorm(x, g):
    xf = x.astype(jnp.float32)
    y = xf * lax.rsqrt(jnp.mean(xf * xf, axis=-1, keepdims=True) + EPS)
    return (y * g.astype(jnp.float32)).astype(x.dtype)

def t5_bucket(dist):
    max_exact = REL_BUCKETS // 2
    d = jnp.maximum(dist, 0)
    ratio = jnp.maximum(d, 1).astype(jnp.float32) / max_exact
    large = max_exact + (jnp.log(ratio) / math.log(REL_MAX_DIST / max_exact)
                         * (REL_BUCKETS - max_exact)).astype(jnp.int32)
    large = jnp.minimum(large, REL_BUCKETS - 1)
    return jnp.where(d < max_exact, d, large)

def apply_rope(x, positions):
    half = ROPE_DIM // 2
    inv_freq = ROPE_THETA ** (-jnp.arange(half, dtype=jnp.float32) / half)
    ang = positions.astype(jnp.float32)[:, None] * inv_freq[None, :]
    cos = jnp.cos(ang)[None, :, None, :]
    sin = jnp.sin(ang)[None, :, None, :]
    xf = x.astype(jnp.float32)
    x1, x2 = xf[..., :half], xf[..., half:]
    out = jnp.concatenate([x1 * cos - x2 * sin, x1 * sin + x2 * cos], axis=-1)
    return out.astype(x.dtype)

def sliding_window_attention(q, k, v, sinks, rel_table):
    Bsz, S = q.shape[0], q.shape[1]
    nb = S // BLOCK
    scale = A_HEAD_DIM ** -0.5
    qb = q.reshape(Bsz, nb, BLOCK, A_KV_HEADS, A_REP, A_HEAD_DIM)

    def band(t):
        tb = t.reshape(Bsz, nb, BLOCK, A_KV_HEADS, A_HEAD_DIM)
        prev = jnp.concatenate([jnp.zeros_like(tb[:, :1]), tb[:, :-1]], axis=1)
        return jnp.concatenate([prev, tb], axis=2)

    kb, vb = band(k), band(v)
    s = jnp.einsum('bnqgrd,bnkgd->bngrqk', qb, kb).astype(jnp.float32) * scale
    qi = jnp.arange(BLOCK)[:, None]
    kj = jnp.arange(2 * BLOCK)[None, :]
    dist = qi + BLOCK - kj
    bias = rel_table[t5_bucket(dist)]
    bias = bias.astype(jnp.float32).transpose(2, 0, 1).reshape(A_KV_HEADS, A_REP, BLOCK, 2 * BLOCK)
    kpos = jnp.arange(nb)[:, None, None] * BLOCK - BLOCK + kj[None]
    mask = (dist >= 0) & (dist < WINDOW) & (kpos >= 0)
    s = jnp.where(mask[None, :, None, None], s + bias, -jnp.inf)
    sink = sinks.astype(jnp.float32).reshape(A_KV_HEADS, A_REP)[None, None, :, :, None, None]
    m = jnp.maximum(jnp.max(s, axis=-1, keepdims=True), sink)
    p = jnp.exp(s - m)
    denom = jnp.sum(p, axis=-1, keepdims=True) + jnp.exp(sink - m)
    p = (p / denom).astype(v.dtype)
    o = jnp.einsum('bngrqk,bnkgd->bnqgrd', p, vb)
    return o.reshape(Bsz, S, A_WIDTH)

def causal_block_attention(q, k, v):
    Bsz, S, H, dq = q.shape
    nb = S // BLOCK
    scale = dq ** -0.5
    qblocks = q.reshape(Bsz, nb, BLOCK, H, dq).transpose(1, 0, 2, 3, 4)
    kpos = jnp.arange(S)

    def one_block(args):
        qb, n = args
        s = jnp.einsum('bqhd,bkhd->bhqk', qb, k).astype(jnp.float32) * scale
        qpos = n * BLOCK + jnp.arange(BLOCK)
        s = jnp.where(kpos[None, :] <= qpos[:, None], s, -jnp.inf)
        p = jax.nn.softmax(s, axis=-1).astype(v.dtype)
        return jnp.einsum('bhqk,bkhd->bqhd', p, v)

    o = lax.map(one_block, (qblocks, jnp.arange(nb)))
    return o.transpose(1, 0, 2, 3, 4).reshape(Bsz, S, H * v.shape[-1])

def mixer_block(x, attn_norm, w_in, b_gate, a_q_norm, a_k_norm, a_sinks, rel_table, w_oa,
                q_a_norm, w_qb, kv_a_norm, w_kvb, b_q_norm, b_k_norm, w_ob, w_o, positions):
    Bsz, S, _ = x.shape
    h = rmsnorm(x, attn_norm)
    proj = h @ w_in
    cuts = [int(c) for c in np.cumsum(IN_SIZES)[:-1]]
    qa, ka, va, cq, ckv, kpe, glog = jnp.split(proj, cuts, axis=-1)

    qa = rmsnorm(qa.reshape(Bsz, S, A_HEADS, A_HEAD_DIM), a_q_norm)
    ka = rmsnorm(ka.reshape(Bsz, S, A_KV_HEADS, A_HEAD_DIM), a_k_norm)
    va = va.reshape(Bsz, S, A_KV_HEADS, A_HEAD_DIM)
    ya = sliding_window_attention(qa, ka, va, a_sinks, rel_table) @ w_oa

    qb = (rmsnorm(cq, q_a_norm) @ w_qb).reshape(Bsz, S, B_HEADS, B_QK_DIM)
    kv = (rmsnorm(ckv, kv_a_norm) @ w_kvb).reshape(Bsz, S, B_HEADS, NOPE_DIM + B_V_DIM)
    k_nope, vb = kv[..., :NOPE_DIM], kv[..., NOPE_DIM:]
    k_pe = jnp.broadcast_to(kpe[:, :, None, :], (Bsz, S, B_HEADS, ROPE_DIM))
    kb = jnp.concatenate([k_nope, k_pe], axis=-1)
    qb = rmsnorm(qb, b_q_norm)
    kb = rmsnorm(kb, b_k_norm)
    qb = jnp.concatenate([qb[..., :NOPE_DIM], apply_rope(qb[..., NOPE_DIM:], positions)], axis=-1)
    kb = jnp.concatenate([kb[..., :NOPE_DIM], apply_rope(kb[..., NOPE_DIM:], positions)], axis=-1)
    yb = causal_block_attention(qb, kb, vb) @ w_ob

    gates = jax.nn.sigmoid((glog + b_gate).astype(jnp.float32)).astype(x.dtype)
    ga, gb = gates[..., :D_MODEL], gates[..., D_MODEL:]
    return (ga * ya + gb * yb) @ w_o

def hier_moe(h, w_rg, b_rg, w_re, b_re, w_gate, w_up, w_down):
    Bsz, S, D = h.shape
    T = Bsz * S
    A = T * TOP_K
    xf = h.reshape(T, D)
    g_prob = jax.nn.softmax((xf @ w_rg + b_rg).astype(jnp.float32), axis=-1)
    g_p, g_idx = lax.top_k(g_prob, 1)
    e_logits = (xf @ w_re + b_re).astype(jnp.float32).reshape(T, N_GROUPS, EXPERTS_PER_GROUP)
    e_in_group = e_logits[jnp.arange(T), g_idx[:, 0]]
    e_top, e_loc = lax.top_k(e_in_group, TOP_K)
    weights = g_p * jax.nn.softmax(e_top, axis=-1)
    expert = g_idx * EXPERTS_PER_GROUP + e_loc

    flat_e = expert.reshape(A)
    flat_w = weights.reshape(A)
    flat_t = jnp.repeat(jnp.arange(T, dtype=jnp.int32), TOP_K)
    order = jnp.argsort(flat_e)
    se, st, sw = flat_e[order], flat_t[order], flat_w[order]
    counts = jnp.zeros((N_EXPERTS,), jnp.int32).at[flat_e].add(1)
    starts = jnp.cumsum(counts) - counts
    padded = ((counts + MOE_BLOCK - 1) // MOE_BLOCK) * MOE_BLOCK
    pends = jnp.cumsum(padded)
    pstarts = pends - padded
    dest = pstarts[se] + (jnp.arange(A, dtype=jnp.int32) - starts[se])
    n_rows = A + N_EXPERTS * MOE_BLOCK
    n_blocks = n_rows // MOE_BLOCK
    row_tok = jnp.zeros((n_rows,), jnp.int32).at[dest].set(st)
    row_w = jnp.zeros((n_rows,), jnp.float32).at[dest].set(sw)
    blk_exp = jnp.minimum(jnp.searchsorted(pends, jnp.arange(n_blocks) * MOE_BLOCK, side='right'),
                          N_EXPERTS - 1)
    xr = xf[row_tok].reshape(n_blocks, MOE_BLOCK, D)

    def expert_block(args):
        xb, e = args
        return (jax.nn.silu(xb @ w_gate[e]) * (xb @ w_up[e])) @ w_down[e]

    yr = lax.map(expert_block, (xr, blk_exp)).reshape(n_rows, D)
    y = jax.ops.segment_sum(yr * row_w[:, None].astype(yr.dtype), row_tok, num_segments=T)
    return y.reshape(Bsz, S, D)

def setup_inputs(seed: int = 0) -> dict:
    key = jax.random.key(seed)
    ks = jax.random.split(key, 32)

    def nrm(k, shape, scale):
        return jax.random.normal(k, shape, jnp.float32) * scale

    def gain(k, shape):
        return 1.0 + 0.02 * jax.random.normal(k, shape, jnp.float32)

    L = DEPTH
    return {
        "x": nrm(ks[0], (BATCH, SEQ, D_MODEL), 1.0),
        "attn_norm": gain(ks[1], (L, D_MODEL)),
        "w_in": nrm(ks[2], (L, D_MODEL, IN_COLS), D_MODEL ** -0.5),
        "b_gate": nrm(ks[3], (L, 2 * D_MODEL), 0.02),
        "a_q_norm": gain(ks[4], (L, A_HEAD_DIM)),
        "a_k_norm": gain(ks[5], (L, A_HEAD_DIM)),
        "a_sinks": nrm(ks[6], (L, A_HEADS), 0.5),
        "rel_bias": nrm(ks[7], (REL_BUCKETS, A_HEADS), 0.5),
        "w_oa": nrm(ks[8], (L, A_WIDTH, D_MODEL), A_WIDTH ** -0.5),
        "q_a_norm": gain(ks[9], (L, Q_LORA)),
        "w_qb": nrm(ks[10], (L, Q_LORA, B_HEADS * B_QK_DIM), Q_LORA ** -0.5),
        "kv_a_norm": gain(ks[11], (L, KV_LORA)),
        "w_kvb": nrm(ks[12], (L, KV_LORA, B_HEADS * (NOPE_DIM + B_V_DIM)), KV_LORA ** -0.5),
        "b_q_norm": gain(ks[13], (L, B_QK_DIM)),
        "b_k_norm": gain(ks[14], (L, B_QK_DIM)),
        "w_ob": nrm(ks[15], (L, B_WIDTH, D_MODEL), B_WIDTH ** -0.5),
        "w_o": nrm(ks[16], (L, D_MODEL, D_MODEL), D_MODEL ** -0.5),
        "ffn_norm": gain(ks[17], (L, D_MODEL)),
        "w_router_group": nrm(ks[18], (L, D_MODEL, N_GROUPS), D_MODEL ** -0.5),
        "b_router_group": nrm(ks[19], (L, N_GROUPS), 0.01),
        "w_router_expert": nrm(ks[20], (L, D_MODEL, N_EXPERTS), D_MODEL ** -0.5),
        "b_router_expert": nrm(ks[21], (L, N_EXPERTS), 0.01),
        "w_exp_gate": nrm(ks[22], (L, N_EXPERTS, D_MODEL, D_EXPERT), D_MODEL ** -0.5),
        "w_exp_up": nrm(ks[23], (L, N_EXPERTS, D_MODEL, D_EXPERT), D_MODEL ** -0.5),
        "w_exp_down": nrm(ks[24], (L, N_EXPERTS, D_EXPERT, D_MODEL), D_EXPERT ** -0.5),
    }

def reference(x, attn_norm, w_in, b_gate, a_q_norm, a_k_norm, a_sinks, rel_bias, w_oa,
              q_a_norm, w_qb, kv_a_norm, w_kvb, b_q_norm, b_k_norm, w_ob, w_o,
              ffn_norm, w_router_group, b_router_group, w_router_expert, b_router_expert,
              w_exp_gate, w_exp_up, w_exp_down):
    positions = jnp.arange(x.shape[1], dtype=jnp.int32)
    for l in range(DEPTH):
        x = x + mixer_block(x, attn_norm[l], w_in[l], b_gate[l], a_q_norm[l], a_k_norm[l],
                            a_sinks[l], rel_bias, w_oa[l], q_a_norm[l], w_qb[l], kv_a_norm[l],
                            w_kvb[l], b_q_norm[l], b_k_norm[l], w_ob[l], w_o[l], positions)
        x = x + hier_moe(rmsnorm(x, ffn_norm[l]), w_router_group[l], b_router_group[l],
                         w_router_expert[l], b_router_expert[l],
                         w_exp_gate[l], w_exp_up[l], w_exp_down[l])
    return x


_drawn_inputs = setup_inputs


def setup_inputs(seed=0):
    import zlib

    import numpy as np

    out = dict(_drawn_inputs(seed))
    spreads = {}
    factors = {'attn_norm': 2.769,
     'b_gate': 3.702,
     'a_q_norm': 3.043,
     'a_k_norm': 2.885,
     'a_sinks': 19.032,
     'q_a_norm': 4.365,
     'kv_a_norm': 3.696,
     'b_q_norm': 4.803,
     'b_k_norm': 2.84,
     'b_router_expert': 2.765,
     'b_router_group': 6.202}
    for name, (base, spread) in spreads.items():
        noise = np.random.default_rng([zlib.crc32(name.encode()), seed]).standard_normal(out[name].shape)
        drawn = base * np.exp(spread * noise) if base else spread * noise
        out[name] = __import__('jax').numpy.asarray(drawn.astype(out[name].dtype))
    for name, factor in factors.items():
        out[name] = (out[name] * factor).astype(out[name].dtype)
    return out
```

```python
import math
from contextlib import ExitStack

import numpy as np

import concourse.bass as bass
from concourse import mybir

F32 = mybir.dt.float32
BF16 = mybir.dt.bfloat16
I32 = mybir.dt.int32
ALU = mybir.AluOpType
ACT = mybir.ActivationFunctionType
AX = mybir.AxisListType.X

P = 128
D = 1024
T = 512
TT = T // P
KD = D // P
L = 2
AH, AKV, AD = 8, 2, 64
WINDOW = 128
BUCKETS, MAX_DIST = 32, 128
BH, QL, KVL, NOPE, ROPE, VD = 8, 256, 128, 64, 32, 64
QK = NOPE + ROPE
THETA = 10000.0
GROUPS, PER_GROUP = 4, 8
EXP = GROUPS * PER_GROUP
FE = 256
EPS = 1e-6
A_SCALE = AD ** -0.5
B_SCALE = QK ** -0.5
NEG = -1e30

C_KPE = 1152
C_GATE = 1184
GROUP_N = 512

SLOTS = 64
ROUNDS = T // SLOTS
UNROLL = 4
TURNS = EXP // UNROLL
EXTRA = UNROLL
PAD = 4096
CREDIT = UNROLL

CONST = {}
_at = 0
for _name, _n in (("ident", P), ("causal", P), ("before", P), ("ones", P), ("cos", TT * ROPE // 2),
                  ("sin", TT * ROPE // 2), ("iota4", GROUPS), ("iota8", PER_GROUP), ("iota32", EXP),
                  ("half", 1), ("rowid", 2 * TT)):
    CONST[_name] = (_at, _n)
    _at += _n
N_CONST = _at
BIAS_W = 384


def constants():
    c = np.zeros((P, N_CONST), np.float32)

    def put(name, v):
        a, n = CONST[name]
        c[:, a:a + n] = v

    i = np.arange(P)
    put("ident", np.eye(P))
    put("causal", np.where(i[None, :] <= i[:, None], 0.0, NEG))
    put("before", i[:, None] < i[None, :])
    put("ones", 1.0)
    half = ROPE // 2
    freq = np.float32(THETA) ** (-np.arange(half, dtype=np.float32) / np.float32(half))
    ang = np.arange(T, dtype=np.float32)[:, None] * freq[None, :]
    fold = lambda a: a.reshape(TT, P, half).transpose(1, 0, 2).reshape(P, TT * half)
    put("cos", fold(np.cos(ang)))
    put("sin", fold(np.sin(ang)))
    put("iota4", np.arange(GROUPS))
    put("iota8", np.arange(PER_GROUP))
    put("iota32", np.arange(EXP))
    put("half", (i >= SLOTS)[:, None])
    rows = 2 * (i[:, None, None] + P * np.arange(TT)[None, :, None]) + np.arange(2)[None, None, :]
    put("rowid", rows.reshape(P, 2 * TT))
    hot = np.zeros((BUCKETS + 1, BIAS_W), np.float32)
    exact = BUCKETS // 2
    for col in range(BIAS_W - 1):
        d = 2 * P - 1 - col
        if 0 <= d < WINDOW:
            ratio = np.float32(max(d, 1)) / np.float32(exact)
            large = exact + int(np.log(ratio) / np.float32(math.log(MAX_DIST / exact))
                                * np.float32(BUCKETS - exact))
            hot[d if d < exact else min(large, BUCKETS - 1), col] = 1.0
        else:
            hot[BUCKETS, col] = NEG
    return c, hot


class Chain:

    def __init__(self, eng, sem):
        self.eng, self.sem, self.n = eng, sem, 0

    def step(self, ins):
        ins.then_inc(self.sem, 1)
        self.n += 1
        self.eng.wait_ge(self.sem, self.n)


def trunk(nc, x, attn_norm, w_in, b_gate, a_q_norm, a_k_norm, a_sinks, rel_bias, w_oa, q_a_norm,
          w_qb, kv_a_norm, w_kvb, b_q_norm, b_k_norm, w_ob, w_o, ffn_norm, w_rg, b_rg, w_re, b_re,
          w_gate, w_up, w_down, consts, hot, out):
    h_dram = nc.dram_tensor("h_rows", (2 * T, D // 2), F32).ap()
    y_dram = nc.dram_tensor("y_rows", (4 * T, D // 2), F32).ap()
    table = nc.dram_tensor("slot_table", (T * EXP, 1), I32).ap()
    bias_dram = nc.dram_tensor("bias_rows", (AH, P, BIAS_W), F32).ap()

    with ExitStack() as ctx:
        base = (nc.sbuf_base + 63) // 64 * 64

        def at(name, shape, dt, off):
            return nc.alloc_sbuf_tensor_at(name, shape, dt, offset=base + off)

        K = 1024
        ring = at("ring", [P, 24 * K], F32, 0)
        qkT = at("qkT", [P, 2 * BH, T], F32, 64 * K)
        X = at("x_rows", [P, TT, D], F32, 96 * K)
        hT = at("hT", [P, KD, T], F32, 112 * K)
        yld = at("y_loaded", [P, 2, 2, D], F32, 112 * K)
        oaT = at("oaT", [P, 4, T], F32, 128 * K)
        obT = at("obT", [P, 4, T], F32, 136 * K)
        rope_t = at("rope_tmp", [P, 4, 2 * BH, ROPE // 2], F32, 136 * K)
        vB = at("vB", [P, TT, BH * VD], F32, 144 * K)
        cqT = at("cqT", [P, 2, T], F32, 152 * K)
        ckvT = at("ckvT", [P, T], F32, 156 * K)
        qTA = at("qTA", [P, 4, T], F32, 158 * K)
        kTA = at("kTA", [P, T], F32, 166 * K)
        vA = at("vA", [P, TT, P], F32, 168 * K)
        sig = at("sig", [P, 2, 2, T], F32, 158 * K)
        xn = at("xn", [P, TT, D], F32, 170 * K)
        sq = at("sq", [P, 2, T], F32, 170 * K)
        qn = at("qn", [P, 2, T], F32, 174 * K)
        qk = at("qk_rows", [P, 2, 2 * BH, QK], F32, 170 * K)
        sq2 = at("sq2", [P, 2 * BH, QK], F32, 182 * K)
        pr = at("probs", [P, 4, T], F32, 170 * K)
        pT = at("probsT", [P, 4, T], F32, 178 * K)
        mT = at("mergedT", [P, KD, T], F32, 170 * K)
        gath = at("gathered", [P, UNROLL, T], F32, 170 * K)
        xeT = at("xeT", [P, 2, 4, P], F32, 178 * K)
        gtmp = at("gu_half", [P, 2, T], F32, 182 * K)
        gsum = at("gu", [P, T], F32, 186 * K)
        gsum2 = at("gu2", [P, T], F32, 144 * K)
        gexp = at("silu_tmp", [P, 2, FE], F32, 146 * K)
        hrow = at("h_expert", [P, 2, FE], F32, 148 * K)
        heT = at("heT", [P, 2, 2, SLOTS], F32, 150 * K)
        ye = at("y_expert", [P, UNROLL, T], F32, 128 * K)
        h2 = at("h2_rows", [P, 2, D], F32, 136 * K)
        lgT = at("logitsT", [GROUPS + EXP, T], F32, 152 * K)
        gu_rows = [gsum, gsum2]
        bias = at("bias", [P, AH, 2 * P], F32, 188 * K)
        misc = 196 * K
        sizes = {}

        def small(name, shape, dt=F32):
            nonlocal misc
            n = 1
            for s in shape[1:]:
                n *= s
            t = at(name, shape, dt, misc)
            misc += (n * mybir.dt.size(dt) + 31) // 32 * 32
            return t

        cst = small("cst", [P, N_CONST])
        causal_bf = small("causal_bf", [P, P], BF16)
        ident_bf = small("ident_bf", [P, P], BF16)
        before_bf = small("before_bf", [P, P], BF16)
        ones_bf = small("ones_bf", [P, P], BF16)
        minus_half = small("minus_half", [P, 48])
        colrows = at("colrows", [28, P], F32, 170 * K + 17 * K)
        cols = small("cols", [P, 28])
        nbg = small("neg_b_gate", [P, 16])
        gainA = small("gainA", [P, 2, AD])
        gainB = small("gainB", [P, 2, QK])
        nsink = small("neg_sink", [P, AH])
        rbias = small("router_bias", [P, GROUPS + EXP])
        kpe = small("kpe", [P, TT, ROPE])
        stats = small("stats", [P, 64])
        st1 = small("st1", [P, 12, 9])
        idx_g = small("idx_gather", [P, EXP + EXTRA], I32)
        idx_s = small("idx_scatter", [P, EXP + EXTRA], I32)
        cur_g = small("cur_gather", [P, UNROLL], I32)
        cur_s = small("cur_scatter", [P, UNROLL], I32)
        wts = small("weights", [P, 2, TT])
        slots_i = small("slots", [P, 2 * TT], I32)
        rowid_i = small("rowid_i", [P, 2 * TT], I32)
        cmax = small("count_max", [P, 1], I32)
        assert base + misc <= nc.sbuf_usable_end, (base + misc, nc.sbuf_usable_end)
        wr = at("w_router", [P, KD, GROUPS + EXP], F32, 156 * K)
        gffn = at("gain_ffn", [P, D], F32, 188 * K)
        unit = at("unit_stats", [P, 48, 8], F32, 186 * K)
        rt = at("routing", [P, 2048], F32, 178 * K)
        pre_rel = at("rel_rows", [BUCKETS + 1, AH], F32, 170 * K)
        pre_hot = at("hot_rows", [BUCKETS + 1, BIAS_W], F32, 171 * K)
        pre_bias = at("bias_sb", [AH, BIAS_W], F32, 173 * K)
        padt = small("pad_table", [P, P], I32)
        assert base + misc <= nc.sbuf_usable_end, (base + misc, nc.sbuf_usable_end)

        def C(name):
            a, n = CONST[name]
            return cst[:, a:a + n]

        ident = C("ident")
        cosv = C("cos").rearrange("p (t c) -> p t c", t=TT)
        sinv = C("sin").rearrange("p (t c) -> p t c", t=TT)

        bank = [ctx.enter_context(nc.psum_tensor(f"bank{i}", [P, 512], F32)) for i in range(8)]

        def slot(s, n=4096, off=0):
            return ring[:, s * 4096 + off:s * 4096 + off + n]

        EXP_OFF = [3 * 4096, 3 * 4096 + 6144, 0, 6144]

        pre_dma, pre_c, pre_b, pre_v, pre_w = (ctx.enter_context(nc.semaphore(n)) for n in
                                        ("pre_dma", "pre_consts", "pre_bias", "pre_vec", "pre_store"))
        with nc.Block() as block:
            @block.sync
            def _(sp):
                sp.dma_start(cst[:, :], consts).then_inc(pre_dma, 16)
                sp.dma_start(X[:, :, :], x[0].rearrange("(t p) d -> p t d", p=P)).then_inc(pre_dma, 16)
                sp.dma_start(pre_hot[:, :], hot).then_inc(pre_dma, 16)
                sp.dma_start(pre_rel[0:BUCKETS, :], rel_bias).then_inc(pre_dma, 16)
                sp.wait_ge(pre_v, 6)
                sp.dma_start(bias_dram, pre_bias[:, :].unsqueeze(1).broadcast_to([AH, P, BIAS_W])).then_inc(pre_w, 16)
                sp.wait_ge(pre_w, 16)

            @block.vector
            def _(dve):
                dve.memset(pre_rel[BUCKETS:BUCKETS + 1, :], 1.0).then_inc(pre_c, 1)
                dve.memset(minus_half[:, :], -0.5).then_inc(pre_c, 1)
                dve.memset(padt[:, :], PAD).then_inc(pre_c, 1)
                dve.memset(idx_g[:, :], PAD).then_inc(pre_c, 1)
                dve.memset(idx_s[:, :], PAD).then_inc(pre_c, 1)
                dve.wait_ge(pre_dma, 64)
                dve.tensor_copy(causal_bf[:, :], C("causal")).then_inc(pre_v, 1)
                dve.tensor_copy(ident_bf[:, :], ident).then_inc(pre_v, 1)
                dve.tensor_copy(before_bf[:, :], C("before")).then_inc(pre_v, 1)
                dve.tensor_copy(ones_bf[:, :], C("ones")).then_inc(pre_v, 1)
                dve.tensor_copy(rowid_i[:, :], C("rowid")).then_inc(pre_v, 1)
                dve.wait_ge(pre_b, 1)
                dve.tensor_copy(pre_bias[:, :], bank[0][0:AH, 0:BIAS_W]).then_inc(pre_v, 1)

            @block.tensor
            def _(pe):
                pe.wait_ge(pre_dma, 64)
                pe.wait_ge(pre_c, 1)
                pe.matmul(bank[0][0:AH, 0:BIAS_W], pre_rel[:, :], pre_hot[:, :],
                          start=True, stop=True).then_inc(pre_b, 1)

        names = []

        def sem(name):
            s = ctx.enter_context(nc.semaphore(name))
            names.append(s)
            return s

        WCH = ["c0", "c1", "c2", "woa", "wob", "g0", "g2", "g1", "g3", "wo0", "wo1"]
        w_in_dma = {n: sem(f"loaded_{n}") for n in WCH}
        ring_free = sem("ring_free")
        small_ld = sem("small_loaded")
        late_ld = sem("late_loaded")
        x_sq, rs_x, xn_ok, hT_ps, hT_ok = (sem(n) for n in ("x_sq", "rs_x", "xn_ok", "hT_ps", "hT_ok"))
        cols_ps, cols_ok = sem("cols_ps"), sem("cols_ok")
        pj, pj_act, pj_ss, pj_rs, pj_dve, qn_ok, tpj, tp_read = (sem(n) for n in (
            "proj", "proj_act", "proj_sums", "proj_rstd", "proj_dve", "qn_ok", "proj_T", "proj_T_read"))
        p2, p2_act, p2_dve, p2_kpe, p2_sq, p2_ss, p2_rs, p2_g, p2_rope, p2_tp, p2_te = (sem(n) for n in (
            "mla", "mla_act", "mla_dve", "mla_kpe", "mla_sq", "mla_sums", "mla_rstd", "mla_gain",
            "mla_rope", "mla_T", "mla_T_read"))
        sc, mx, ex, pn, tp, te, pv, pvu, oe = (sem(n) for n in (
            "scores", "maxima", "exps", "probs_ok", "probsT_ps", "probsT_ok", "pv_group", "pv_unit", "o_read"))
        gates_ps, ge, y_ps, mg = (sem(n) for n in ("gates_ps", "gate_exp", "y_ps", "merged"))
        wo_ps, xw = sem("wo_ps"), sem("x_mixed")
        f_sq, f_rs, h2_ok, h2t_ps, h2T_ok, lg_ps, lt_ok, lgt = (sem(n) for n in (
            "f_sq", "f_rstd", "h2_ok", "h2T_ps", "h2T_ok", "logitsT_ps", "logitsT_ok", "logits_ps"))
        h2_dma = [sem(f"h2_stored{i}") for i in range(2)]
        r_exp_in, r_exp_out, onehots, ranks, slots_ok, counts_ok, wts_ok = (sem(n) for n in (
            "r_exp_in", "r_exp_out", "onehots", "ranks", "slots_ok", "counts_ok", "weights_ok"))
        tbl_init, tbl_sc, tbl_ld, idx_ok = (sem(n) for n in (
            "table_init", "table_scattered", "table_loaded", "idx_ok"))
        wfree = [sem(f"expert_free{j}") for j in range(UNROLL)]
        wload = [sem(f"expert_loaded{j}") for j in range(UNROLL)]
        gdma = [sem(f"gathered{j}") for j in range(UNROLL)]
        sdma = [sem(f"scattered{j}") for j in range(UNROLL)]
        cg, cs_, xtp, xte, gu, gcp, gsm, gex, g1_, g2_, g3_, hh, htp, hte, yp, yev = (sem(n) for n in (
            "cur_g", "cur_s", "e_xT_ps", "e_xT_ok", "e_gu_ps", "e_gu_half", "e_gu_ok", "e_exp", "e_den",
            "e_recip", "e_silu", "e_h", "e_hT_ps", "e_hT_ok", "e_y_ps", "e_y_ok"))
        moe_done = sem("moe_done")
        yl = [sem(f"y_loaded{i}") for i in range(2)]
        comb = sem("combined")
        dch, ach, pch = sem("dve_chain"), sem("act_chain"), sem("pool_chain")
        gath_ok = sem("gather_cleared")
        passed = sem("pool_passed")
        y_free = sem("y_expert_free")
        sem_range = range(names[0].num, names[-1].num + 1)
        assert len(sem_range) == len(names)

        UNITS = [("A", n, g, jj) for n in range(TT) for g in range(AKV) for jj in range(2)] + \
                [("B", h, n, 0) for h in range(BH) for n in range(TT)]
        NU = len(UNITS)
        GROUP_OF = [u // 4 if u < 16 else 4 + (u - 16) // 8 for u in range(NU)]
        LAST_OF = [u == NU - 1 or GROUP_OF[u] != GROUP_OF[u + 1] for u in range(NU)]

        with nc.Fori(0, L) as l:
            with nc.Block() as block:
                @block.sync
                def _(sp):
                    def w_in_cols(a, n):
                        return w_in[l].rearrange("(k p) n -> p k n", p=P)[:, :, a:a + n]

                    def k_view(s, n, off=0, k=KD):
                        return slot(s, k * n, off).rearrange("p (k n) -> p k n", k=k)

                    def load(name, *pairs):
                        for dst, src in pairs:
                            sp.dma_start(dst, src).then_inc(w_in_dma[name], 16)

                    load("c0", (k_view(0, 512), w_in_cols(0, 512)))
                    load("c1", (k_view(1, 512), w_in_cols(512, 512)))
                    load("c2", (k_view(2, 160), w_in_cols(1024, 160)),
                         (k_view(2, BH * QK, 1280, 2), w_qb[l].rearrange("(k p) n -> p k n", p=P)),
                         (slot(2, 1024, 2816), w_kvb[l]))
                    oa = w_oa[l].rearrange("(g j d) n -> g d j n", g=2, j=4)
                    load("woa", *[(k_view(3, 1024, 0, 4)[g * AD:(g + 1) * AD], oa[g]) for g in range(2)])
                    sp.wait_ge(ring_free, 1)
                    load("wob", (k_view(0, 1024, 0, 4), w_ob[l].rearrange("(k p) n -> p k n", p=P)))
                    sp.wait_ge(ring_free, 2)
                    load("g0", (k_view(1, 512), w_in_cols(C_GATE, 512)))
                    sp.wait_ge(ring_free, 3)
                    load("g2", (k_view(2, 512), w_in_cols(C_GATE + 1024, 512)))
                    sp.wait_ge(ring_free, 4)
                    load("g1", (k_view(4, 512), w_in_cols(C_GATE + 512, 512)))
                    load("g3", (k_view(5, 512), w_in_cols(C_GATE + 1536, 512)))
                    sp.wait_ge(ring_free, 5)
                    wo_v = w_o[l].rearrange("(k p) n -> p k n", p=P)
                    load("wo0", (k_view(1, 512), wo_v[:, :, 0:512]))
                    load("wo1", (k_view(2, 512), wo_v[:, :, 512:1024]))
                    sp.wait_ge(mg, 1)
                    sp.dma_start(wr[:, :, 0:GROUPS], w_rg[l].rearrange("(k p) n -> p k n", p=P)).then_inc(late_ld, 16)
                    sp.dma_start(wr[:, :, GROUPS:], w_re[l].rearrange("(k p) n -> p k n", p=P)).then_inc(late_ld, 16)
                    sp.dma_start(gffn[:, :], ffn_norm[l].unsqueeze(0).broadcast_to([P, D])).then_inc(late_ld, 16)

                    def load_expert(e, j, use):
                        sp.wait_ge(wfree[j], use + 1)
                        o = EXP_OFF[j]
                        for k, w in enumerate((w_gate, w_up)):
                            sp.dma_start(ring[:, o + 2048 * k:o + 2048 * (k + 1)].rearrange("p (n c) -> p n c", n=2),
                                         w[l, e].rearrange("(n p j) f -> p n (j f)", n=2, j=4)).then_inc(wload[j], 16)
                        sp.dma_start(ring[:, o + 4096:o + 6144],
                                     w_down[l, e].rearrange("(p k) n -> p (k n)", k=2)).then_inc(wload[j], 16)

                    def turns(rnd):
                        with sp.Fori(0, TURNS) as i:
                            for j in range(UNROLL):
                                load_expert(i * UNROLL + j, j, rnd * TURNS + i)

                    turns(0)
                    sp.wait_ge(counts_ok, 1)
                    most = sp.value_load(cmax[0:1, 0:1], min_val=0, max_val=T)
                    with sp.Fori(1, ROUNDS) as rnd:
                        with sp.If(most > rnd * SLOTS):
                            turns(rnd)
                    sp.wait_ge(moe_done, 1)
                    yv = y_dram.rearrange("(t p k h) c -> t p k (h c)", p=P, k=2, h=2)
                    for tt in range(TT):
                        if tt >= 2:
                            sp.wait_ge(comb, tt - 1)
                        sp.dma_start(yld[:, tt % 2], yv[tt]).then_inc(yl[tt % 2], 16)
                    for tt in range(TT):
                        sp.wait_ge(yl[tt % 2], 16 * (tt // 2 + 1))

                @block.scalar
                def _(act):
                    for dst, src in (
                        (colrows[0:8, :], attn_norm[l].rearrange("(k p) -> k p", p=P)),
                        (colrows[8:24, :], b_gate[l].rearrange("(k p) -> k p", p=P)),
                        (colrows[24:26, :], q_a_norm[l].rearrange("(k p) -> k p", p=P)),
                        (colrows[26:27, :], kv_a_norm[l].unsqueeze(0)),
                        (gainA[:, 0, :], a_q_norm[l].unsqueeze(0).broadcast_to([P, AD])),
                        (gainA[:, 1, :], a_k_norm[l].unsqueeze(0).broadcast_to([P, AD])),
                        (gainB[:, 0, :], b_q_norm[l].unsqueeze(0).broadcast_to([P, QK])),
                        (gainB[:, 1, :], b_k_norm[l].unsqueeze(0).broadcast_to([P, QK])),
                        (nsink[:, :], a_sinks[l].unsqueeze(0).broadcast_to([P, AH])),
                        (rbias[:, 0:GROUPS], b_rg[l].unsqueeze(0).broadcast_to([P, GROUPS])),
                        (rbias[:, GROUPS:], b_re[l].unsqueeze(0).broadcast_to([P, EXP])),
                        (bias[:, :, :], bass.AP(bias_dram.tensor, P - 1, [[BIAS_W - 1, P], [P * BIAS_W, AH], [1, 2 * P]])),
                    ):
                        act.dma_start(dst, src).then_inc(small_ld, 16)
                    for tt in range(TT):
                        act.activation(hT[:, 2 * tt:2 * tt + 2, :], X[:, tt, :].rearrange("p (a b) -> p a b", a=2),
                                       ACT.Square, accum_out=stats[:, tt:tt + 1]).then_inc(x_sq, 1)

                    for i in range(3 * TT):
                        c, tt = divmod(i, TT)
                        b = bank[i % 4]
                        act.wait_ge(pj, i + 1)
                        if i >= 2:
                            act.wait_ge(pj_ss, i - 1)
                        if i == 0:
                            act.wait_ge(hT_ps, 8)
                        if c == 0:
                            act.activation(sq[:, i % 2, :], b[:, :], ACT.Square).then_inc(pj_act, 1)
                        elif c == 1:
                            act.activation(sq[:, i % 2, 0:P], b[:, 0:P], ACT.Square)
                            act.activation(sq[:, i % 2, QL:2 * QL], b[:, QL:2 * QL], ACT.Square,
                                           accum_out=st1[:, i, 8:9])
                            act.activation(vA[:, tt, :], b[:, P:2 * P], ACT.Copy).then_inc(pj_act, 1)
                        else:
                            act.activation(sq[:, i % 2, 0:KVL], b[:, 0:KVL], ACT.Square,
                                           accum_out=st1[:, i, 8:9])
                            act.activation(kpe[:, tt, :], b[:, KVL:KVL + ROPE], ACT.Copy).then_inc(pj_act, 1)

                    def mla_T(tt):
                        for b in range(4):
                            act.wait_ge(p2_tp, 4 * tt + b + 1)
                            act.activation(qkT[0:QK, 4 * b:4 * b + 4, tt * P:(tt + 1) * P],
                                           bank[4 + b][0:QK, :].rearrange("p (h q) -> p h q", h=4),
                                           ACT.Copy).then_inc(p2_te, 1)

                    for tt in range(TT):
                        act.wait_ge(p2, tt + 1)
                        if tt == 0:
                            act.wait_ge(tpj, 12)
                            act.wait_ge(pj_ss, 12)
                        if tt >= 2:
                            act.wait_ge(p2_tp, 4 * (tt - 1))
                        for b in range(2):
                            kv = bank[2 + b][:, :].rearrange("p (h d) -> p h d", h=4)
                            act.activation(qk[:, tt % 2, BH + 4 * b:BH + 4 * b + 4, 0:NOPE], kv[:, :, 0:NOPE], ACT.Copy)
                            ins = act.activation(vB[:, tt, 4 * b * VD:4 * (b + 1) * VD].rearrange("p (h d) -> p h d", h=4),
                                                 kv[:, :, NOPE:], ACT.Copy)
                        ins.then_inc(p2_act, 1)
                        act.wait_ge(p2_act, tt + 1)
                        act.wait_ge(p2_dve, tt + 1)
                        act.wait_ge(p2_kpe, tt + 1)
                        if tt >= 1:
                            act.wait_ge(p2_ss, tt)
                        act.activation(sq2[:, :, :], qk[:, tt % 2, :, :], ACT.Square).then_inc(p2_sq, 1)
                        if tt >= 1:
                            mla_T(tt - 1)
                    mla_T(TT - 1)

                    def exp_unit(u):
                        kind, a, b_, c_ = UNITS[u]
                        act.wait_ge(mx, u + 1)
                        if kind == "A":
                            w = P if a == 0 else 2 * P
                            for hh in range(2):
                                act.activation(pr[:, u % 4, hh * w:(hh + 1) * w], pr[:, u % 4, hh * w:(hh + 1) * w],
                                               ACT.Exp, bias=unit[:, u, hh:hh + 1], accum_out=unit[:, u, 4 + hh:5 + hh])
                            act.activation(unit[:, u, 6:8], unit[:, u, 2:4], ACT.Exp).then_inc(ex, 1)
                        else:
                            w = P * (b_ + 1)
                            if u >= 4:
                                act.wait_ge(tp, u - 3)
                            act.activation(pr[:, u % 4, 0:w], bank[u % 4][:, 0:w], ACT.Exp, bias=unit[:, u, 0:1],
                                           scale=B_SCALE, accum_out=unit[:, u, 4:5]).then_inc(ex, 1)

                    def probsT(u):
                        act.wait_ge(tp, u + 1)
                        if u >= 4:
                            act.wait_ge(pvu, u - 3)
                        kind, a, b_, c_ = UNITS[u]
                        w = (2 * P if a == 0 else 4 * P) if kind == "A" else P * (b_ + 1)
                        act.activation(pT[:, u % 4, 0:w], bank[4 + u % 2][:, 0:w], ACT.Copy).then_inc(te, 1)

                    def o_out(G):
                        act.wait_ge(pv, G + 1)
                        b = bank[6 + G % 2]
                        if G < 4:
                            act.activation(oaT[:, :, G * P:(G + 1) * P], b[:, :].rearrange("p (j q) -> p j q", j=4),
                                           ACT.Copy).then_inc(oe, 1)
                        else:
                            act.activation(obT[:, G - 4, :], b[:, :], ACT.Copy).then_inc(oe, 1)

                    for s in range(NU + 4):
                        if s < NU:
                            exp_unit(s)
                        if 0 <= s - 2 < NU:
                            probsT(s - 2)
                        if 0 <= s - 4 < NU and LAST_OF[s - 4]:
                            o_out(GROUP_OF[s - 4])

                    for m in range(KD):
                        act.wait_ge(gates_ps, m + 1)
                        if m >= 2:
                            act.wait_ge(mg, m - 1)
                        b0 = 4 * (m % 2)
                        act.activation(sig[:, m % 2, 0, :], bank[b0][:, :], ACT.Exp, bias=nbg[:, m:m + 1], scale=-1.0)
                        act.activation(sig[:, m % 2, 1, :], bank[b0 + 1][:, :], ACT.Exp, bias=nbg[:, 8 + m:9 + m],
                                       scale=-1.0).then_inc(ge, 1)

                    for tt in range(TT):
                        act.wait_ge(xw, 5 + tt)
                        act.wait_ge(mg, 8)
                        act.activation(sig[:, 0, :, :], X[:, tt, :].rearrange("p (a b) -> p a b", a=2),
                                       ACT.Square, accum_out=stats[:, 8 + tt:9 + tt]).then_inc(f_sq, 1)
                        act.wait_ge(h2_ok, tt + 1)
                        act.dma_start(h_dram.rearrange("(t p h) c -> t p (h c)", p=P, h=2)[tt],
                                      h2[:, tt % 2, :]).then_inc(h2_dma[tt % 2], 16)
                        for b in range(2):
                            act.wait_ge(h2t_ps, 2 * tt + b + 1)
                            act.activation(hT[:, 4 * b:4 * b + 4, tt * P:(tt + 1) * P],
                                           bank[2 * (tt % 2) + b][:, :].rearrange("p (k q) -> p k q", k=4),
                                           ACT.Copy).then_inc(h2T_ok, 1)
                    act.wait_ge(r_exp_in, 1)
                    act.activation(rt[:, 16:32], rt[:, 0:16], ACT.Exp).then_inc(r_exp_out, 1)
                    act.wait_ge(r_exp_in, 2)
                    act.activation(rt[:, 36:40], rt[:, 32:36], ACT.Exp).then_inc(r_exp_out, 1)

                    for s in (xte, gcp, gex, hte, yev):
                        act.sem_inc(s, CREDIT)

                    def turns(rnd):
                        with act.Fori(0, TURNS) as i:
                            def v(j):
                                return rnd * EXP + i * UNROLL + j + 1

                            def xT_out(j):
                                act.wait_ge(xtp, v(j) + CREDIT)
                                act.wait_ge(gu, v(j) + CREDIT - 2)
                                act.activation(xeT[:, j % 2, :, :], bank[j % 2][:, :].rearrange("p (k q) -> p k q", k=4),
                                               ACT.Copy).then_inc(xte, 1)

                            def gu_half(j):
                                act.wait_ge(gu, v(j) + CREDIT)
                                act.wait_ge(gsm, v(j) + CREDIT - 2)
                                act.activation(gtmp[0:SLOTS, j % 2, :], bank[2 + j % 2][SLOTS:P, :], ACT.Copy).then_inc(gcp, 1)
                                act.wait_ge(gsm, v(j) + CREDIT)
                                act.activation(gexp[0:SLOTS, j % 2, :], gu_rows[j % 2][0:SLOTS, 0:FE], ACT.Exp,
                                               scale=-1.0).then_inc(gex, 1)

                            def h_out(j):
                                act.wait_ge(htp, v(j) + CREDIT)
                                act.wait_ge(yp, v(j) + CREDIT - 2)
                                act.activation(heT[:, j % 2, :, :],
                                               bank[4 + j % 2][:, 0:2 * P].rearrange("p (k q) -> p k q", k=2)[:, :, 0:SLOTS],
                                               ACT.Copy).then_inc(hte, 1)
                                act.wait_ge(yp, v(j) + CREDIT)
                                act.wait_ge(y_free, v(j))
                                act.activation(ye[:, j, :], bank[6 + j % 2][:, :], ACT.Copy).then_inc(yev, 1)

                            xT_out(0)
                            gu_half(0)
                            for j in range(1, UNROLL):
                                xT_out(j)
                                h_out(j - 1)
                                gu_half(j)
                            h_out(UNROLL - 1)

                    act.wait_ge(gath_ok, 2)
                    turns(0)
                    act.wait_ge(counts_ok, 1)
                    most = act.value_load(cmax[0:1, 0:1], min_val=0, max_val=T)
                    with act.Fori(1, ROUNDS) as rnd:
                        with act.If(most > rnd * SLOTS):
                            turns(rnd)

                @block.tensor
                def _(pe):
                    for i in range(2 * TT):
                        tt, kh = divmod(i, 2)
                        pe.wait_ge(xn_ok, tt + 1)
                        if i == 7:
                            pe.wait_ge(cols_ok, 1)
                        for k in range(4):
                            ins = pe.transpose(bank[i][:, k * P:(k + 1) * P],
                                               xn[:, tt, (4 * kh + k) * P:(4 * kh + k + 1) * P], ident)
                        ins.then_inc(hT_ps, 1)
                        if i == 0:
                            pe.wait_ge(small_ld, 16 * 12)
                            pe.transpose(bank[7][:, 0:27], colrows[0:27, :], ident[0:27, 0:27]).then_inc(cols_ps, 1)

                    def project(i):
                        c, tt = divmod(i, TT)
                        n = 160 if c == 2 else 512
                        w = slot(c, KD * n).rearrange("p (k n) -> p k n", k=KD)
                        if tt == 0:
                            pe.wait_ge(w_in_dma[f"c{c}"], 48 if c == 2 else 16)
                        if i == 0:
                            pe.wait_ge(hT_ok, 8)
                        if i >= 4:
                            pe.wait_ge(pj_act, i - 3)
                            pe.wait_ge(pj_dve, i - 3)
                        for k in range(KD):
                            ins = pe.matmul(bank[i % 4][:, 0:n], hT[:, k, tt * P:(tt + 1) * P], w[:, k, :],
                                            start=k == 0, stop=k == KD - 1)
                        ins.then_inc(pj, 1)

                    def project_T(i):
                        c, tt = divmod(i, TT)
                        pe.wait_ge(qn_ok, i + 1)
                        if i >= 2:
                            pe.wait_ge(tp_read, i - 1)
                        b = bank[4 + i % 2]
                        q = qn[:, i % 2, :]
                        for j in range((4, 3, 1)[c]):
                            ins = pe.transpose(b[:, j * P:(j + 1) * P], q[:, j * P:(j + 1) * P], ident)
                        ins.then_inc(tpj, 1)

                    for i in range(3 * TT):
                        project(i)
                        if i % TT == TT - 1 and i < 2 * TT:
                            pe.wait_ge(pj, i + 1)
                            pe.sem_inc(ring_free, 1)
                        if i >= 1:
                            project_T(i - 1)
                    project_T(3 * TT - 1)

                    wqb = slot(2, 2 * BH * QK, 1280).rearrange("p (k n) -> p k n", k=2)
                    wkv = slot(2, 1024, 2816)

                    def mla(tt):
                        if tt == 0:
                            pe.wait_ge(tp_read, 12)
                            pe.wait_ge(pj_act, 12)
                            pe.wait_ge(pj_dve, 12)
                        else:
                            pe.wait_ge(p2_act, tt)
                            pe.wait_ge(p2_dve, tt)
                        for b in range(2):
                            for k in range(2):
                                pe.matmul(bank[b][:, 0:4 * QK], cqT[:, k, tt * P:(tt + 1) * P],
                                          wqb[:, k, b * 4 * QK:(b + 1) * 4 * QK], start=k == 0, stop=k == 1)
                        for b in range(2):
                            ins = pe.matmul(bank[2 + b][:, :], ckvT[:, tt * P:(tt + 1) * P],
                                            wkv[:, b * 512:(b + 1) * 512], start=True, stop=True)
                        ins.then_inc(p2, 1)

                    def mla_T(tt):
                        pe.wait_ge(p2_rope, tt + 1)
                        for b in range(4):
                            if tt >= 1:
                                pe.wait_ge(p2_te, 4 * (tt - 1) + b + 1)
                            for h in range(4):
                                ins = pe.transpose(bank[4 + b][0:QK, h * P:(h + 1) * P],
                                                   qk[:, tt % 2, 4 * b + h, :], ident)
                            ins.then_inc(p2_tp, 1)

                    for tt in range(TT):
                        mla(tt)
                        if tt >= 1:
                            mla_T(tt - 1)
                    pe.wait_ge(p2, TT)
                    pe.sem_inc(ring_free, 1)
                    mla_T(TT - 1)

                    def scores(u):
                        kind, a, b_, c_ = UNITS[u]
                        if u < 4:
                            pe.wait_ge(p2_act, 4)
                            pe.wait_ge(p2_dve, 4)
                        else:
                            pe.wait_ge(ex, u - 3)
                        if u == 0:
                            pe.wait_ge(tp_read, 12)
                        b = bank[u % 4]
                        if kind == "A":
                            n, g, jj = a, b_, c_
                            w = P if n == 0 else 2 * P
                            k0 = max(n - 1, 0) * P
                            for hh in range(2):
                                ins = pe.matmul(b[:, hh * w:(hh + 1) * w],
                                                qTA[g * AD:(g + 1) * AD, 2 * jj + hh, n * P:(n + 1) * P],
                                                kTA[g * AD:(g + 1) * AD, k0:k0 + w], start=True, stop=True)
                            ins.then_inc(sc, 1)
                        else:
                            h, n = a, b_
                            if u == 16:
                                pe.wait_ge(p2_te, 16)
                            w = P * (n + 1)
                            pe.matmul(b[:, 0:w], qkT[0:QK, h, n * P:(n + 1) * P], qkT[0:QK, BH + h, 0:w],
                                      start=True, stop=False)
                            pe.matmul(b[:, n * P:w], ident_bf[:, :], causal_bf[:, :],
                                      start=False, stop=True).then_inc(sc, 1)

                    def transposes(u):
                        kind, a, b_, c_ = UNITS[u]
                        pe.wait_ge(pn, u + 1)
                        if u < 2:
                            pe.wait_ge(p2_te, 16)
                        else:
                            pe.wait_ge(te, u - 1)
                        b = bank[4 + u % 2]
                        if kind == "A":
                            nk = 1 if a == 0 else 2
                            for kb in range(nk):
                                for hh in range(2):
                                    ins = pe.transpose(b[:, (kb * 2 + hh) * P:(kb * 2 + hh + 1) * P],
                                                       pr[:, u % 4, (hh * nk + kb) * P:(hh * nk + kb + 1) * P], ident)
                        else:
                            for kb in range(b_ + 1):
                                ins = pe.transpose(b[:, kb * P:(kb + 1) * P], pr[:, u % 4, kb * P:(kb + 1) * P], ident)
                        ins.then_inc(tp, 1)

                    def values(u):
                        kind, a, b_, c_ = UNITS[u]
                        G = GROUP_OF[u]
                        pe.wait_ge(te, u + 1)
                        if (u == 0 or GROUP_OF[u - 1] != G):
                            if G >= 2:
                                pe.wait_ge(oe, G - 1)
                            else:
                                pe.wait_ge(p2_te, 16)
                        o = bank[6 + G % 2]
                        if kind == "A":
                            n, g, jj = a, b_, c_
                            kbs = [n] if n == 0 else [n - 1, n]
                            for x_, kb in enumerate(kbs):
                                ins = pe.matmul(o[g * AD:(g + 1) * AD, jj * 2 * P:(jj + 1) * 2 * P],
                                                vA[:, kb, g * AD:(g + 1) * AD],
                                                pT[:, u % 4, x_ * 2 * P:(x_ + 1) * 2 * P],
                                                start=x_ == 0, stop=x_ == len(kbs) - 1)
                        else:
                            h, n = a, b_
                            for kb in range(n + 1):
                                ins = pe.matmul(o[(h % 2) * VD:(h % 2 + 1) * VD, n * P:(n + 1) * P],
                                                vB[:, kb, h * VD:(h + 1) * VD], pT[:, u % 4, kb * P:(kb + 1) * P],
                                                start=kb == 0, stop=kb == n)
                        ins.then_inc(pvu, 1)
                        if LAST_OF[u]:
                            pe.wait_ge(pvu, u + 1)
                            pe.sem_inc(pv, 1)

                    for s in range(NU + 3):
                        if s < NU:
                            scores(s)
                        if 0 <= s - 2 < NU:
                            transposes(s - 2)
                        if 0 <= s - 3 < NU:
                            values(s - 3)
                        if s == NU:
                            pe.wait_ge(sc, NU)
                            pe.sem_inc(ring_free, 1)

                    WG = [(1, 2), (4, 5)]
                    woa_v = slot(3).rearrange("p (k n) -> p k n", k=4)
                    wob_v = slot(0).rearrange("p (k n) -> p k n", k=4)
                    for m in range(KD):
                        b0 = 4 * (m % 2)
                        if m == 0:
                            pe.wait_ge(ex, NU)
                            pe.wait_ge(te, NU)
                            pe.wait_ge(oe, 8)
                            pe.wait_ge(w_in_dma["g0"], 16)
                            pe.wait_ge(w_in_dma["g2"], 16)
                            pe.wait_ge(w_in_dma["woa"], 32)
                            pe.wait_ge(w_in_dma["wob"], 16)
                        if m >= 2:
                            pe.wait_ge(mg, m - 1)
                        if m == 4:
                            pe.wait_ge(w_in_dma["g1"], 16)
                            pe.wait_ge(w_in_dma["g3"], 16)
                        for z in range(2):
                            w = slot(WG[m // 4][z]).rearrange("p (k n) -> p k n", k=KD)
                            for k in range(KD):
                                ins = pe.matmul(bank[b0 + z][:, :], w[:, k, (m % 4) * P:(m % 4 + 1) * P], hT[:, k, :],
                                                start=k == 0, stop=k == KD - 1)
                        ins.then_inc(gates_ps, 1)
                        for z, (w, o) in enumerate(((woa_v, oaT), (wob_v, obT))):
                            for k in range(4):
                                ins = pe.matmul(bank[b0 + 2 + z][:, :], w[:, k, m * P:(m + 1) * P], o[:, k, :],
                                                start=k == 0, stop=k == 3)
                        ins.then_inc(y_ps, 1)
                        if m == 3:
                            pe.wait_ge(y_ps, 4)
                            pe.sem_inc(ring_free, 1)
                    pe.wait_ge(y_ps, 8)
                    pe.sem_inc(wfree[0], 1)
                    pe.sem_inc(wfree[1], 1)

                    pe.wait_ge(mg, 8)
                    for i in range(2 * TT):
                        nh, tt = divmod(i, TT)
                        if tt == 0:
                            pe.wait_ge(w_in_dma[f"wo{nh}"], 16)
                        w = slot(1 + nh).rearrange("p (k n) -> p k n", k=KD)
                        for k in range(KD):
                            ins = pe.matmul(bank[i][:, :], mT[:, k, tt * P:(tt + 1) * P], w[:, k, :],
                                            start=k == 0, stop=k == KD - 1)
                        ins.then_inc(wo_ps, 1)
                    pe.wait_ge(wo_ps, 8)
                    pe.sem_inc(wfree[2], 1)
                    pe.sem_inc(wfree[3], 1)

                    pe.wait_ge(late_ld, 48)
                    pe.wait_ge(xw, 8)
                    for tt in range(TT):
                        pe.wait_ge(h2_ok, tt + 1)
                        for b in range(2):
                            if tt >= 2:
                                pe.wait_ge(h2T_ok, 2 * (tt - 2) + b + 1)
                            for k in range(4):
                                ins = pe.transpose(bank[2 * (tt % 2) + b][:, k * P:(k + 1) * P],
                                                   h2[:, tt % 2, (4 * b + k) * P:(4 * b + k + 1) * P], ident)
                            ins.then_inc(h2t_ps, 1)
                        pe.wait_ge(h2T_ok, 2 * tt + 2)
                        if tt >= 2:
                            pe.wait_ge(lt_ok, tt - 1)
                        for k in range(KD):
                            ins = pe.matmul(bank[4 + tt % 2][0:GROUPS + EXP, 0:P], wr[:, k, :],
                                            hT[:, k, tt * P:(tt + 1) * P], start=k == 0, stop=k == KD - 1)
                        ins.then_inc(lg_ps, 1)
                        pe.wait_ge(lt_ok, tt + 1)
                        pe.transpose(bank[6][:, tt * 36:(tt + 1) * 36], lgT[:, tt * P:(tt + 1) * P],
                                     ident[0:36, 0:36]).then_inc(lgt, 1)

                    pe.wait_ge(onehots, 1)
                    cnt = rt[:, 1024:1024 + TT * EXP // 2].bitcast(BF16)
                    pe.matmul(bank[7][:, 0:TT * EXP], before_bf[:, :], cnt, start=True, stop=False, skip_group_check=True)
                    for s in range(1, TT):
                        pe.matmul(bank[7][:, s * EXP:TT * EXP], ones_bf[:, :], cnt[:, 0:(TT - s) * EXP],
                                  start=False, stop=s == TT - 1, skip_group_check=True)
                    for s in range(TT):
                        ins = pe.matmul(bank[5][:, 0:EXP], ones_bf[:, :], cnt[:, s * EXP:(s + 1) * EXP],
                                        start=s == 0, stop=s == TT - 1)
                    ins.then_inc(ranks, 1)

                    for s in (xtp, gu, htp, yp):
                        pe.sem_inc(s, CREDIT)
                    pe.wait_ge(slots_ok, 1)

                    def turns(rnd):
                        with pe.Fori(0, TURNS) as i:
                            def v(j):
                                return rnd * EXP + i * UNROLL + j + 1

                            def x_T(j):
                                pe.wait_ge(gdma[j], 16 * (rnd * (TURNS + 1) + i + 1))
                                pe.wait_ge(xte, v(j) + CREDIT - 2)
                                g = gath[:, j, :].rearrange("s (p c) -> s c p", c=4)
                                for c in range(4):
                                    ins = pe.transpose(bank[j % 2][:, c * P:(c + 1) * P], g[:, c, :], ident)
                                ins.then_inc(xtp, 1)

                            def gate_up(j):
                                pe.wait_ge(wload[j], 48 * (rnd * TURNS + i + 1))
                                pe.wait_ge(xte, v(j) + CREDIT)
                                pe.wait_ge(gsm, v(j) + CREDIT - 2)
                                w = ring[:, EXP_OFF[j]:EXP_OFF[j] + 4096].rearrange("p (z k f) -> p k z f", z=2, k=8)
                                for c in range(4):
                                    for n in range(2):
                                        ins = pe.matmul(bank[2 + j % 2][n * SLOTS:(n + 1) * SLOTS, :],
                                                        xeT[:, j % 2, c, n * SLOTS:(n + 1) * SLOTS], w[:, n * 4 + c],
                                                        start=c == 0, stop=c == 3)
                                ins.then_inc(gu, 1)

                            def down(j):
                                pe.wait_ge(hh, v(j) + CREDIT)
                                pe.wait_ge(hte, v(j) + CREDIT - 2)
                                hv = hrow[:, j % 2, :].rearrange("s (p k) -> s k p", k=2)
                                for k in range(2):
                                    ins = pe.transpose(bank[4 + j % 2][:, k * P:(k + 1) * P], hv[:, k, :], ident)
                                ins.then_inc(htp, 1)
                                pe.wait_ge(hte, v(j) + CREDIT)
                                pe.wait_ge(yev, v(j) + CREDIT - 2)
                                w = ring[:, EXP_OFF[j] + 4096:EXP_OFF[j] + 6144].rearrange("p (k n) -> p k n", k=2)
                                for k in range(2):
                                    for n in range(2):
                                        ins = pe.matmul(bank[6 + j % 2][n * SLOTS:(n + 1) * SLOTS, :],
                                                        heT[:, j % 2, k, :], w[:, k, n * 512:(n + 1) * 512],
                                                        start=k == 0, stop=k == 1)
                                ins.then_inc(yp, 1)
                                pe.wait_ge(yp, v(j) + CREDIT)
                                pe.sem_inc(wfree[j], 1)

                            x_T(0)
                            gate_up(0)
                            for j in range(1, UNROLL):
                                x_T(j)
                                gate_up(j)
                                down(j - 1)
                            down(UNROLL - 1)

                    turns(0)
                    most = pe.value_load(cmax[0:1, 0:1], min_val=0, max_val=T)
                    with pe.Fori(1, ROUNDS) as rnd:
                        with pe.If(most > rnd * SLOTS):
                            turns(rnd)

                @block.vector
                def _(dve):
                    ch = Chain(dve, dch)
                    dve.wait_ge(rs_x, 1)
                    for tt in range(TT):
                        dve.tensor_scalar(xn[:, tt, :], X[:, tt, :], stats[:, 4 + tt:5 + tt], None,
                                          ALU.mult).then_inc(xn_ok, 1)
                    dve.wait_ge(cols_ps, 1)
                    ch.step(dve.tensor_copy(cols[:, 0:27], bank[7][:, 0:27]))
                    dve.tensor_scalar(nbg[:, :], cols[:, 8:24], -1.0, None, ALU.mult).then_inc(cols_ok, 1)
                    ch.step(dve.tensor_scalar(nsink[:, :], nsink[:, :], -1.0, None, ALU.mult))
                    for i in range(8):
                        tt, kh = divmod(i, 2)
                        dve.wait_ge(hT_ps, i + 1)
                        if i == 0:
                            dve.wait_ge(x_sq, 4)
                        dve.tensor_tensor(hT[:, 4 * kh:4 * kh + 4, tt * P:(tt + 1) * P],
                                          bank[i][:, :].rearrange("p (k q) -> p k q", k=4),
                                          cols[:, 4 * kh:4 * kh + 4].unsqueeze(2).broadcast_to([P, 4, P]),
                                          ALU.mult).then_inc(hT_ok, 1)

                    def proj_norm(i):
                        c, tt = divmod(i, TT)
                        b, q = bank[i % 4], qn[:, i % 2, :]
                        dve.wait_ge(pj_act, i + 1)
                        if c < 2:
                            nh = AH if c == 0 else AKV
                            dve.tensor_reduce(st1[:, i, 0:nh], sq[:, i % 2, 0:nh * AD].rearrange("p (h d) -> p h d", h=nh),
                                              AX, ALU.add).then_inc(pj_ss, 1)
                        else:
                            dve.engine_nop().then_inc(pj_ss, 1)
                        dve.wait_ge(pj_rs, i + 1)
                        if i >= 2:
                            dve.wait_ge(tpj, i - 1)
                        r = st1[:, i, :]
                        if c == 0:
                            ch.step(dve.tensor_tensor(
                                q.rearrange("p (j g d) -> p g j d", g=2, d=AD),
                                b[:, :].rearrange("p (g j d) -> p g j d", g=2, d=AD),
                                r[:, 0:AH].rearrange("p (g j) -> p g j", g=2).unsqueeze(3).broadcast_to([P, 2, 4, AD]),
                                ALU.mult))
                            dve.sem_inc(pj_dve, 1)
                            qv = q.rearrange("p (h d) -> p h d", h=AH)
                            dve.tensor_tensor(qv, qv, gainA[:, 0, :].unsqueeze(1).broadcast_to([P, AH, AD]),
                                              ALU.mult).then_inc(qn_ok, 1)
                        elif c == 1:
                            ch.step(dve.tensor_tensor(
                                q[:, 0:P].rearrange("p (g d) -> p g d", g=AKV), b[:, 0:P].rearrange("p (g d) -> p g d", g=AKV),
                                r[:, 0:AKV].unsqueeze(2).broadcast_to([P, AKV, AD]), ALU.mult))
                            ch.step(dve.tensor_scalar(q[:, P:P + QL], b[:, 2 * P:2 * P + QL], r[:, 8:9], None, ALU.mult))
                            dve.sem_inc(pj_dve, 1)
                            kv = q[:, 0:P].rearrange("p (g d) -> p g d", g=AKV)
                            dve.tensor_tensor(kv, kv, gainA[:, 1, :].unsqueeze(1).broadcast_to([P, AKV, AD]),
                                              ALU.mult).then_inc(qn_ok, 1)
                        else:
                            ch.step(dve.tensor_scalar(q[:, 0:KVL], b[:, 0:KVL], r[:, 8:9], None, ALU.mult))
                            dve.sem_inc(pj_dve, 1)
                            dve.sem_inc(qn_ok, 1)

                    def proj_T(i):
                        c, tt = divmod(i, TT)
                        b = bank[4 + i % 2]
                        ts = slice(tt * P, (tt + 1) * P)
                        dve.wait_ge(tpj, i + 1)
                        if c == 0:
                            dve.tensor_copy(qTA[:, :, ts], b[:, :].rearrange("p (j q) -> p j q", j=4)).then_inc(tp_read, 1)
                        elif c == 1:
                            dve.tensor_copy(kTA[:, ts], b[:, 0:P])
                            ch.step(dve.tensor_tensor(cqT[:, :, ts], b[:, P:3 * P].rearrange("p (k q) -> p k q", k=2),
                                                      cols[:, 24:26].unsqueeze(2).broadcast_to([P, 2, P]), ALU.mult))
                            dve.sem_inc(tp_read, 1)
                        else:
                            dve.tensor_scalar(ckvT[:, ts], b[:, 0:P], cols[:, 26:27], None, ALU.mult).then_inc(tp_read, 1)

                    for i in range(3 * TT):
                        proj_norm(i)
                        if i >= 1:
                            proj_T(i - 1)
                    proj_T(3 * TT - 1)

                    def mla_rows(tt):
                        dve.wait_ge(p2, tt + 1)
                        if tt >= 2:
                            dve.wait_ge(p2_tp, 4 * (tt - 1))
                        for b in range(2):
                            ins = dve.tensor_copy(qk[:, tt % 2, 4 * b:4 * b + 4, :],
                                                  bank[b][:, 0:4 * QK].rearrange("p (h d) -> p h d", h=4))
                        ins.then_inc(p2_dve, 1)
                        dve.wait_ge(p2_sq, tt + 1)
                        dve.tensor_reduce(st2(tt), sq2[:, :, :], AX,
                                          ALU.add).then_inc(p2_ss, 1)
                        dve.wait_ge(p2_rs, tt + 1)
                        v = qk[:, tt % 2, :, :]
                        ch.step(dve.tensor_tensor(v, v, st2(tt).unsqueeze(2).broadcast_to([P, 2 * BH, QK]), ALU.mult))
                        v4 = v.rearrange("p (z h) d -> p z h d", z=2)
                        dve.tensor_tensor(v4, v4, gainB[:, :, :].unsqueeze(2).broadcast_to([P, 2, BH, QK]),
                                          ALU.mult).then_inc(p2_g, 1)

                    def st2(tt):
                        return st1[:, :, :].rearrange("p a b -> p (a b)")[:, 16 * tt:16 * tt + 16]

                    for tt in range(TT):
                        mla_rows(tt)

                    def maxima(u):
                        kind, a, b_, c_ = UNITS[u]
                        dve.wait_ge(sc, u + 1)
                        if kind == "A":
                            n, g, jj = a, b_, c_
                            if u == 0:
                                dve.wait_ge(p2_tp, 16)
                            if u >= 4:
                                dve.wait_ge(tp, u - 3)
                            w = P if n == 0 else 2 * P
                            h0 = 4 * g + 2 * jj
                            s = pr[:, u % 4, 0:2 * w].rearrange("p (h k) -> p h k", h=2)
                            ch.step(dve.scalar_tensor_tensor(s, bank[u % 4][:, 0:2 * w].rearrange("p (h k) -> p h k", h=2),
                                                             A_SCALE, bias[:, h0:h0 + 2, 2 * P - w:2 * P], ALU.mult, ALU.add))
                            ch.step(dve.tensor_reduce(unit[:, u, 4:6], s, AX, ALU.max))
                            ch.step(dve.scalar_tensor_tensor(unit[:, u, 0:2], unit[:, u, 4:6], -1.0, nsink[:, h0:h0 + 2],
                                                             ALU.mult, ALU.min))
                            dve.tensor_tensor(unit[:, u, 2:4], unit[:, u, 0:2], nsink[:, h0:h0 + 2],
                                              ALU.subtract).then_inc(mx, 1)
                        else:
                            w = P * (b_ + 1)
                            ch.step(dve.tensor_reduce(unit[:, u, 1:2], bank[u % 4][:, 0:w], AX, ALU.max))
                            dve.tensor_scalar(unit[:, u, 0:1], unit[:, u, 1:2], -B_SCALE, None, ALU.mult).then_inc(mx, 1)

                    def normalise(u):
                        kind, a, b_, c_ = UNITS[u]
                        dve.wait_ge(ex, u + 1)
                        if kind == "A":
                            w = P if a == 0 else 2 * P
                            ch.step(dve.tensor_tensor(unit[:, u, 4:6], unit[:, u, 4:6], unit[:, u, 6:8], ALU.add))
                            ch.step(dve.reciprocal(unit[:, u, 2:4], unit[:, u, 4:6]))
                            s = pr[:, u % 4, 0:2 * w].rearrange("p (h k) -> p h k", h=2)
                            dve.tensor_tensor(s, s, unit[:, u, 2:4].unsqueeze(2).broadcast_to([P, 2, w]),
                                              ALU.mult).then_inc(pn, 1)
                        else:
                            w = P * (b_ + 1)
                            ch.step(dve.reciprocal(unit[:, u, 2:3], unit[:, u, 4:5]))
                            dve.tensor_scalar(pr[:, u % 4, 0:w], pr[:, u % 4, 0:w], unit[:, u, 2:3], None,
                                              ALU.mult).then_inc(pn, 1)

                    for s in range(NU + 1):
                        if s < NU:
                            maxima(s)
                        if s >= 1:
                            normalise(s - 1)

                    for m in range(KD):
                        s = sig[:, m % 2, :, :]
                        b0 = 4 * (m % 2)
                        dve.wait_ge(ge, m + 1)
                        ch.step(dve.tensor_scalar(s, s, 1.0, None, ALU.add))
                        ch.step(dve.reciprocal(s, s))
                        dve.wait_ge(y_ps, m + 1)
                        ch.step(dve.tensor_tensor(s[:, 0], s[:, 0], bank[b0 + 2][:, :], ALU.mult))
                        ch.step(dve.tensor_tensor(s[:, 1], s[:, 1], bank[b0 + 3][:, :], ALU.mult))
                        if m == 0:
                            dve.wait_ge(pvu, NU)
                        dve.tensor_tensor(mT[:, m, :], s[:, 0], s[:, 1], ALU.add).then_inc(mg, 1)
                    for i in range(2 * TT):
                        nh, tt = divmod(i, TT)
                        dve.wait_ge(wo_ps, i + 1)
                        xv = X[:, tt, nh * 512:(nh + 1) * 512]
                        dve.tensor_tensor(xv, bank[i][:, :], xv, ALU.add).then_inc(xw, 1)

                    dve.wait_ge(late_ld, 48)
                    for tt in range(TT):
                        dve.wait_ge(f_rs, tt + 1)
                        if tt >= 2:
                            dve.wait_ge(h2_dma[tt % 2], 16)
                            dve.wait_ge(h2t_ps, 2 * tt - 2)
                        ch.step(dve.tensor_scalar(h2[:, tt % 2, :], X[:, tt, :], stats[:, 12 + tt:13 + tt], None, ALU.mult))
                        dve.tensor_tensor(h2[:, tt % 2, :], h2[:, tt % 2, :], gffn[:, :], ALU.mult).then_inc(h2_ok, 1)
                        if tt >= 1:
                            dve.wait_ge(lg_ps, tt)
                            dve.tensor_copy(lgT[:, (tt - 1) * P:tt * P], bank[4 + (tt - 1) % 2][0:36, 0:P]).then_inc(lt_ok, 1)
                    dve.wait_ge(lg_ps, TT)
                    dve.tensor_copy(lgT[:, (TT - 1) * P:], bank[4 + (TT - 1) % 2][0:36, 0:P]).then_inc(lt_ok, 1)
                    dve.wait_ge(lgt, TT)
                    dve.wait_ge(wo_ps, 8)

                    used = [40]

                    def tmp(*shape):
                        n = 1
                        for d_ in shape:
                            n *= d_
                        a = used[0]
                        used[0] += n
                        assert used[0] <= 1024
                        v = rt[:, a:a + n]
                        if len(shape) == 2:
                            v = v.rearrange("p (a b) -> p a b", b=shape[1])
                        if len(shape) == 3:
                            v = v.rearrange("p (a b c) -> p a b c", b=shape[1], c=shape[2])
                        return v

                    def bc(v, *shape):
                        return v.broadcast_to([P, *shape])

                    lg = tmp(TT, GROUPS + EXP)
                    ch.step(dve.tensor_tensor(lg, bank[6][:, 0:TT * 36].rearrange("p (t c) -> p t c", t=TT),
                                              bc(rbias[:, :].unsqueeze(1), TT, 36), ALU.add))

                    def argmax(v, n, iota, d):
                        m = tmp(TT, 1)
                        ch.step(dve.tensor_reduce(m[:, :, 0], v, AX, ALU.max))
                        ch.step(dve.tensor_tensor(d, v, bc(m, TT, n), ALU.subtract))
                        t = tmp(TT, n)
                        ch.step(dve.tensor_scalar(t, d, 0.0, -64.0, ALU.is_ge, ALU.mult))
                        ch.step(dve.tensor_tensor(t, t, bc(iota.unsqueeze(1), TT, n), ALU.add))
                        first = tmp(TT, 1)
                        ch.step(dve.tensor_reduce(first[:, :, 0], t, AX, ALU.min))
                        one = tmp(TT, n)
                        ch.step(dve.tensor_tensor(one, t, bc(first, TT, n), ALU.is_equal))
                        return m, one

                    gd = rt[:, 0:16].rearrange("p (t c) -> p t c", t=TT)
                    _, og = argmax(lg[:, :, 0:GROUPS], GROUPS, C("iota4"), gd)
                    dve.engine_nop().then_inc(r_exp_in, 1)
                    pick = tmp(TT, EXP)
                    pick4 = pick.rearrange("p t (g e) -> p t g e", g=GROUPS)
                    el = tmp(TT, PER_GROUP)
                    for tt in range(TT):
                        ch.step(dve.tensor_tensor(pick4[:, tt], lg[:, tt, GROUPS:].rearrange("p (g e) -> p g e", g=GROUPS),
                                                  bc(og[:, tt].unsqueeze(2), GROUPS, PER_GROUP), ALU.mult))
                    ch.step(dve.tensor_reduce(el, pick4.rearrange("p t g e -> p t e g"), AX, ALU.add))
                    e1d, e2d = tmp(TT, PER_GROUP), tmp(TT, PER_GROUP)
                    m1, o1 = argmax(el, PER_GROUP, C("iota8"), e1d)
                    ch.step(dve.scalar_tensor_tensor(el, o1, NEG, el, ALU.mult, ALU.add))
                    m2, o2 = argmax(el, PER_GROUP, C("iota8"), e2d)
                    dm = rt[:, 32:36]
                    dve.tensor_tensor(dm, m2[:, :, 0], m1[:, :, 0], ALU.subtract).then_inc(r_exp_in, 1)
                    hot1, hot2 = tmp(TT, EXP), tmp(TT, EXP)
                    for o_, hot_ in ((o1, hot1), (o2, hot2)):
                        for tt in range(TT):
                            ch.step(dve.tensor_tensor(hot_[:, tt].rearrange("p (g e) -> p g e", g=GROUPS),
                                                      bc(og[:, tt].unsqueeze(2), GROUPS, PER_GROUP),
                                                      bc(o_[:, tt].unsqueeze(1), GROUPS, PER_GROUP), ALU.mult))
                    cnt = rt[:, 1024:1024 + TT * EXP // 2].bitcast(BF16).rearrange("p (t e) -> p t e", t=TT)
                    dve.tensor_tensor(cnt, hot1, hot2, ALU.add).then_inc(onehots, 1)
                    dve.wait_ge(r_exp_out, 2)
                    gsum_, gp, den = tmp(TT), tmp(TT), tmp(TT)
                    ch.step(dve.tensor_reduce(gsum_, rt[:, 16:32].rearrange("p (t c) -> p t c", t=TT), AX, ALU.add))
                    ch.step(dve.reciprocal(gp, gsum_))
                    ch.step(dve.tensor_scalar(den, rt[:, 36:40], 1.0, None, ALU.add))
                    ch.step(dve.reciprocal(den, den))
                    ch.step(dve.tensor_tensor(wts[:, 0, :], gp, den, ALU.mult))
                    dve.tensor_tensor(wts[:, 1, :], wts[:, 0, :], rt[:, 36:40], ALU.mult).then_inc(wts_ok, 1)
                    dve.wait_ge(ranks, 1)
                    pos = tmp(TT, EXP)
                    ch.step(dve.scalar_tensor_tensor(pos, bank[7][:, 0:TT * EXP].rearrange("p (t e) -> p t e", t=TT),
                                                     float(EXP), bc(C("iota32").unsqueeze(1), TT, EXP), ALU.mult, ALU.add))
                    for k_, hot_ in enumerate((hot1, hot2)):
                        ch.step(dve.tensor_tensor(hot_, hot_, pos, ALU.mult))
                        sl = tmp(TT)
                        ch.step(dve.tensor_reduce(sl, hot_, AX, ALU.add))
                        ch.step(dve.tensor_copy(slots_i[:, :].rearrange("p (t k) -> p t k", k=2)[:, :, k_], sl))
                    mxc = tmp(1)
                    ch.step(dve.tensor_reduce(mxc, bank[5][:, 0:EXP], AX, ALU.max))
                    ch.step(dve.tensor_copy(cmax[:, :], mxc))
                    dve.sem_inc(slots_ok, 1)
                    dve.sem_inc(counts_ok, 1)

                    dve.wait_ge(wo_ps, 8)
                    dve.memset(gath[:, :, :], 0.0).then_inc(gath_ok, 1)
                    dve.memset(hrow[SLOTS:P, :, :], 0.0).then_inc(gath_ok, 1)
                    for s in (gsm, g1_, g2_, g3_, hh):
                        dve.sem_inc(s, CREDIT)

                    def indices(rnd):
                        dve.wait_ge(tbl_ld, 32 * (rnd + 1))
                        g, s = idx_g[:, 0:EXP], idx_s[:, 0:EXP]
                        dve.tensor_scalar(g, idx_s[:, 0:EXP], -2, None, ALU.bitwise_and).then_inc(idx_ok, 1)
                        dve.wait_ge(idx_ok, rnd * 3 + 1)
                        dve.tensor_scalar(g, g, C("half"), None, ALU.add).then_inc(idx_ok, 1)
                        dve.tensor_scalar(s, s, 2.0, C("half"), ALU.mult, ALU.add).then_inc(idx_ok, 1)

                    def turns(rnd):
                        with dve.Fori(0, TURNS) as i:
                            for j in range(UNROLL):
                                v = rnd * EXP + i * UNROLL + j + 1
                                r = gu_rows[j % 2]
                                e, h = gexp[0:SLOTS, j % 2, :], hrow[0:SLOTS, j % 2, :]
                                dve.wait_ge(gcp, v + CREDIT)
                                dve.wait_ge(hh, v + CREDIT - 2)
                                dve.tensor_tensor(r[0:SLOTS, :], bank[2 + j % 2][0:SLOTS, :], gtmp[0:SLOTS, j % 2, :],
                                                  ALU.add).then_inc(gsm, 1)
                                dve.wait_ge(gex, v + CREDIT)
                                dve.tensor_scalar(e, e, 1.0, None, ALU.add).then_inc(g1_, 1)
                                dve.wait_ge(g1_, v + CREDIT)
                                dve.reciprocal(e, e).then_inc(g2_, 1)
                                dve.wait_ge(g2_, v + CREDIT)
                                dve.tensor_tensor(e, e, r[0:SLOTS, 0:FE], ALU.mult).then_inc(g3_, 1)
                                dve.wait_ge(g3_, v + CREDIT)
                                dve.wait_ge(htp, v + CREDIT - 2)
                                dve.tensor_tensor(h, e, r[0:SLOTS, FE:2 * FE], ALU.mult).then_inc(hh, 1)

                    indices(0)
                    turns(0)
                    most = dve.value_load(cmax[0:1, 0:1], min_val=0, max_val=T)
                    with dve.Fori(1, ROUNDS) as rnd:
                        with dve.If(most > rnd * SLOTS):
                            indices(rnd)
                            turns(rnd)

                    for tt in range(TT):
                        dve.wait_ge(yl[tt % 2], 16 * (tt // 2 + 1))
                        yv = yld[:, tt % 2]
                        ch.step(dve.tensor_scalar(yv[:, 0, :], yv[:, 0, :], wts[:, 0, tt:tt + 1], None, ALU.mult))
                        ch.step(dve.scalar_tensor_tensor(yv[:, 0, :], yv[:, 1, :], wts[:, 1, tt:tt + 1], yv[:, 0, :],
                                                         ALU.mult, ALU.add))
                        dve.tensor_tensor(X[:, tt, :], X[:, tt, :], yv[:, 0, :], ALU.add).then_inc(comb, 1)

                @block.gpsimd
                def _(pool):
                    ch = Chain(pool, pch)

                    def rstd(dst, src, n, width):
                        ch.step(pool.tensor_scalar(dst, src, 1.0 / width, EPS, ALU.mult, ALU.add))
                        return pool.tensor_tensor(dst, dst, minus_half[:, 0:n], ALU.pow)

                    pool.dma_start(table.rearrange("(p c) one -> p (c one)", p=P), padt[:, :]).then_inc(tbl_init, 16)
                    pool.wait_ge(x_sq, 4)
                    rstd(stats[:, 4:8], stats[:, 0:4], 4, D).then_inc(rs_x, 1)
                    for i in range(3 * TT):
                        c = i // TT
                        pool.wait_ge(pj_act, i + 1)
                        pool.wait_ge(pj_ss, i + 1)
                        r = st1[:, i, :]
                        if c == 0:
                            rstd(r[:, 0:8], r[:, 0:8], 8, AD).then_inc(pj_rs, 1)
                        elif c == 1:
                            rstd(r[:, 0:2], r[:, 0:2], 2, AD)
                            rstd(r[:, 8:9], r[:, 8:9], 1, QL).then_inc(pj_rs, 1)
                        else:
                            rstd(r[:, 8:9], r[:, 8:9], 1, KVL).then_inc(pj_rs, 1)
                    pool.wait_ge(tpj, 12)
                    for tt in range(TT):
                        if tt >= 2:
                            pool.wait_ge(p2_tp, 4 * (tt - 1))
                        v = qk[:, tt % 2, :, :]
                        pool.tensor_copy(v[:, BH:, NOPE:], kpe[:, tt, :].unsqueeze(1).broadcast_to([P, BH, ROPE]))\
                            .then_inc(p2_kpe, 1)
                        pool.wait_ge(p2_ss, tt + 1)
                        r = st1[:, :, :].rearrange("p a b -> p (a b)")[:, 16 * tt:16 * tt + 16]
                        rstd(r, r, 16, QK).then_inc(p2_rs, 1)
                        pool.wait_ge(p2_g, tt + 1)
                        hf = ROPE // 2
                        x1, x2 = v[:, :, NOPE:NOPE + hf], v[:, :, NOPE + hf:]
                        cb = cosv[:, tt, :].unsqueeze(1).broadcast_to([P, 2 * BH, hf])
                        sb = sinv[:, tt, :].unsqueeze(1).broadcast_to([P, 2 * BH, hf])
                        pool.tensor_tensor(rope_t[:, 0], x1, cb, ALU.mult)
                        pool.tensor_tensor(rope_t[:, 1], x2, sb, ALU.mult)
                        pool.tensor_tensor(rope_t[:, 2], x1, sb, ALU.mult)
                        ch.step(pool.tensor_tensor(rope_t[:, 3], x2, cb, ALU.mult))
                        pool.tensor_tensor(x1, rope_t[:, 0], rope_t[:, 1], ALU.subtract)
                        pool.tensor_tensor(x2, rope_t[:, 2], rope_t[:, 3], ALU.add).then_inc(p2_rope, 1)
                        pool.wait_ge(p2_rope, tt + 1)
                    for tt in range(TT):
                        pool.wait_ge(f_sq, tt + 1)
                        rstd(stats[:, 12 + tt:13 + tt], stats[:, 8 + tt:9 + tt], 1, D).then_inc(f_rs, 1)
                    pool.wait_ge(slots_ok, 1)
                    pool.wait_ge(tbl_init, 16)
                    for c in range(2 * TT):
                        pool.indirect_dma_start(table, bass.IndirectOffsetOnAxis(slots_i[:, c:c + 1], 0),
                                                rowid_i[:, c:c + 1], None, bounds_check=T * EXP - 1,
                                                oob_is_err=False).then_inc(tbl_sc, 16)
                    pool.wait_ge(tbl_sc, 16 * 2 * TT)
                    tv = table.rearrange("(s e) one -> s (e one)", e=EXP)

                    def load_table(rnd):
                        for n in range(2):
                            pool.dma_start(idx_s[n * SLOTS:(n + 1) * SLOTS, 0:EXP],
                                           tv[bass.ds(rnd * SLOTS, SLOTS), :]).then_inc(tbl_ld, 16)

                    def gather(e, j, use):
                        pool.tensor_copy(cur_g[:, j:j + 1], idx_g[:, bass.ds(e, 1)]).then_inc(cg, 1)
                        pool.wait_ge(cg, use)
                        pool.sem_inc(passed, 1)
                        pool.indirect_dma_start(gath[:, j, :], None, h_dram,
                                                bass.IndirectOffsetOnAxis(cur_g[:, j:j + 1], 0),
                                                bounds_check=2 * T - 1, oob_is_err=False).then_inc(gdma[j], 16)

                    def scatter(e, j, use):
                        pool.tensor_copy(cur_s[:, j:j + 1], idx_s[:, bass.ds(e, 1)]).then_inc(cs_, 1)
                        pool.wait_ge(cs_, use)
                        pool.sem_inc(passed, 1)
                        pool.indirect_dma_start(y_dram, bass.IndirectOffsetOnAxis(cur_s[:, j:j + 1], 0),
                                                ye[:, j, :], None, bounds_check=4 * T - 1,
                                                oob_is_err=False).then_inc(sdma[j], 16)

                    pool.sem_inc(y_free, CREDIT)

                    def turns(rnd):
                        first = rnd * (EXP + UNROLL)
                        for j in range(UNROLL):
                            gather(j, j, first + j + 1)
                        with pool.Fori(0, TURNS) as i:
                            def v(j):
                                return rnd * EXP + i * UNROLL + j + 1

                            def ahead(j):
                                pool.wait_ge(xtp, v(j) + CREDIT)
                                pool.sem_inc(passed, 1)
                                gather(i * UNROLL + j + UNROLL, j, first + UNROLL + i * UNROLL + j + 1)

                            def store(j):
                                pool.wait_ge(yev, v(j) + CREDIT)
                                pool.sem_inc(passed, 1)
                                scatter(i * UNROLL + j, j, v(j))

                            def stored(j):
                                pool.wait_ge(sdma[j], 16 * (rnd * TURNS + i + 1))
                                pool.sem_inc(y_free, 1)

                            ahead(0)
                            for j in range(1, UNROLL):
                                ahead(j)
                                store(j - 1)
                                if j >= 2:
                                    stored(j - 2)
                            store(UNROLL - 1)
                            stored(UNROLL - 2)
                            stored(UNROLL - 1)
                        for j in range(UNROLL):
                            pool.wait_ge(gdma[j], 16 * (rnd + 1) * (TURNS + 1))
                        pool.sem_inc(passed, 1)

                    load_table(0)
                    pool.wait_ge(idx_ok, 3)
                    pool.wait_ge(gath_ok, 2)
                    pool.wait_ge(h2_dma[0], 32)
                    pool.wait_ge(h2_dma[1], 32)
                    turns(0)
                    most = pool.value_load(cmax[0:1, 0:1], min_val=0, max_val=T)
                    with pool.Fori(1, ROUNDS) as rnd:
                        with pool.If(most > rnd * SLOTS):
                            load_table(rnd)
                            pool.wait_ge(idx_ok, rnd * 3 + 3)
                            pool.sem_inc(passed, 1)
                            turns(rnd)
                    pool.sem_inc(moe_done, 1)
                    pool.dma_reset(sem_range)

            nc.all_engine_barrier(sems_to_clear=sem_range)

        out_sem = ctx.enter_context(nc.semaphore("out_stored"))
        with nc.Block() as block:
            @block.sync
            def _(sp):
                sp.dma_start(out[0].rearrange("(t p) d -> p t d", p=P), X[:, :, :]).then_inc(out_sem, 16)
                sp.wait_ge(out_sem, 16)


_INS = ["x", "attn_norm", "w_in", "b_gate", "a_q_norm", "a_k_norm", "a_sinks", "rel_bias", "w_oa",
        "q_a_norm", "w_qb", "kv_a_norm", "w_kvb", "b_q_norm", "b_k_norm", "w_ob", "w_o", "ffn_norm",
        "w_router_group", "b_router_group", "w_router_expert", "b_router_expert", "w_exp_gate",
        "w_exp_up", "w_exp_down"]


def kernel(**inputs):
    import concourse.bacc as bacc
    from concourse.bass_utils import run_bass_kernel_spmd

    nc = bacc.Bacc("TRN2", target_bir_lowering=False, num_devices=1)
    arrays = {name: np.ascontiguousarray(inputs[name]) for name in _INS}
    arrays["consts"], arrays["hot"] = constants()
    args = [nc.dram_tensor(f"{n}_dram", a.shape, mybir.dt.from_np(a.dtype), kind="ExternalInput").ap()
            for n, a in arrays.items()]
    out = nc.dram_tensor("out_dram", (1, T, D), F32, kind="ExternalOutput").ap()
    trunk(nc, *args, out)
    r = run_bass_kernel_spmd(nc, [{f"{n}_dram": a for n, a in arrays.items()}], core_ids=[0])
    return r.results[0]["out_dram"]
```

```python
import math
from contextlib import ExitStack

import numpy as np

import concourse.bass as bass
from concourse import mybir

F32 = mybir.dt.float32
BF16 = mybir.dt.bfloat16
I32 = mybir.dt.int32
ALU = mybir.AluOpType
ACT = mybir.ActivationFunctionType
AX = mybir.AxisListType.X

P = 128
D = 1024
T = 512
TT = T // P
KD = D // P
L = 2
AH, AKV, AD = 8, 2, 64
WINDOW = 128
BUCKETS, MAX_DIST = 32, 128
BH, QL, KVL, NOPE, ROPE, VD = 8, 256, 128, 64, 32, 64
QK = NOPE + ROPE
THETA = 10000.0
GROUPS, PER_GROUP = 4, 8
EXP = GROUPS * PER_GROUP
FE = 256
EPS = 1e-6
A_SCALE = AD ** -0.5
B_SCALE = QK ** -0.5
NEG = -1e30

C_KPE = 1152
C_GATE = 1184
GROUP_N = 512

SLOTS = 64
ROUNDS = T // SLOTS
UNROLL = 4
TURNS = EXP // UNROLL
EXTRA = UNROLL
PAD = 4096
FIRST = 0
XPER = EXP + 1
CREDIT = UNROLL

CONST = {}
_at = 0
for _name, _n in (("ident", P), ("causal", P), ("before", P), ("ones", P), ("cos", TT * ROPE // 2),
                  ("sin", TT * ROPE // 2), ("iota4", GROUPS), ("iota8", PER_GROUP), ("iota32", EXP),
                  ("half", 1), ("rowid", 2 * TT)):
    CONST[_name] = (_at, _n)
    _at += _n
N_CONST = _at
BIAS_W = 384


def constants():
    c = np.zeros((P, N_CONST), np.float32)

    def put(name, v):
        a, n = CONST[name]
        c[:, a:a + n] = v

    i = np.arange(P)
    put("ident", np.eye(P))
    put("causal", np.where(i[None, :] <= i[:, None], 0.0, NEG))
    put("before", i[:, None] < i[None, :])
    put("ones", 1.0)
    half = ROPE // 2
    freq = np.float32(THETA) ** (-np.arange(half, dtype=np.float32) / np.float32(half))
    ang = np.arange(T, dtype=np.float32)[:, None] * freq[None, :]
    fold = lambda a: a.reshape(TT, P, half).transpose(1, 0, 2).reshape(P, TT * half)
    put("cos", fold(np.cos(ang)))
    put("sin", fold(np.sin(ang)))
    put("iota4", np.arange(GROUPS))
    put("iota8", np.arange(PER_GROUP))
    put("iota32", np.arange(EXP))
    put("half", (i >= SLOTS)[:, None])
    rows = 2 * (i[:, None, None] + P * np.arange(TT)[None, :, None]) + np.arange(2)[None, None, :]
    put("rowid", rows.reshape(P, 2 * TT))
    hot = np.zeros((BUCKETS + 1, BIAS_W), np.float32)
    exact = BUCKETS // 2
    for col in range(BIAS_W - 1):
        d = 2 * P - 1 - col
        if 0 <= d < WINDOW:
            ratio = np.float32(max(d, 1)) / np.float32(exact)
            large = exact + int(np.log(ratio) / np.float32(math.log(MAX_DIST / exact))
                                * np.float32(BUCKETS - exact))
            hot[d if d < exact else min(large, BUCKETS - 1), col] = 1.0
        else:
            hot[BUCKETS, col] = NEG
    return c, hot


class Chain:

    def __init__(self, eng, sem):
        self.eng, self.sem, self.n = eng, sem, 0

    def step(self, ins):
        ins.then_inc(self.sem, 1)
        self.n += 1
        self.eng.wait_ge(self.sem, self.n)


def trunk(nc, x, attn_norm, w_in, b_gate, a_q_norm, a_k_norm, a_sinks, rel_bias, w_oa, q_a_norm,
          w_qb, kv_a_norm, w_kvb, b_q_norm, b_k_norm, w_ob, w_o, ffn_norm, w_rg, b_rg, w_re, b_re,
          w_gate, w_up, w_down, consts, hot, out):
    h_dram = nc.dram_tensor("h_rows", (2 * T, D // 2), F32).ap()
    y_dram = nc.dram_tensor("y_rows", (4 * T, D // 2), F32).ap()
    table = nc.dram_tensor("slot_table", (T * EXP, 1), I32).ap()
    bias_dram = nc.dram_tensor("bias_rows", (AH, P, BIAS_W), F32).ap()

    with ExitStack() as ctx:
        base = (nc.sbuf_base + 63) // 64 * 64

        def at(name, shape, dt, off):
            return nc.alloc_sbuf_tensor_at(name, shape, dt, offset=base + off)

        K = 1024
        ring = at("ring", [P, 24 * K], F32, 0)
        qkT = at("qkT", [P, 2 * BH, T], F32, 64 * K)
        X = at("x_rows", [P, TT, D], F32, 96 * K)
        hT = at("hT", [P, KD, T], F32, 112 * K)
        yld = at("y_loaded", [P, TT, 2, D], F32, 112 * K)
        oaT = at("oaT", [P, 4, T], F32, 128 * K)
        obT = at("obT", [P, 4, T], F32, 136 * K)
        rope_t = at("rope_tmp", [P, 4, 2 * BH, ROPE // 2], F32, 136 * K)
        vB = at("vB", [P, TT, BH * VD], F32, 144 * K)
        cqT = at("cqT", [P, 2, T], F32, 152 * K)
        ckvT = at("ckvT", [P, T], F32, 156 * K)
        qTA = at("qTA", [P, 4, T], F32, 158 * K)
        kTA = at("kTA", [P, T], F32, 166 * K)
        vA = at("vA", [P, TT, P], F32, 168 * K)
        gate_e = [at("gate_exp0", [P, 4, 2, T], F32, 16 * K), at("gate_exp1", [P, 4, 2, T], F32, 152 * K)]
        fsq = at("ffn_squares", [P, D], F32, 158 * K)
        xn = at("xn", [P, TT, D], F32, 170 * K)
        sq = at("sq", [P, 2, T], F32, 170 * K)
        qn = at("qn", [P, 2, T], F32, 174 * K)
        qk = at("qk_rows", [P, 2, 2 * BH, QK], F32, 170 * K)
        sq2 = at("sq2", [P, 2 * BH, QK], F32, 182 * K)
        pr = at("probs", [P, 4, T], F32, 170 * K)
        pT = at("probsT", [P, 4, T], F32, 178 * K)
        mT = at("mergedT", [P, KD, T], F32, 170 * K)
        gath = at("gathered", [P, UNROLL, T], F32, 170 * K)
        xeT = at("xeT", [P, 2, 4, P], F32, 178 * K)
        gtmp = at("gu_half", [P, 2, T], F32, 182 * K)
        gsum = at("gu", [P, T], F32, 186 * K)
        gsum2 = at("gu2", [P, T], F32, 144 * K)
        gexp = at("silu_tmp", [P, 2, FE], F32, 146 * K)
        hrow = at("h_expert", [P, 2, FE], F32, 148 * K)
        heT = at("heT", [P, 2, 2, SLOTS], F32, 150 * K)
        ye = at("y_expert", [P, UNROLL, T], F32, 128 * K)
        h2 = at("h2_rows", [P, 2, D], F32, 136 * K)
        lgT = at("logitsT", [GROUPS + EXP, T], F32, 152 * K)
        gu_rows = [gsum, gsum2]
        bias = at("bias", [P, AH, 2 * P], F32, 188 * K)
        misc = 196 * K
        sizes = {}

        def small(name, shape, dt=F32):
            nonlocal misc
            n = 1
            for s in shape[1:]:
                n *= s
            t = at(name, shape, dt, misc)
            misc += (n * mybir.dt.size(dt) + 31) // 32 * 32
            return t

        cst = small("cst", [P, N_CONST])
        causal_bf = small("causal_bf", [P, P], BF16)
        ident_bf = small("ident_bf", [P, P], BF16)
        before_bf = small("before_bf", [P, P], BF16)
        ones_bf = small("ones_bf", [P, P], BF16)
        minus_half = small("minus_half", [P, 48])
        colrows = at("colrows", [28, P], F32, 170 * K + 17 * K)
        cols = small("cols", [P, 28])
        nbg = small("neg_b_gate", [P, 16])
        gainA = small("gainA", [P, 2, AD])
        gainB = small("gainB", [P, 2, QK])
        nsink = small("neg_sink", [P, AH])
        rbias = small("router_bias", [P, GROUPS + EXP])
        kpe = small("kpe", [P, TT, ROPE])
        stats = small("stats", [P, 64])
        st1 = small("st1", [P, 12, 9])
        idx_g = small("idx_gather", [P, EXP + EXTRA], I32)
        idx_s = small("idx_scatter", [P, EXP + EXTRA], I32)
        cur_g = small("cur_gather", [P, UNROLL], I32)
        cur_s = small("cur_scatter", [P, UNROLL], I32)
        wts = small("weights", [P, 2, TT])
        slots_i = small("slots", [P, 2 * TT], I32)
        rowid_i = small("rowid_i", [P, 2 * TT], I32)
        cmax = small("count_max", [P, 1], I32)
        assert base + misc <= nc.sbuf_usable_end, (base + misc, nc.sbuf_usable_end)
        wr = at("w_router", [P, KD, GROUPS + EXP], F32, 168 * K)
        gffn = at("gain_ffn", [P, D], F32, 188 * K)
        unit = at("unit_stats", [P, 48, 8], F32, 186 * K)
        rt = at("routing", [P, 2048], F32, 178 * K)
        pre_rel = at("rel_rows", [BUCKETS + 1, AH], F32, 170 * K)
        pre_hot = at("hot_rows", [BUCKETS + 1, BIAS_W], F32, 171 * K)
        pre_bias = at("bias_sb", [AH, BIAS_W], F32, 173 * K)
        padt = small("pad_table", [P, P], I32)
        assert base + misc <= nc.sbuf_usable_end, (base + misc, nc.sbuf_usable_end)

        def C(name):
            a, n = CONST[name]
            return cst[:, a:a + n]

        ident = C("ident")
        cosv = C("cos").rearrange("p (t c) -> p t c", t=TT)
        sinv = C("sin").rearrange("p (t c) -> p t c", t=TT)

        bank = [ctx.enter_context(nc.psum_tensor(f"bank{i}", [P, 512], F32)) for i in range(8)]

        def slot(s, n=4096, off=0):
            return ring[:, s * 4096 + off:s * 4096 + off + n]

        EXP_OFF = [j * 6144 for j in range(UNROLL)]

        pre_dma, pre_c, pre_b, pre_v, pre_w = (ctx.enter_context(nc.semaphore(n)) for n in
                                        ("pre_dma", "pre_consts", "pre_bias", "pre_vec", "pre_store"))
        with nc.Block() as block:
            @block.sync
            def _(sp):
                sp.dma_start(cst[:, :], consts).then_inc(pre_dma, 16)
                sp.dma_start(X[:, :, :], x[0].rearrange("(t p) d -> p t d", p=P)).then_inc(pre_dma, 16)
                sp.dma_start(pre_hot[:, :], hot).then_inc(pre_dma, 16)
                sp.dma_start(pre_rel[0:BUCKETS, :], rel_bias).then_inc(pre_dma, 16)
                sp.wait_ge(pre_v, 6)
                sp.dma_start(bias_dram, pre_bias[:, :].unsqueeze(1).broadcast_to([AH, P, BIAS_W])).then_inc(pre_w, 16)
                sp.wait_ge(pre_w, 16)

            @block.vector
            def _(dve):
                dve.memset(pre_rel[BUCKETS:BUCKETS + 1, :], 1.0).then_inc(pre_c, 1)
                dve.memset(minus_half[:, :], -0.5).then_inc(pre_c, 1)
                dve.memset(padt[:, :], PAD).then_inc(pre_c, 1)
                dve.memset(idx_g[:, :], PAD).then_inc(pre_c, 1)
                dve.memset(idx_s[:, :], PAD).then_inc(pre_c, 1)
                dve.wait_ge(pre_dma, 64)
                dve.tensor_copy(causal_bf[:, :], C("causal")).then_inc(pre_v, 1)
                dve.tensor_copy(ident_bf[:, :], ident).then_inc(pre_v, 1)
                dve.tensor_copy(before_bf[:, :], C("before")).then_inc(pre_v, 1)
                dve.tensor_copy(ones_bf[:, :], C("ones")).then_inc(pre_v, 1)
                dve.tensor_copy(rowid_i[:, :], C("rowid")).then_inc(pre_v, 1)
                dve.wait_ge(pre_b, 1)
                dve.tensor_copy(pre_bias[:, :], bank[0][0:AH, 0:BIAS_W]).then_inc(pre_v, 1)

            @block.tensor
            def _(pe):
                pe.wait_ge(pre_dma, 64)
                pe.wait_ge(pre_c, 1)
                pe.matmul(bank[0][0:AH, 0:BIAS_W], pre_rel[:, :], pre_hot[:, :],
                          start=True, stop=True).then_inc(pre_b, 1)

        names = []

        def sem(name):
            s = ctx.enter_context(nc.semaphore(name))
            names.append(s)
            return s

        WCH = ["c0", "c1", "c2", "woa", "wob", "g0", "g2", "g1", "g3", "wo0", "wo1"]
        w_in_dma = {n: sem(f"loaded_{n}") for n in WCH}
        small_ld = sem("small_loaded")
        late_ld = sem("late_loaded")
        x_sq, rs_x, xn_ok, hT_ps, hT_ok = (sem(n) for n in ("x_sq", "rs_x", "xn_ok", "hT_ps", "hT_ok"))
        cols_ps, cols_ok = sem("cols_ps"), sem("cols_ok")
        pj, pj_act, pj_ss, pj_rs, pj_dve, qn_ok, tpj, tp_read = (sem(n) for n in (
            "proj", "proj_act", "proj_sums", "proj_rstd", "proj_dve", "qn_ok", "proj_T", "proj_T_read"))
        p2, p2_act, p2_dve, p2_kpe, p2_sq, p2_ss, p2_rs, p2_g, p2_rope, p2_tp, p2_te = (sem(n) for n in (
            "mla", "mla_act", "mla_dve", "mla_kpe", "mla_sq", "mla_sums", "mla_rstd", "mla_gain",
            "mla_rope", "mla_T", "mla_T_read"))
        sc, mx, ex, pn, tp, te, pv, pvu, oe = (sem(n) for n in (
            "scores", "maxima", "exps", "probs_ok", "probsT_ps", "probsT_ok", "pv_group", "pv_unit", "o_read"))
        gates_ps, ge, y_ps, mg = (sem(n) for n in ("gates_ps", "gate_exp", "y_ps", "merged"))
        wo_ps, xw = sem("wo_ps"), sem("x_mixed")
        f_sq, f_rs, h2_ok, h2t_ps, h2T_ok, lg_ps, lt_ok, lgt = (sem(n) for n in (
            "f_sq", "f_rstd", "h2_ok", "h2T_ps", "h2T_ok", "logitsT_ps", "logitsT_ok", "logits_ps"))
        h2_dma = [sem(f"h2_stored{i}") for i in range(2)]
        r_exp_in, r_exp_out, onehots, ranks, slots_ok, counts_ok, wts_ok = (sem(n) for n in (
            "r_exp_in", "r_exp_out", "onehots", "ranks", "slots_ok", "counts_ok", "weights_ok"))
        tbl_init, tbl_sc, tbl_ld, idx_ok = (sem(n) for n in (
            "table_init", "table_scattered", "table_loaded", "idx_ok"))
        wload = [sem(f"expert_loaded{j}") for j in range(UNROLL)]
        gdma = [sem(f"gathered{j}") for j in range(UNROLL)]
        sdma = [sem(f"scattered{j}") for j in range(UNROLL)]
        cg, cs_, xtp, xte, gu, gcp, gsm, gex, g1_, g2_, g3_, hh, htp, hte, yp, yev = (sem(n) for n in (
            "cur_g", "cur_s", "e_xT_ps", "e_xT_ok", "e_gu_ps", "e_gu_half", "e_gu_ok", "e_exp", "e_den",
            "e_recip", "e_silu", "e_h", "e_hT_ps", "e_hT_ok", "e_y_ps", "e_y_ok"))
        moe_done = sem("moe_done")
        yl = [sem(f"y_loaded{i}") for i in range(TT)]
        comb = sem("combined")
        dch, ach, pch = sem("dve_chain"), sem("act_chain"), sem("pool_chain")
        gath_ok = sem("gather_cleared")
        passed = sem("pool_passed")
        sem_range = range(names[0].num, names[-1].num + 1)
        assert len(sem_range) == len(names)

        UNITS = [("A", n, g, jj) for n in range(TT) for g in range(AKV) for jj in range(2)] + \
                [("B", h, n, 0) for h in range(BH) for n in range(TT)]
        NU = len(UNITS)
        GROUP_OF = [u // 4 if u < 16 else 4 + (u - 16) // 8 for u in range(NU)]
        LAST_OF = [u == NU - 1 or GROUP_OF[u] != GROUP_OF[u + 1] for u in range(NU)]

        MLA_JOBS = TT
        STEPS = NU + 3
        JOBS = 2 * KD
        GATE_MM = JOBS * KD
        UNIT_MM = GATE_MM - MLA_JOBS * KD
        GATE_DONE = [MLA_JOBS * KD + min(UNIT_MM, max(0, -(-UNIT_MM * (s_ - 1) // (STEPS - 4)))) for s_ in range(STEPS)]
        GATE_JOBS_DONE = [n_ // KD for n_ in GATE_DONE]

        def gate_job(q):
            c_, j_ = divmod(q, 4)
            z_ = c_ % 2
            b_ = bank[7] if q < MLA_JOBS else bank[6 + q % 2]
            return 2 * z_, j_ * P, gate_e[c_ // 2][:, j_, z_, :], 4 * (c_ // 2) + j_, z_, b_

        with nc.Fori(0, L) as l:
            with nc.Block() as block:
                @block.sync
                def _(sp):
                    def w_in_cols(a, n):
                        return w_in[l].rearrange("(k p) n -> p k n", p=P)[:, :, a:a + n]

                    def k_view(s, n, off=0, k=KD):
                        return slot(s, k * n, off).rearrange("p (k n) -> p k n", k=k)

                    def load(name, *pairs):
                        for dst, src in pairs:
                            sp.dma_start(dst, src).then_inc(w_in_dma[name], 16)

                    load("c0", (k_view(0, 512), w_in_cols(0, 512)))
                    load("c1", (k_view(1, 512), w_in_cols(512, 512)))
                    load("c2", (k_view(2, 160), w_in_cols(1024, 160)),
                         (k_view(2, BH * QK, 1280, 2), w_qb[l].rearrange("(k p) n -> p k n", p=P)),
                         (slot(2, 1024, 2816), w_kvb[l]))
                    oa = w_oa[l].rearrange("(g j d) n -> g d j n", g=2, j=4)
                    load("woa", *[(k_view(3, 1024, 0, 4)[g * AD:(g + 1) * AD], oa[g]) for g in range(2)])
                    sp.wait_ge(pj, TT)
                    load("g0", (k_view(0, 512), w_in_cols(C_GATE, 512)))
                    sp.wait_ge(p2, TT)
                    load("g2", (k_view(2, 512), w_in_cols(C_GATE + 1024, 512)))
                    sp.wait_ge(gates_ps, 4)
                    load("g1", (k_view(0, 512), w_in_cols(C_GATE + 512, 512)))
                    sp.wait_ge(gates_ps, 8)
                    load("g3", (k_view(2, 512), w_in_cols(C_GATE + 1536, 512)))
                    sp.wait_ge(gates_ps, 12)
                    load("wob", (k_view(0, 1024, 0, 4), w_ob[l].rearrange("(k p) n -> p k n", p=P)))
                    sp.wait_ge(sc, NU)
                    wo_v = w_o[l].rearrange("(k p) n -> p k n", p=P)
                    load("wo0", (k_view(4, 512), wo_v[:, :, 0:512]))
                    load("wo1", (k_view(5, 512), wo_v[:, :, 512:1024]))
                    sp.wait_ge(mg, 1)
                    sp.dma_start(wr[:, :, 0:GROUPS], w_rg[l].rearrange("(k p) n -> p k n", p=P)).then_inc(late_ld, 16)
                    sp.dma_start(wr[:, :, GROUPS:], w_re[l].rearrange("(k p) n -> p k n", p=P)).then_inc(late_ld, 16)
                    sp.dma_start(gffn[:, :], ffn_norm[l].unsqueeze(0).broadcast_to([P, D])).then_inc(late_ld, 16)

                    def load_expert(e, j):
                        o = EXP_OFF[j]
                        for k, w in enumerate((w_gate, w_up)):
                            sp.dma_start(ring[:, o + 2048 * k:o + 2048 * (k + 1)].rearrange("p (n c) -> p n c", n=2),
                                         w[l, e].rearrange("(n p j) f -> p n (j f)", n=2, j=4)).then_inc(wload[j], 16)
                        sp.dma_start(ring[:, o + 4096:o + 6144],
                                     w_down[l, e].rearrange("(p k) n -> p (k n)", k=2)).then_inc(wload[j], 16)

                    def turns(rnd):
                        for j in range(UNROLL):
                            if rnd is FIRST:
                                if j % 2 == 0:
                                    sp.wait_ge(mg if j == 0 else wo_ps, 8)
                            else:
                                sp.wait_ge(yp, rnd * EXP + j + 1)
                            load_expert(j, j)
                        with sp.Fori(1, TURNS) as i:
                            for j in range(UNROLL):
                                sp.wait_ge(yp, rnd * EXP + i * UNROLL + j + 1)
                                load_expert(i * UNROLL + j, j)

                    turns(FIRST)
                    sp.wait_ge(counts_ok, 1)
                    most = sp.value_load(cmax[0:1, 0:1], min_val=0, max_val=T)
                    with sp.Fori(1, ROUNDS) as rnd:
                        with sp.If(most > rnd * SLOTS):
                            turns(rnd)
                    sp.wait_ge(moe_done, 1)
                    yv = y_dram.rearrange("(t p k h) c -> t p k (h c)", p=P, k=2, h=2)
                    for tt in range(TT):
                        sp.dma_start(yld[:, tt], yv[tt]).then_inc(yl[tt], 16)
                    for tt in range(TT):
                        sp.wait_ge(yl[tt], 16)

                @block.scalar
                def _(act):
                    for dst, src in (
                        (colrows[0:8, :], attn_norm[l].rearrange("(k p) -> k p", p=P)),
                        (colrows[8:24, :], b_gate[l].rearrange("(k p) -> k p", p=P)),
                        (colrows[24:26, :], q_a_norm[l].rearrange("(k p) -> k p", p=P)),
                        (colrows[26:27, :], kv_a_norm[l].unsqueeze(0)),
                        (gainA[:, 0, :], a_q_norm[l].unsqueeze(0).broadcast_to([P, AD])),
                        (gainA[:, 1, :], a_k_norm[l].unsqueeze(0).broadcast_to([P, AD])),
                        (gainB[:, 0, :], b_q_norm[l].unsqueeze(0).broadcast_to([P, QK])),
                        (gainB[:, 1, :], b_k_norm[l].unsqueeze(0).broadcast_to([P, QK])),
                        (nsink[:, :], a_sinks[l].unsqueeze(0).broadcast_to([P, AH])),
                        (rbias[:, 0:GROUPS], b_rg[l].unsqueeze(0).broadcast_to([P, GROUPS])),
                        (rbias[:, GROUPS:], b_re[l].unsqueeze(0).broadcast_to([P, EXP])),
                        (bias[:, :, :], bass.AP(bias_dram.tensor, P - 1, [[BIAS_W - 1, P], [P * BIAS_W, AH], [1, 2 * P]])),
                    ):
                        act.dma_start(dst, src).then_inc(small_ld, 16)
                    for tt in range(TT):
                        act.activation(hT[:, 2 * tt:2 * tt + 2, :], X[:, tt, :].rearrange("p (a b) -> p a b", a=2),
                                       ACT.Square, accum_out=stats[:, tt:tt + 1]).then_inc(x_sq, 1)

                    for i in range(3 * TT):
                        c, tt = divmod(i, TT)
                        b = bank[i % 4]
                        act.wait_ge(pj, i + 1)
                        if i >= 2:
                            act.wait_ge(pj_ss, i - 1)
                        if i == 0:
                            act.wait_ge(hT_ps, 8)
                        if c == 0:
                            act.activation(sq[:, i % 2, :], b[:, :], ACT.Square).then_inc(pj_act, 1)
                        elif c == 1:
                            act.activation(sq[:, i % 2, 0:P], b[:, 0:P], ACT.Square)
                            act.activation(sq[:, i % 2, QL:2 * QL], b[:, QL:2 * QL], ACT.Square,
                                           accum_out=st1[:, i, 8:9])
                            act.activation(vA[:, tt, :], b[:, P:2 * P], ACT.Copy).then_inc(pj_act, 1)
                        else:
                            act.activation(sq[:, i % 2, 0:KVL], b[:, 0:KVL], ACT.Square,
                                           accum_out=st1[:, i, 8:9])
                            act.activation(kpe[:, tt, :], b[:, KVL:KVL + ROPE], ACT.Copy).then_inc(pj_act, 1)

                    def gate_exp(q):
                        _, _, dst, m, z, b = gate_job(q)
                        act.wait_ge(gates_ps, q + 1)
                        if q == 2 * 4:
                            act.wait_ge(sc, 16)
                        act.activation(dst, b[:, :], ACT.Exp, bias=nbg[:, 8 * z + m:8 * z + m + 1],
                                       scale=-1.0).then_inc(ge, 1)

                    def mla_T(tt):
                        for b in range(4):
                            act.wait_ge(p2_tp, 4 * tt + b + 1)
                            act.activation(qkT[0:QK, 4 * b:4 * b + 4, tt * P:(tt + 1) * P],
                                           bank[4 + (4 * tt + b) % 3][0:QK, :].rearrange("p (h q) -> p h q", h=4),
                                           ACT.Copy).then_inc(p2_te, 1)

                    for tt in range(TT):
                        act.wait_ge(p2, tt + 1)
                        if tt == 0:
                            act.wait_ge(tpj, 12)
                            act.wait_ge(pj_ss, 12)
                        if tt >= 2:
                            act.wait_ge(p2_tp, 4 * (tt - 1))
                        for b in range(2):
                            kv = bank[2 + b][:, :].rearrange("p (h d) -> p h d", h=4)
                            act.activation(qk[:, tt % 2, BH + 4 * b:BH + 4 * b + 4, 0:NOPE], kv[:, :, 0:NOPE], ACT.Copy)
                            ins = act.activation(vB[:, tt, 4 * b * VD:4 * (b + 1) * VD].rearrange("p (h d) -> p h d", h=4),
                                                 kv[:, :, NOPE:], ACT.Copy)
                        ins.then_inc(p2_act, 1)
                        act.wait_ge(p2_act, tt + 1)
                        act.wait_ge(p2_dve, tt + 1)
                        act.wait_ge(p2_kpe, tt + 1)
                        if tt >= 1:
                            act.wait_ge(p2_ss, tt)
                        act.activation(sq2[:, :, :], qk[:, tt % 2, :, :], ACT.Square).then_inc(p2_sq, 1)
                        if tt >= 1:
                            gate_exp(tt - 1)
                            mla_T(tt - 1)
                    gate_exp(TT - 1)
                    mla_T(TT - 1)

                    def exp_unit(u):
                        kind, a, b_, c_ = UNITS[u]
                        act.wait_ge(mx, u + 1)
                        if kind == "A":
                            w = P if a == 0 else 2 * P
                            for hh in range(2):
                                act.activation(pr[:, u % 4, hh * w:(hh + 1) * w], pr[:, u % 4, hh * w:(hh + 1) * w],
                                               ACT.Exp, bias=unit[:, u, hh:hh + 1], accum_out=unit[:, u, 4 + hh:5 + hh])
                            act.activation(unit[:, u, 6:8], unit[:, u, 2:4], ACT.Exp).then_inc(ex, 1)
                        else:
                            w = P * (b_ + 1)
                            if u >= 4:
                                act.wait_ge(tp, u - 3)
                            act.activation(pr[:, u % 4, 0:w], bank[u % 3][:, 0:w], ACT.Exp, bias=unit[:, u, 0:1],
                                           scale=B_SCALE, accum_out=unit[:, u, 4:5]).then_inc(ex, 1)

                    def probsT(u):
                        act.wait_ge(tp, u + 1)
                        if u >= 4:
                            act.wait_ge(pvu, u - 3)
                        kind, a, b_, c_ = UNITS[u]
                        w = (2 * P if a == 0 else 4 * P) if kind == "A" else P * (b_ + 1)
                        act.activation(pT[:, u % 4, 0:w], bank[3 + u % 2][:, 0:w], ACT.Copy).then_inc(te, 1)

                    def o_out(G):
                        act.wait_ge(pv, G + 1)
                        b = bank[5]
                        if G < 4:
                            act.activation(oaT[:, :, G * P:(G + 1) * P], b[:, :].rearrange("p (j q) -> p j q", j=4),
                                           ACT.Copy).then_inc(oe, 1)
                        else:
                            act.activation(obT[:, G - 4, :], b[:, :], ACT.Copy).then_inc(oe, 1)

                    done = MLA_JOBS
                    for s in range(NU + 4):
                        if 0 <= s - 4 < NU and LAST_OF[s - 4]:
                            o_out(GROUP_OF[s - 4])
                        if s < NU:
                            exp_unit(s)
                        if 0 <= s - 2 < NU:
                            probsT(s - 2)
                        while s >= 1 and done < GATE_JOBS_DONE[min(s, STEPS) - 1]:
                            gate_exp(done)
                            done += 1

                    for tt in range(TT):
                        act.wait_ge(xw, 5 + tt)
                        act.wait_ge(mg, 8)
                        act.activation(fsq[:, :], X[:, tt, :], ACT.Square, accum_out=stats[:, 8 + tt:9 + tt]).then_inc(f_sq, 1)
                        act.wait_ge(h2_ok, tt + 1)
                        act.dma_start(h_dram.rearrange("(t p h) c -> t p (h c)", p=P, h=2)[tt],
                                      h2[:, tt % 2, :]).then_inc(h2_dma[tt % 2], 16)
                        for b in range(2):
                            act.wait_ge(h2t_ps, 2 * tt + b + 1)
                            act.activation(hT[:, 4 * b:4 * b + 4, tt * P:(tt + 1) * P],
                                           bank[2 * (tt % 2) + b][:, :].rearrange("p (k q) -> p k q", k=4),
                                           ACT.Copy).then_inc(h2T_ok, 1)
                    act.wait_ge(r_exp_in, 1)
                    act.activation(rt[:, 16:32], rt[:, 0:16], ACT.Exp).then_inc(r_exp_out, 1)
                    act.wait_ge(r_exp_in, 2)
                    act.activation(rt[:, 36:40], rt[:, 32:36], ACT.Exp).then_inc(r_exp_out, 1)

                    for s in (xte, gcp, gex, hte, yev):
                        act.sem_inc(s, CREDIT)

                    def turns(rnd):
                        def xT_out(i, j):
                            act.wait_ge(xtp, rnd * XPER + i * UNROLL + j + 1 + CREDIT)
                            act.wait_ge(gu, rnd * EXP + i * UNROLL + j + 1 + CREDIT - 2)
                            act.activation(xeT[:, j % 2, :, :], bank[j % 2][:, :].rearrange("p (k q) -> p k q", k=4),
                                           ACT.Copy).then_inc(xte, 1)

                        def gu_half(v, j):
                            act.wait_ge(gu, v + CREDIT)
                            act.wait_ge(gsm, v + CREDIT - 2)
                            act.activation(gtmp[0:SLOTS, j % 2, :], bank[2 + j % 2][SLOTS:P, :], ACT.Copy).then_inc(gcp, 1)

                        def gate_exp(v, j):
                            act.wait_ge(gsm, v + CREDIT)
                            act.activation(gexp[0:SLOTS, j % 2, :], gu_rows[j % 2][0:SLOTS, 0:FE], ACT.Exp,
                                           scale=-1.0).then_inc(gex, 1)

                        def hT_out(v, j):
                            act.wait_ge(htp, v + CREDIT)
                            act.wait_ge(yp, v + CREDIT - 2)
                            act.activation(heT[:, j % 2, :, :],
                                           bank[4 + j % 2][:, 0:2 * P].rearrange("p (k q) -> p k q", k=2)[:, :, 0:SLOTS],
                                           ACT.Copy).then_inc(hte, 1)

                        def y_out(i, v, j):
                            act.wait_ge(yp, v + CREDIT)
                            if not (rnd is FIRST and i is FIRST):
                                act.wait_ge(sdma[j], 16 * (rnd * TURNS + i))
                            act.activation(ye[:, j, :], bank[6 + j % 2][:, :], ACT.Copy).then_inc(yev, 1)

                        def turn(i):
                            for j in range(UNROLL):
                                v = rnd * EXP + i * UNROLL + j + 1
                                last = i if j else i - 1
                                before = j > 0 or i is not FIRST
                                gu_half(v, j)
                                if before:
                                    hT_out(v - 1, (j - 1) % UNROLL)
                                xT_out(i, j + 1)
                                gate_exp(v, j)
                                if before:
                                    y_out(last, v - 1, (j - 1) % UNROLL)

                        xT_out(0, 0)
                        turn(FIRST)
                        with act.Fori(1, TURNS) as i:
                            turn(i)
                        hT_out((rnd + 1) * EXP, UNROLL - 1)
                        y_out(TURNS - 1, (rnd + 1) * EXP, UNROLL - 1)

                    act.wait_ge(gath_ok, 2)
                    turns(FIRST)
                    act.wait_ge(counts_ok, 1)
                    most = act.value_load(cmax[0:1, 0:1], min_val=0, max_val=T)
                    with act.Fori(1, ROUNDS) as rnd:
                        with act.If(most > rnd * SLOTS):
                            turns(rnd)

                @block.tensor
                def _(pe):
                    for i in range(2 * TT):
                        tt, kh = divmod(i, 2)
                        pe.wait_ge(xn_ok, tt + 1)
                        if i == 7:
                            pe.wait_ge(cols_ok, 1)
                        for k in range(4):
                            ins = pe.transpose(bank[i][:, k * P:(k + 1) * P],
                                               xn[:, tt, (4 * kh + k) * P:(4 * kh + k + 1) * P], ident)
                        ins.then_inc(hT_ps, 1)
                        if i == 0:
                            pe.wait_ge(small_ld, 16 * 12)
                            pe.transpose(bank[7][:, 0:27], colrows[0:27, :], ident[0:27, 0:27]).then_inc(cols_ps, 1)

                    def project(i):
                        c, tt = divmod(i, TT)
                        n = 160 if c == 2 else 512
                        w = slot(c, KD * n).rearrange("p (k n) -> p k n", k=KD)
                        if tt == 0:
                            pe.wait_ge(w_in_dma[f"c{c}"], 48 if c == 2 else 16)
                        if i == 0:
                            pe.wait_ge(hT_ok, 8)
                        if i >= 4:
                            pe.wait_ge(pj_act, i - 3)
                            pe.wait_ge(pj_dve, i - 3)
                        for k in range(KD):
                            ins = pe.matmul(bank[i % 4][:, 0:n], hT[:, k, tt * P:(tt + 1) * P], w[:, k, :],
                                            start=k == 0, stop=k == KD - 1)
                        ins.then_inc(pj, 1)

                    def project_T(i):
                        c, tt = divmod(i, TT)
                        pe.wait_ge(qn_ok, i + 1)
                        if i >= 2:
                            pe.wait_ge(tp_read, i - 1)
                        b = bank[4 + i % 2]
                        q = qn[:, i % 2, :]
                        for j in range((4, 3, 1)[c]):
                            ins = pe.transpose(b[:, j * P:(j + 1) * P], q[:, j * P:(j + 1) * P], ident)
                        ins.then_inc(tpj, 1)

                    for i in range(3 * TT):
                        project(i)
                        if i >= 1:
                            project_T(i - 1)
                    project_T(3 * TT - 1)

                    wqb = slot(2, 2 * BH * QK, 1280).rearrange("p (k n) -> p k n", k=2)
                    wkv = slot(2, 1024, 2816)

                    def mla(tt):
                        if tt == 0:
                            pe.wait_ge(tp_read, 12)
                            pe.wait_ge(pj_act, 12)
                            pe.wait_ge(pj_dve, 12)
                        else:
                            pe.wait_ge(p2_act, tt)
                            pe.wait_ge(p2_dve, tt)
                        for b in range(2):
                            for k in range(2):
                                pe.matmul(bank[b][:, 0:4 * QK], cqT[:, k, tt * P:(tt + 1) * P],
                                          wqb[:, k, b * 4 * QK:(b + 1) * 4 * QK], start=k == 0, stop=k == 1)
                        for b in range(2):
                            ins = pe.matmul(bank[2 + b][:, :], ckvT[:, tt * P:(tt + 1) * P],
                                            wkv[:, b * 512:(b + 1) * 512], start=True, stop=True)
                        ins.then_inc(p2, 1)

                    def mla_T(tt):
                        pe.wait_ge(p2_rope, tt + 1)
                        for b in range(4):
                            t = 4 * tt + b
                            if t >= 3:
                                pe.wait_ge(p2_te, t - 2)
                            for h in range(4):
                                ins = pe.transpose(bank[4 + t % 3][0:QK, h * P:(h + 1) * P],
                                                   qk[:, tt % 2, 4 * b + h, :], ident)
                            ins.then_inc(p2_tp, 1)

                    def gate_matmul(i):
                        q, k = divmod(i, KD)
                        slot_, col, _, _, _, b = gate_job(q)
                        if q % 4 == 0 and k == 0:
                            pe.wait_ge(w_in_dma[("g0", "g2", "g1", "g3")[q // 4]], 16)
                        if k == 0:
                            if q == MLA_JOBS:
                                pe.wait_ge(p2_te, 16)
                            elif q > MLA_JOBS:
                                pe.wait_ge(ge, q - 1)
                            elif q > 0:
                                pe.wait_ge(ge, q)
                        w = slot(slot_).rearrange("p (k n) -> p k n", k=KD)
                        ins = pe.matmul(b[:, :], w[:, k, col:col + P], hT[:, k, :],
                                        start=k == 0, stop=k == KD - 1)
                        if k == KD - 1:
                            ins.then_inc(gates_ps, 1)

                    for tt in range(TT):
                        mla(tt)
                        if tt >= 1:
                            for k in range(KD):
                                gate_matmul((tt - 1) * KD + k)
                            mla_T(tt - 1)
                    for k in range(KD):
                        gate_matmul((TT - 1) * KD + k)
                    mla_T(TT - 1)

                    def scores(u):
                        kind, a, b_, c_ = UNITS[u]
                        if u < 3:
                            pe.wait_ge(p2_act, 4)
                            pe.wait_ge(p2_dve, 4)
                        else:
                            pe.wait_ge(ex, u - 2)
                        if u == 0:
                            pe.wait_ge(tp_read, 12)
                        b = bank[u % 3]
                        if kind == "A":
                            n, g, jj = a, b_, c_
                            w = P if n == 0 else 2 * P
                            k0 = max(n - 1, 0) * P
                            for hh in range(2):
                                ins = pe.matmul(b[:, hh * w:(hh + 1) * w],
                                                qTA[g * AD:(g + 1) * AD, 2 * jj + hh, n * P:(n + 1) * P],
                                                kTA[g * AD:(g + 1) * AD, k0:k0 + w], start=True, stop=True)
                            ins.then_inc(sc, 1)
                        else:
                            h, n = a, b_
                            if u == 16:
                                pe.wait_ge(p2_te, 16)
                            w = P * (n + 1)
                            pe.matmul(b[:, 0:w], qkT[0:QK, h, n * P:(n + 1) * P], qkT[0:QK, BH + h, 0:w],
                                      start=True, stop=False)
                            pe.matmul(b[:, n * P:w], ident_bf[:, :], causal_bf[:, :],
                                      start=False, stop=True).then_inc(sc, 1)

                    def transposes(u):
                        kind, a, b_, c_ = UNITS[u]
                        pe.wait_ge(pn, u + 1)
                        if u < 2:
                            pe.wait_ge(p2_te, 16)
                        else:
                            pe.wait_ge(te, u - 1)
                        b = bank[3 + u % 2]
                        if kind == "A":
                            nk = 1 if a == 0 else 2
                            for kb in range(nk):
                                for hh in range(2):
                                    ins = pe.transpose(b[:, (kb * 2 + hh) * P:(kb * 2 + hh + 1) * P],
                                                       pr[:, u % 4, (hh * nk + kb) * P:(hh * nk + kb + 1) * P], ident)
                        else:
                            for kb in range(b_ + 1):
                                ins = pe.transpose(b[:, kb * P:(kb + 1) * P], pr[:, u % 4, kb * P:(kb + 1) * P], ident)
                        ins.then_inc(tp, 1)

                    def values(u):
                        kind, a, b_, c_ = UNITS[u]
                        G = GROUP_OF[u]
                        pe.wait_ge(te, u + 1)
                        if (u == 0 or GROUP_OF[u - 1] != G):
                            if G >= 1:
                                pe.wait_ge(oe, G)
                            else:
                                pe.wait_ge(p2_te, 16)
                        o = bank[5]
                        if kind == "A":
                            n, g, jj = a, b_, c_
                            kbs = [n] if n == 0 else [n - 1, n]
                            for x_, kb in enumerate(kbs):
                                ins = pe.matmul(o[g * AD:(g + 1) * AD, jj * 2 * P:(jj + 1) * 2 * P],
                                                vA[:, kb, g * AD:(g + 1) * AD],
                                                pT[:, u % 4, x_ * 2 * P:(x_ + 1) * 2 * P],
                                                start=x_ == 0, stop=x_ == len(kbs) - 1)
                        else:
                            h, n = a, b_
                            for kb in range(n + 1):
                                ins = pe.matmul(o[(h % 2) * VD:(h % 2 + 1) * VD, n * P:(n + 1) * P],
                                                vB[:, kb, h * VD:(h + 1) * VD], pT[:, u % 4, kb * P:(kb + 1) * P],
                                                start=kb == 0, stop=kb == n)
                        ins.then_inc(pvu, 1)
                        if LAST_OF[u]:
                            pe.wait_ge(pvu, u + 1)
                            pe.sem_inc(pv, 1)

                    done = MLA_JOBS * KD
                    for s in range(STEPS):
                        for part in range(3):
                            if part == 0 and s < NU:
                                scores(s)
                            if part == 1 and 0 <= s - 2 < NU:
                                transposes(s - 2)
                            if part == 2 and 0 <= s - 3 < NU:
                                values(s - 3)
                            before = GATE_DONE[s - 1] if s else 0
                            until = before + -(-(GATE_DONE[s] - before) * (part + 1) // 3)
                            while done < until:
                                gate_matmul(done)
                                done += 1

                    woa_v = slot(3).rearrange("p (k n) -> p k n", k=4)
                    wob_v = slot(0).rearrange("p (k n) -> p k n", k=4)
                    for m in range(KD):
                        if m == 0:
                            pe.wait_ge(te, NU)
                            pe.wait_ge(oe, 8)
                            pe.wait_ge(ge, JOBS)
                            pe.wait_ge(w_in_dma["woa"], 32)
                            pe.wait_ge(w_in_dma["wob"], 16)
                        if m >= 2:
                            pe.wait_ge(mg, m - 1)
                        for z, (w, o) in enumerate(((woa_v, oaT), (wob_v, obT))):
                            for k in range(4):
                                ins = pe.matmul(bank[4 + 2 * (m % 2) + z][:, :], w[:, k, m * P:(m + 1) * P], o[:, k, :],
                                                start=k == 0, stop=k == 3)
                        ins.then_inc(y_ps, 1)

                    for i in range(2 * TT):
                        nh, tt = divmod(i, TT)
                        if tt == 0:
                            pe.wait_ge(w_in_dma[f"wo{nh}"], 16)
                        if i == 0:
                            pe.wait_ge(ex, NU)
                        w = slot(4 + nh).rearrange("p (k n) -> p k n", k=KD)
                        for k in range(KD):
                            if i == 0:
                                pe.wait_ge(mg, k + 1)
                            ins = pe.matmul(bank[i][:, :], mT[:, k, tt * P:(tt + 1) * P], w[:, k, :],
                                            start=k == 0, stop=k == KD - 1)
                        ins.then_inc(wo_ps, 1)

                    pe.wait_ge(late_ld, 48)
                    pe.wait_ge(xw, 8)
                    for tt in range(TT):
                        pe.wait_ge(h2_ok, tt + 1)
                        for b in range(2):
                            if tt >= 2:
                                pe.wait_ge(h2T_ok, 2 * (tt - 2) + b + 1)
                            for k in range(4):
                                ins = pe.transpose(bank[2 * (tt % 2) + b][:, k * P:(k + 1) * P],
                                                   h2[:, tt % 2, (4 * b + k) * P:(4 * b + k + 1) * P], ident)
                            ins.then_inc(h2t_ps, 1)
                        pe.wait_ge(h2T_ok, 2 * tt + 2)
                        if tt >= 2:
                            pe.wait_ge(lt_ok, tt - 1)
                        for k in range(KD):
                            ins = pe.matmul(bank[4 + tt % 2][0:GROUPS + EXP, 0:P], wr[:, k, :],
                                            hT[:, k, tt * P:(tt + 1) * P], start=k == 0, stop=k == KD - 1)
                        ins.then_inc(lg_ps, 1)
                        pe.wait_ge(lt_ok, tt + 1)
                        pe.transpose(bank[6][:, tt * 36:(tt + 1) * 36], lgT[:, tt * P:(tt + 1) * P],
                                     ident[0:36, 0:36]).then_inc(lgt, 1)

                    pe.wait_ge(onehots, 1)
                    cnt = rt[:, 1024:1024 + TT * EXP // 2].bitcast(BF16)
                    pe.matmul(bank[7][:, 0:TT * EXP], before_bf[:, :], cnt, start=True, stop=False, skip_group_check=True)
                    for s in range(1, TT):
                        pe.matmul(bank[7][:, s * EXP:TT * EXP], ones_bf[:, :], cnt[:, 0:(TT - s) * EXP],
                                  start=False, stop=s == TT - 1, skip_group_check=True)
                    for s in range(TT):
                        ins = pe.matmul(bank[5][:, 0:EXP], ones_bf[:, :], cnt[:, s * EXP:(s + 1) * EXP],
                                        start=s == 0, stop=s == TT - 1)
                    ins.then_inc(ranks, 1)

                    for s in (xtp, gu, htp, yp):
                        pe.sem_inc(s, CREDIT)
                    pe.wait_ge(slots_ok, 1)

                    def turns(rnd):
                        def x_T(i, j):
                            v = rnd * XPER + i * UNROLL + j + 1
                            pe.wait_ge(gdma[j % UNROLL], 16 * (rnd * (TURNS + 1) + i + j // UNROLL + 1))
                            pe.wait_ge(xte, v + CREDIT - (1 if i is FIRST and j == 0 else 2))
                            g = gath[:, j % UNROLL, :].rearrange("s (p c) -> s c p", c=4)
                            for c in range(4):
                                ins = pe.transpose(bank[j % 2][:, c * P:(c + 1) * P], g[:, c, :], ident)
                            ins.then_inc(xtp, 1)

                        def gate_up(i, j):
                            v = rnd * EXP + i * UNROLL + j + 1
                            pe.wait_ge(wload[j], 48 * (rnd * TURNS + i + 1))
                            pe.wait_ge(xte, rnd * XPER + i * UNROLL + j + 1 + CREDIT)
                            pe.wait_ge(gsm, v + CREDIT - 2)
                            w = ring[:, EXP_OFF[j]:EXP_OFF[j] + 4096].rearrange("p (z k f) -> p k z f", z=2, k=8)
                            for c in range(4):
                                for n in range(2):
                                    ins = pe.matmul(bank[2 + j % 2][n * SLOTS:(n + 1) * SLOTS, :],
                                                    xeT[:, j % 2, c, n * SLOTS:(n + 1) * SLOTS], w[:, n * 4 + c],
                                                    start=c == 0, stop=c == 3)
                            ins.then_inc(gu, 1)

                        def h_T(v, j):
                            pe.wait_ge(hh, v + CREDIT)
                            pe.wait_ge(hte, v + CREDIT - 2)
                            hv = hrow[:, j % 2, :].rearrange("s (p k) -> s k p", k=2)
                            for k in range(2):
                                ins = pe.transpose(bank[4 + j % 2][:, k * P:(k + 1) * P], hv[:, k, :], ident)
                            ins.then_inc(htp, 1)

                        def down(v, j):
                            pe.wait_ge(hte, v + CREDIT)
                            pe.wait_ge(yev, v + CREDIT - 2)
                            w = ring[:, EXP_OFF[j] + 4096:EXP_OFF[j] + 6144].rearrange("p (k n) -> p k n", k=2)
                            for k in range(2):
                                for n in range(2):
                                    ins = pe.matmul(bank[6 + j % 2][n * SLOTS:(n + 1) * SLOTS, :],
                                                    heT[:, j % 2, k, :], w[:, k, n * 512:(n + 1) * 512],
                                                    start=k == 0, stop=k == 1)
                            ins.then_inc(yp, 1)

                        def turn(i):
                            for j in range(UNROLL):
                                before = rnd * EXP + i * UNROLL + j
                                some = j > 0 or i is not FIRST
                                gate_up(i, j)
                                if some:
                                    h_T(before, (j - 1) % UNROLL)
                                x_T(i, j + 1)
                                if some:
                                    down(before, (j - 1) % UNROLL)

                        x_T(FIRST, 0)
                        turn(FIRST)
                        with pe.Fori(1, TURNS) as i:
                            turn(i)
                        h_T((rnd + 1) * EXP, UNROLL - 1)
                        down((rnd + 1) * EXP, UNROLL - 1)

                    turns(FIRST)
                    most = pe.value_load(cmax[0:1, 0:1], min_val=0, max_val=T)
                    with pe.Fori(1, ROUNDS) as rnd:
                        with pe.If(most > rnd * SLOTS):
                            turns(rnd)

                @block.vector
                def _(dve):
                    ch = Chain(dve, dch)
                    dve.wait_ge(rs_x, 1)
                    for tt in range(TT):
                        dve.tensor_scalar(xn[:, tt, :], X[:, tt, :], stats[:, 4 + tt:5 + tt], None,
                                          ALU.mult).then_inc(xn_ok, 1)
                    dve.wait_ge(cols_ps, 1)
                    ch.step(dve.tensor_copy(cols[:, 0:27], bank[7][:, 0:27]))
                    dve.tensor_scalar(nbg[:, :], cols[:, 8:24], -1.0, None, ALU.mult).then_inc(cols_ok, 1)
                    ch.step(dve.tensor_scalar(nsink[:, :], nsink[:, :], -1.0, None, ALU.mult))
                    for i in range(8):
                        tt, kh = divmod(i, 2)
                        dve.wait_ge(hT_ps, i + 1)
                        if i == 0:
                            dve.wait_ge(x_sq, 4)
                        dve.tensor_tensor(hT[:, 4 * kh:4 * kh + 4, tt * P:(tt + 1) * P],
                                          bank[i][:, :].rearrange("p (k q) -> p k q", k=4),
                                          cols[:, 4 * kh:4 * kh + 4].unsqueeze(2).broadcast_to([P, 4, P]),
                                          ALU.mult).then_inc(hT_ok, 1)

                    def proj_norm(i):
                        c, tt = divmod(i, TT)
                        b, q = bank[i % 4], qn[:, i % 2, :]
                        dve.wait_ge(pj_act, i + 1)
                        if c < 2:
                            nh = AH if c == 0 else AKV
                            dve.tensor_reduce(st1[:, i, 0:nh], sq[:, i % 2, 0:nh * AD].rearrange("p (h d) -> p h d", h=nh),
                                              AX, ALU.add).then_inc(pj_ss, 1)
                        else:
                            dve.engine_nop().then_inc(pj_ss, 1)
                        dve.wait_ge(pj_rs, i + 1)
                        if i >= 2:
                            dve.wait_ge(tpj, i - 1)
                        r = st1[:, i, :]
                        if c == 0:
                            ch.step(dve.tensor_tensor(
                                q.rearrange("p (j g d) -> p g j d", g=2, d=AD),
                                b[:, :].rearrange("p (g j d) -> p g j d", g=2, d=AD),
                                r[:, 0:AH].rearrange("p (g j) -> p g j", g=2).unsqueeze(3).broadcast_to([P, 2, 4, AD]),
                                ALU.mult))
                            dve.sem_inc(pj_dve, 1)
                            qv = q.rearrange("p (h d) -> p h d", h=AH)
                            dve.tensor_tensor(qv, qv, gainA[:, 0, :].unsqueeze(1).broadcast_to([P, AH, AD]),
                                              ALU.mult).then_inc(qn_ok, 1)
                        elif c == 1:
                            ch.step(dve.tensor_tensor(
                                q[:, 0:P].rearrange("p (g d) -> p g d", g=AKV), b[:, 0:P].rearrange("p (g d) -> p g d", g=AKV),
                                r[:, 0:AKV].unsqueeze(2).broadcast_to([P, AKV, AD]), ALU.mult))
                            ch.step(dve.tensor_scalar(q[:, P:P + QL], b[:, 2 * P:2 * P + QL], r[:, 8:9], None, ALU.mult))
                            dve.sem_inc(pj_dve, 1)
                            kv = q[:, 0:P].rearrange("p (g d) -> p g d", g=AKV)
                            dve.tensor_tensor(kv, kv, gainA[:, 1, :].unsqueeze(1).broadcast_to([P, AKV, AD]),
                                              ALU.mult).then_inc(qn_ok, 1)
                        else:
                            ch.step(dve.tensor_scalar(q[:, 0:KVL], b[:, 0:KVL], r[:, 8:9], None, ALU.mult))
                            dve.sem_inc(pj_dve, 1)
                            dve.sem_inc(qn_ok, 1)

                    def proj_T(i):
                        c, tt = divmod(i, TT)
                        b = bank[4 + i % 2]
                        ts = slice(tt * P, (tt + 1) * P)
                        dve.wait_ge(tpj, i + 1)
                        if c == 0:
                            dve.tensor_copy(qTA[:, :, ts], b[:, :].rearrange("p (j q) -> p j q", j=4)).then_inc(tp_read, 1)
                        elif c == 1:
                            dve.tensor_copy(kTA[:, ts], b[:, 0:P])
                            ch.step(dve.tensor_tensor(cqT[:, :, ts], b[:, P:3 * P].rearrange("p (k q) -> p k q", k=2),
                                                      cols[:, 24:26].unsqueeze(2).broadcast_to([P, 2, P]), ALU.mult))
                            dve.sem_inc(tp_read, 1)
                        else:
                            dve.tensor_scalar(ckvT[:, ts], b[:, 0:P], cols[:, 26:27], None, ALU.mult).then_inc(tp_read, 1)

                    for i in range(3 * TT):
                        proj_norm(i)
                        if i >= 1:
                            proj_T(i - 1)
                    proj_T(3 * TT - 1)

                    def mla_rows(tt):
                        dve.wait_ge(p2, tt + 1)
                        if tt >= 2:
                            dve.wait_ge(p2_tp, 4 * (tt - 1))
                        for b in range(2):
                            ins = dve.tensor_copy(qk[:, tt % 2, 4 * b:4 * b + 4, :],
                                                  bank[b][:, 0:4 * QK].rearrange("p (h d) -> p h d", h=4))
                        ins.then_inc(p2_dve, 1)
                        dve.wait_ge(p2_sq, tt + 1)
                        dve.tensor_reduce(st2(tt), sq2[:, :, :], AX,
                                          ALU.add).then_inc(p2_ss, 1)
                        dve.wait_ge(p2_rs, tt + 1)
                        v = qk[:, tt % 2, :, :]
                        ch.step(dve.tensor_tensor(v, v, st2(tt).unsqueeze(2).broadcast_to([P, 2 * BH, QK]), ALU.mult))
                        v4 = v.rearrange("p (z h) d -> p z h d", z=2)
                        dve.tensor_tensor(v4, v4, gainB[:, :, :].unsqueeze(2).broadcast_to([P, 2, BH, QK]),
                                          ALU.mult).then_inc(p2_g, 1)

                    def st2(tt):
                        return st1[:, :, :].rearrange("p a b -> p (a b)")[:, 16 * tt:16 * tt + 16]

                    def sigmoid(q):
                        e = gate_job(q)[2]
                        dve.wait_ge(ge, q + 1)
                        ch.step(dve.tensor_scalar(e, e, 1.0, None, ALU.add))
                        ch.step(dve.reciprocal(e, e))

                    for tt in range(TT):
                        mla_rows(tt)
                        if tt >= 2:
                            sigmoid(tt - 2)
                    for q in range(TT - 2, MLA_JOBS):
                        sigmoid(q)

                    def maxima(u):
                        kind, a, b_, c_ = UNITS[u]
                        dve.wait_ge(sc, u + 1)
                        if kind == "A":
                            n, g, jj = a, b_, c_
                            if u == 0:
                                dve.wait_ge(p2_tp, 16)
                            if u >= 4:
                                dve.wait_ge(tp, u - 3)
                            w = P if n == 0 else 2 * P
                            h0 = 4 * g + 2 * jj
                            s = pr[:, u % 4, 0:2 * w].rearrange("p (h k) -> p h k", h=2)
                            ch.step(dve.scalar_tensor_tensor(s, bank[u % 3][:, 0:2 * w].rearrange("p (h k) -> p h k", h=2),
                                                             A_SCALE, bias[:, h0:h0 + 2, 2 * P - w:2 * P], ALU.mult, ALU.add))
                            ch.step(dve.tensor_reduce(unit[:, u, 4:6], s, AX, ALU.max))
                            ch.step(dve.scalar_tensor_tensor(unit[:, u, 0:2], unit[:, u, 4:6], -1.0, nsink[:, h0:h0 + 2],
                                                             ALU.mult, ALU.min))
                            dve.tensor_tensor(unit[:, u, 2:4], unit[:, u, 0:2], nsink[:, h0:h0 + 2],
                                              ALU.subtract).then_inc(mx, 1)
                        else:
                            w = P * (b_ + 1)
                            ch.step(dve.tensor_reduce(unit[:, u, 1:2], bank[u % 3][:, 0:w], AX, ALU.max))
                            dve.tensor_scalar(unit[:, u, 0:1], unit[:, u, 1:2], -B_SCALE, None, ALU.mult).then_inc(mx, 1)

                    def normalise(u):
                        kind, a, b_, c_ = UNITS[u]
                        dve.wait_ge(ex, u + 1)
                        if kind == "A":
                            w = P if a == 0 else 2 * P
                            ch.step(dve.tensor_tensor(unit[:, u, 4:6], unit[:, u, 4:6], unit[:, u, 6:8], ALU.add))
                            ch.step(dve.reciprocal(unit[:, u, 2:4], unit[:, u, 4:6]))
                            s = pr[:, u % 4, 0:2 * w].rearrange("p (h k) -> p h k", h=2)
                            dve.tensor_tensor(s, s, unit[:, u, 2:4].unsqueeze(2).broadcast_to([P, 2, w]),
                                              ALU.mult).then_inc(pn, 1)
                        else:
                            w = P * (b_ + 1)
                            ch.step(dve.reciprocal(unit[:, u, 2:3], unit[:, u, 4:5]))
                            dve.tensor_scalar(pr[:, u % 4, 0:w], pr[:, u % 4, 0:w], unit[:, u, 2:3], None,
                                              ALU.mult).then_inc(pn, 1)

                    done = MLA_JOBS
                    for s in range(STEPS + 1):
                        if s < NU:
                            maxima(s)
                        if 1 <= s <= NU:
                            normalise(s - 1)
                        while s >= 3 and done < GATE_JOBS_DONE[s - 3]:
                            sigmoid(done)
                            done += 1
                    while done < JOBS:
                        sigmoid(done)
                        done += 1

                    for m in range(KD):
                        s = gate_e[m // 4][:, m % 4, :, :]
                        b0 = 4 + 2 * (m % 2)
                        dve.wait_ge(y_ps, m + 1)
                        ch.step(dve.tensor_tensor(s[:, 0], s[:, 0], bank[b0][:, :], ALU.mult))
                        ch.step(dve.tensor_tensor(s[:, 1], s[:, 1], bank[b0 + 1][:, :], ALU.mult))
                        if m == 0:
                            dve.wait_ge(pvu, NU)
                        dve.tensor_tensor(mT[:, m, :], s[:, 0], s[:, 1], ALU.add).then_inc(mg, 1)
                    for i in range(2 * TT):
                        nh, tt = divmod(i, TT)
                        dve.wait_ge(wo_ps, i + 1)
                        xv = X[:, tt, nh * 512:(nh + 1) * 512]
                        dve.tensor_tensor(xv, bank[i][:, :], xv, ALU.add).then_inc(xw, 1)

                    dve.wait_ge(late_ld, 48)
                    for tt in range(TT):
                        dve.wait_ge(f_rs, tt + 1)
                        if tt >= 2:
                            dve.wait_ge(h2_dma[tt % 2], 16)
                            dve.wait_ge(h2t_ps, 2 * tt - 2)
                        ch.step(dve.tensor_scalar(h2[:, tt % 2, :], X[:, tt, :], stats[:, 12 + tt:13 + tt], None, ALU.mult))
                        dve.tensor_tensor(h2[:, tt % 2, :], h2[:, tt % 2, :], gffn[:, :], ALU.mult).then_inc(h2_ok, 1)
                        if tt >= 1:
                            dve.wait_ge(lg_ps, tt)
                            dve.tensor_copy(lgT[:, (tt - 1) * P:tt * P], bank[4 + (tt - 1) % 2][0:36, 0:P]).then_inc(lt_ok, 1)
                    dve.wait_ge(lg_ps, TT)
                    dve.tensor_copy(lgT[:, (TT - 1) * P:], bank[4 + (TT - 1) % 2][0:36, 0:P]).then_inc(lt_ok, 1)
                    dve.wait_ge(lgt, TT)
                    dve.wait_ge(wo_ps, 8)

                    used = [40]

                    def tmp(*shape):
                        n = 1
                        for d_ in shape:
                            n *= d_
                        a = used[0]
                        used[0] += n
                        assert used[0] <= 1024
                        v = rt[:, a:a + n]
                        if len(shape) == 2:
                            v = v.rearrange("p (a b) -> p a b", b=shape[1])
                        if len(shape) == 3:
                            v = v.rearrange("p (a b c) -> p a b c", b=shape[1], c=shape[2])
                        return v

                    def bc(v, *shape):
                        return v.broadcast_to([P, *shape])

                    lg = tmp(TT, GROUPS + EXP)
                    ch.step(dve.tensor_tensor(lg, bank[6][:, 0:TT * 36].rearrange("p (t c) -> p t c", t=TT),
                                              bc(rbias[:, :].unsqueeze(1), TT, 36), ALU.add))

                    def argmax(v, n, iota, d):
                        m = tmp(TT, 1)
                        ch.step(dve.tensor_reduce(m[:, :, 0], v, AX, ALU.max))
                        ch.step(dve.tensor_tensor(d, v, bc(m, TT, n), ALU.subtract))
                        t = tmp(TT, n)
                        ch.step(dve.tensor_scalar(t, d, 0.0, -64.0, ALU.is_ge, ALU.mult))
                        ch.step(dve.tensor_tensor(t, t, bc(iota.unsqueeze(1), TT, n), ALU.add))
                        first = tmp(TT, 1)
                        ch.step(dve.tensor_reduce(first[:, :, 0], t, AX, ALU.min))
                        one = tmp(TT, n)
                        ch.step(dve.tensor_tensor(one, t, bc(first, TT, n), ALU.is_equal))
                        return m, one

                    gd = rt[:, 0:16].rearrange("p (t c) -> p t c", t=TT)
                    _, og = argmax(lg[:, :, 0:GROUPS], GROUPS, C("iota4"), gd)
                    dve.engine_nop().then_inc(r_exp_in, 1)
                    pick = tmp(TT, EXP)
                    pick4 = pick.rearrange("p t (g e) -> p t g e", g=GROUPS)
                    el = tmp(TT, PER_GROUP)
                    for tt in range(TT):
                        ch.step(dve.tensor_tensor(pick4[:, tt], lg[:, tt, GROUPS:].rearrange("p (g e) -> p g e", g=GROUPS),
                                                  bc(og[:, tt].unsqueeze(2), GROUPS, PER_GROUP), ALU.mult))
                    ch.step(dve.tensor_reduce(el, pick4.rearrange("p t g e -> p t e g"), AX, ALU.add))
                    e1d, e2d = tmp(TT, PER_GROUP), tmp(TT, PER_GROUP)
                    m1, o1 = argmax(el, PER_GROUP, C("iota8"), e1d)
                    ch.step(dve.scalar_tensor_tensor(el, o1, NEG, el, ALU.mult, ALU.add))
                    m2, o2 = argmax(el, PER_GROUP, C("iota8"), e2d)
                    dm = rt[:, 32:36]
                    dve.tensor_tensor(dm, m2[:, :, 0], m1[:, :, 0], ALU.subtract).then_inc(r_exp_in, 1)
                    hot1, hot2 = tmp(TT, EXP), tmp(TT, EXP)
                    for o_, hot_ in ((o1, hot1), (o2, hot2)):
                        for tt in range(TT):
                            ch.step(dve.tensor_tensor(hot_[:, tt].rearrange("p (g e) -> p g e", g=GROUPS),
                                                      bc(og[:, tt].unsqueeze(2), GROUPS, PER_GROUP),
                                                      bc(o_[:, tt].unsqueeze(1), GROUPS, PER_GROUP), ALU.mult))
                    cnt = rt[:, 1024:1024 + TT * EXP // 2].bitcast(BF16).rearrange("p (t e) -> p t e", t=TT)
                    dve.tensor_tensor(cnt, hot1, hot2, ALU.add).then_inc(onehots, 1)
                    dve.wait_ge(r_exp_out, 2)
                    gsum_, gp, den = tmp(TT), tmp(TT), tmp(TT)
                    ch.step(dve.tensor_reduce(gsum_, rt[:, 16:32].rearrange("p (t c) -> p t c", t=TT), AX, ALU.add))
                    ch.step(dve.reciprocal(gp, gsum_))
                    ch.step(dve.tensor_scalar(den, rt[:, 36:40], 1.0, None, ALU.add))
                    ch.step(dve.reciprocal(den, den))
                    ch.step(dve.tensor_tensor(wts[:, 0, :], gp, den, ALU.mult))
                    dve.tensor_tensor(wts[:, 1, :], wts[:, 0, :], rt[:, 36:40], ALU.mult).then_inc(wts_ok, 1)
                    dve.wait_ge(ranks, 1)
                    pos = tmp(TT, EXP)
                    ch.step(dve.scalar_tensor_tensor(pos, bank[7][:, 0:TT * EXP].rearrange("p (t e) -> p t e", t=TT),
                                                     float(EXP), bc(C("iota32").unsqueeze(1), TT, EXP), ALU.mult, ALU.add))
                    for k_, hot_ in enumerate((hot1, hot2)):
                        ch.step(dve.tensor_tensor(hot_, hot_, pos, ALU.mult))
                        sl = tmp(TT)
                        ch.step(dve.tensor_reduce(sl, hot_, AX, ALU.add))
                        ch.step(dve.tensor_copy(slots_i[:, :].rearrange("p (t k) -> p t k", k=2)[:, :, k_], sl))
                    mxc = tmp(1)
                    ch.step(dve.tensor_reduce(mxc, bank[5][:, 0:EXP], AX, ALU.max))
                    ch.step(dve.tensor_copy(cmax[:, :], mxc))
                    dve.sem_inc(slots_ok, 1)
                    dve.sem_inc(counts_ok, 1)

                    dve.wait_ge(wo_ps, 8)
                    dve.memset(gath[:, :, :], 0.0).then_inc(gath_ok, 1)
                    dve.memset(hrow[SLOTS:P, :, :], 0.0).then_inc(gath_ok, 1)
                    for s in (gsm, g1_, g2_, g3_, hh):
                        dve.sem_inc(s, CREDIT)

                    def indices(rnd):
                        dve.wait_ge(tbl_ld, 32 * (rnd + 1))
                        g, s = idx_g[:, 0:EXP], idx_s[:, 0:EXP]
                        dve.tensor_scalar(g, idx_s[:, 0:EXP], -2, None, ALU.bitwise_and).then_inc(idx_ok, 1)
                        dve.wait_ge(idx_ok, rnd * 3 + 1)
                        dve.tensor_scalar(g, g, C("half"), None, ALU.add).then_inc(idx_ok, 1)
                        dve.tensor_scalar(s, s, 2.0, C("half"), ALU.mult, ALU.add).then_inc(idx_ok, 1)

                    def turns(rnd):
                        with dve.Fori(0, TURNS) as i:
                            for j in range(UNROLL):
                                v = rnd * EXP + i * UNROLL + j + 1
                                r = gu_rows[j % 2]
                                e, h = gexp[0:SLOTS, j % 2, :], hrow[0:SLOTS, j % 2, :]
                                dve.wait_ge(gcp, v + CREDIT)
                                dve.wait_ge(hh, v + CREDIT - 2)
                                dve.tensor_tensor(r[0:SLOTS, :], bank[2 + j % 2][0:SLOTS, :], gtmp[0:SLOTS, j % 2, :],
                                                  ALU.add).then_inc(gsm, 1)
                                dve.wait_ge(gex, v + CREDIT)
                                dve.tensor_scalar(e, e, 1.0, None, ALU.add).then_inc(g1_, 1)
                                dve.wait_ge(g1_, v + CREDIT)
                                dve.reciprocal(e, e).then_inc(g2_, 1)
                                dve.wait_ge(g2_, v + CREDIT)
                                dve.tensor_tensor(e, e, r[0:SLOTS, 0:FE], ALU.mult).then_inc(g3_, 1)
                                dve.wait_ge(g3_, v + CREDIT)
                                dve.wait_ge(htp, v + CREDIT - 2)
                                dve.tensor_tensor(h, e, r[0:SLOTS, FE:2 * FE], ALU.mult).then_inc(hh, 1)

                    indices(0)
                    turns(0)
                    most = dve.value_load(cmax[0:1, 0:1], min_val=0, max_val=T)
                    with dve.Fori(1, ROUNDS) as rnd:
                        with dve.If(most > rnd * SLOTS):
                            indices(rnd)
                            turns(rnd)

                    for tt in range(TT):
                        dve.wait_ge(yl[tt], 16)
                        yv = yld[:, tt]
                        ch.step(dve.tensor_scalar(yv[:, 0, :], yv[:, 0, :], wts[:, 0, tt:tt + 1], None, ALU.mult))
                        ch.step(dve.scalar_tensor_tensor(yv[:, 0, :], yv[:, 1, :], wts[:, 1, tt:tt + 1], yv[:, 0, :],
                                                         ALU.mult, ALU.add))
                        dve.tensor_tensor(X[:, tt, :], X[:, tt, :], yv[:, 0, :], ALU.add).then_inc(comb, 1)

                @block.gpsimd
                def _(pool):
                    ch = Chain(pool, pch)

                    def rstd(dst, src, n, width):
                        ch.step(pool.tensor_scalar(dst, src, 1.0 / width, EPS, ALU.mult, ALU.add))
                        return pool.tensor_tensor(dst, dst, minus_half[:, 0:n], ALU.pow)

                    pool.dma_start(table.rearrange("(p c) one -> p (c one)", p=P), padt[:, :]).then_inc(tbl_init, 16)
                    pool.wait_ge(x_sq, 4)
                    rstd(stats[:, 4:8], stats[:, 0:4], 4, D).then_inc(rs_x, 1)
                    for i in range(3 * TT):
                        c = i // TT
                        pool.wait_ge(pj_act, i + 1)
                        pool.wait_ge(pj_ss, i + 1)
                        r = st1[:, i, :]
                        if c == 0:
                            rstd(r[:, 0:8], r[:, 0:8], 8, AD).then_inc(pj_rs, 1)
                        elif c == 1:
                            rstd(r[:, 0:2], r[:, 0:2], 2, AD)
                            rstd(r[:, 8:9], r[:, 8:9], 1, QL).then_inc(pj_rs, 1)
                        else:
                            rstd(r[:, 8:9], r[:, 8:9], 1, KVL).then_inc(pj_rs, 1)
                    pool.wait_ge(tpj, 12)
                    for tt in range(TT):
                        if tt >= 2:
                            pool.wait_ge(p2_tp, 4 * (tt - 1))
                        v = qk[:, tt % 2, :, :]
                        pool.tensor_copy(v[:, BH:, NOPE:], kpe[:, tt, :].unsqueeze(1).broadcast_to([P, BH, ROPE]))\
                            .then_inc(p2_kpe, 1)
                        pool.wait_ge(p2_ss, tt + 1)
                        r = st1[:, :, :].rearrange("p a b -> p (a b)")[:, 16 * tt:16 * tt + 16]
                        rstd(r, r, 16, QK).then_inc(p2_rs, 1)
                        pool.wait_ge(p2_g, tt + 1)
                        hf = ROPE // 2
                        x1, x2 = v[:, :, NOPE:NOPE + hf], v[:, :, NOPE + hf:]
                        cb = cosv[:, tt, :].unsqueeze(1).broadcast_to([P, 2 * BH, hf])
                        sb = sinv[:, tt, :].unsqueeze(1).broadcast_to([P, 2 * BH, hf])
                        pool.tensor_tensor(rope_t[:, 0], x1, cb, ALU.mult)
                        pool.tensor_tensor(rope_t[:, 1], x2, sb, ALU.mult)
                        pool.tensor_tensor(rope_t[:, 2], x1, sb, ALU.mult)
                        ch.step(pool.tensor_tensor(rope_t[:, 3], x2, cb, ALU.mult))
                        pool.tensor_tensor(x1, rope_t[:, 0], rope_t[:, 1], ALU.subtract)
                        pool.tensor_tensor(x2, rope_t[:, 2], rope_t[:, 3], ALU.add).then_inc(p2_rope, 1)
                        pool.wait_ge(p2_rope, tt + 1)
                    for tt in range(TT):
                        pool.wait_ge(f_sq, tt + 1)
                        rstd(stats[:, 12 + tt:13 + tt], stats[:, 8 + tt:9 + tt], 1, D).then_inc(f_rs, 1)
                    pool.wait_ge(slots_ok, 1)
                    pool.wait_ge(tbl_init, 16)
                    for c in range(2 * TT):
                        pool.indirect_dma_start(table, bass.IndirectOffsetOnAxis(slots_i[:, c:c + 1], 0),
                                                rowid_i[:, c:c + 1], None, bounds_check=T * EXP - 1,
                                                oob_is_err=False).then_inc(tbl_sc, 16)
                    pool.wait_ge(tbl_sc, 16 * 2 * TT)
                    tv = table.rearrange("(s e) one -> s (e one)", e=EXP)

                    def load_table(rnd):
                        for n in range(2):
                            pool.dma_start(idx_s[n * SLOTS:(n + 1) * SLOTS, 0:EXP],
                                           tv[bass.ds(rnd * SLOTS, SLOTS), :]).then_inc(tbl_ld, 16)

                    def gather(e, j, use):
                        pool.tensor_copy(cur_g[:, j:j + 1], idx_g[:, bass.ds(e, 1)]).then_inc(cg, 1)
                        pool.wait_ge(cg, use)
                        pool.sem_inc(passed, 1)
                        pool.indirect_dma_start(gath[:, j, :], None, h_dram,
                                                bass.IndirectOffsetOnAxis(cur_g[:, j:j + 1], 0),
                                                bounds_check=2 * T - 1, oob_is_err=False).then_inc(gdma[j], 16)

                    def scatter(e, j, use):
                        pool.tensor_copy(cur_s[:, j:j + 1], idx_s[:, bass.ds(e, 1)]).then_inc(cs_, 1)
                        pool.wait_ge(cs_, use)
                        pool.sem_inc(passed, 1)
                        pool.indirect_dma_start(y_dram, bass.IndirectOffsetOnAxis(cur_s[:, j:j + 1], 0),
                                                ye[:, j, :], None, bounds_check=4 * T - 1,
                                                oob_is_err=False).then_inc(sdma[j], 16)

                    def turns(rnd):
                        first = rnd * (EXP + UNROLL)
                        if rnd is not FIRST:
                            pool.wait_ge(xtp, rnd * XPER + CREDIT)
                            pool.sem_inc(passed, 1)
                        for j in range(UNROLL):
                            gather(j, j, first + j + 1)

                        def ahead(i, j):
                            pool.wait_ge(xtp, rnd * XPER + i * UNROLL + j + 1 + CREDIT)
                            pool.sem_inc(passed, 1)
                            gather(i * UNROLL + j + UNROLL, j, first + UNROLL + i * UNROLL + j + 1)

                        def store(i, j):
                            pool.wait_ge(yev, rnd * EXP + i * UNROLL + j + 1 + CREDIT)
                            pool.sem_inc(passed, 1)
                            scatter(i * UNROLL + j, j, rnd * EXP + i * UNROLL + j + 1)

                        def turn(i):
                            for j in range(UNROLL):
                                ahead(i, j)
                                if j > 0:
                                    store(i, j - 1)
                                elif i is not FIRST:
                                    store(i - 1, UNROLL - 1)

                        turn(FIRST)
                        with pool.Fori(1, TURNS) as i:
                            turn(i)
                        store(TURNS - 1, UNROLL - 1)
                        for j in range(UNROLL):
                            pool.wait_ge(gdma[j], 16 * (rnd + 1) * (TURNS + 1))
                            pool.wait_ge(sdma[j], 16 * (rnd + 1) * TURNS)
                        pool.sem_inc(passed, 1)

                    load_table(0)
                    pool.wait_ge(idx_ok, 3)
                    pool.wait_ge(gath_ok, 2)
                    pool.wait_ge(h2_dma[0], 32)
                    pool.wait_ge(h2_dma[1], 32)
                    turns(FIRST)
                    most = pool.value_load(cmax[0:1, 0:1], min_val=0, max_val=T)
                    with pool.Fori(1, ROUNDS) as rnd:
                        with pool.If(most > rnd * SLOTS):
                            load_table(rnd)
                            pool.wait_ge(idx_ok, rnd * 3 + 3)
                            pool.sem_inc(passed, 1)
                            turns(rnd)
                    pool.sem_inc(moe_done, 1)
                    pool.dma_reset(sem_range)

            nc.all_engine_barrier(sems_to_clear=sem_range)

        out_sem = ctx.enter_context(nc.semaphore("out_stored"))
        with nc.Block() as block:
            @block.sync
            def _(sp):
                sp.dma_start(out[0].rearrange("(t p) d -> p t d", p=P), X[:, :, :]).then_inc(out_sem, 16)
                sp.wait_ge(out_sem, 16)


_INS = ["x", "attn_norm", "w_in", "b_gate", "a_q_norm", "a_k_norm", "a_sinks", "rel_bias", "w_oa",
        "q_a_norm", "w_qb", "kv_a_norm", "w_kvb", "b_q_norm", "b_k_norm", "w_ob", "w_o", "ffn_norm",
        "w_router_group", "b_router_group", "w_router_expert", "b_router_expert", "w_exp_gate",
        "w_exp_up", "w_exp_down"]


def kernel(**inputs):
    import concourse.bacc as bacc
    from concourse.bass_utils import run_bass_kernel_spmd

    nc = bacc.Bacc("TRN2", target_bir_lowering=False, num_devices=1)
    arrays = {name: np.ascontiguousarray(inputs[name]) for name in _INS}
    arrays["consts"], arrays["hot"] = constants()
    args = [nc.dram_tensor(f"{n}_dram", a.shape, mybir.dt.from_np(a.dtype), kind="ExternalInput").ap()
            for n, a in arrays.items()]
    out = nc.dram_tensor("out_dram", (1, T, D), F32, kind="ExternalOutput").ap()
    trunk(nc, *args, out)
    r = run_bass_kernel_spmd(nc, [{f"{n}_dram": a for n, a in arrays.items()}], core_ids=[0])
    return r.results[0]["out_dram"]
```

```python
import math
from contextlib import ExitStack

import numpy as np

import concourse.bass as bass
from concourse import mybir

F32 = mybir.dt.float32
F32R = mybir.dt.float32r
BF16 = mybir.dt.bfloat16
I32 = mybir.dt.int32
ALU = mybir.AluOpType
ACT = mybir.ActivationFunctionType
AX = mybir.AxisListType.X

P = 128
D = 1024
T = 512
TT = T // P
KD = D // P
L = 2
AH, AKV, AD = 8, 2, 64
WINDOW = 128
BUCKETS, MAX_DIST = 32, 128
BH, QL, KVL, NOPE, ROPE, VD = 8, 256, 128, 64, 32, 64
QK = NOPE + ROPE
THETA = 10000.0
GROUPS, PER_GROUP = 4, 8
EXP = GROUPS * PER_GROUP
FE = 256
EPS = 1e-6
A_SCALE = AD ** -0.5
B_SCALE = QK ** -0.5
NEG = -1e30

C_KPE = 1152
C_GATE = 1184
GROUP_N = 512

SLOTS = 64
ROUNDS = T // SLOTS
UNROLL = 4
TURNS = EXP // UNROLL
EXTRA = UNROLL
PAD = 4096
FIRST = 0
XPER = EXP + 1
CREDIT = UNROLL

CONST = {}
_at = 0
for _name, _n in (("ident", P), ("causal", P), ("before", P), ("ones", P), ("cos", TT * ROPE // 2),
                  ("sin", TT * ROPE // 2), ("iota4", GROUPS), ("iota8", PER_GROUP), ("iota32", EXP),
                  ("half", 1), ("rowid", 2 * TT), ("iota_slot", P)):
    CONST[_name] = (_at, _n)
    _at += _n
N_CONST = _at
BIAS_W = 384


def constants():
    c = np.zeros((P, N_CONST), np.float32)

    def put(name, v):
        a, n = CONST[name]
        c[:, a:a + n] = v

    i = np.arange(P)
    put("ident", np.eye(P))
    put("causal", np.where(i[None, :] <= i[:, None], 0.0, NEG))
    put("before", i[:, None] < i[None, :])
    put("ones", 1.0)
    half = ROPE // 2
    freq = np.float32(THETA) ** (-np.arange(half, dtype=np.float32) / np.float32(half))
    ang = np.arange(T, dtype=np.float32)[:, None] * freq[None, :]
    fold = lambda a: a.reshape(TT, P, half).transpose(1, 0, 2).reshape(P, TT * half)
    put("cos", fold(np.cos(ang)))
    put("sin", fold(np.sin(ang)))
    put("iota4", np.arange(GROUPS))
    put("iota8", np.arange(PER_GROUP))
    put("iota32", np.arange(EXP))
    put("half", (i >= SLOTS)[:, None])
    rows = 2 * (i[:, None, None] + P * np.arange(TT)[None, :, None]) + np.arange(2)[None, None, :]
    put("rowid", rows.reshape(P, 2 * TT) - PAD)
    put("iota_slot", i % SLOTS)
    hot = np.zeros((BUCKETS + 1, BIAS_W), np.float32)
    exact = BUCKETS // 2
    for col in range(BIAS_W - 1):
        d = 2 * P - 1 - col
        if 0 <= d < WINDOW:
            ratio = np.float32(max(d, 1)) / np.float32(exact)
            large = exact + int(np.log(ratio) / np.float32(math.log(MAX_DIST / exact))
                                * np.float32(BUCKETS - exact))
            hot[d if d < exact else min(large, BUCKETS - 1), col] = 1.0
        else:
            hot[BUCKETS, col] = NEG
    return c, hot


class Chain:

    def __init__(self, eng, sem):
        self.eng, self.sem, self.n = eng, sem, 0

    def step(self, ins):
        ins.then_inc(self.sem, 1)
        self.n += 1
        self.eng.wait_ge(self.sem, self.n)


def trunk(nc, x, attn_norm, w_in, b_gate, a_q_norm, a_k_norm, a_sinks, rel_bias, w_oa, q_a_norm,
          w_qb, kv_a_norm, w_kvb, b_q_norm, b_k_norm, w_ob, w_o, ffn_norm, w_rg, b_rg, w_re, b_re,
          w_gate, w_up, w_down, consts, hot, out):
    h_dram = nc.dram_tensor("h_rows", (2 * T, D // 2), F32).ap()
    y_dram = nc.dram_tensor("y_rows", (4 * T, D // 2), F32).ap()
    bias_dram = nc.dram_tensor("bias_rows", (AH, P, BIAS_W), F32).ap()

    with ExitStack() as ctx:
        base = (nc.sbuf_base + 63) // 64 * 64

        def at(name, shape, dt, off):
            return nc.alloc_sbuf_tensor_at(name, shape, dt, offset=base + off)

        K = 1024
        ring = at("ring", [P, 24 * K], F32, 0)
        qkT = at("qkT", [P, 2 * BH, T], F32, 64 * K)
        X = at("x_rows", [P, TT, D], F32, 96 * K)
        hT = at("hT", [P, KD, T], F32, 112 * K)
        yld = at("y_loaded", [P, TT, 2, D], F32, 112 * K)
        oab = at("oabT", [P, 2, 4, T], F32, 128 * K)
        oaT, obT = oab[:, 0], oab[:, 1]
        rope_t = at("rope_tmp", [P, 4, 2 * BH, ROPE // 2], F32, 136 * K)
        vB = at("vB", [P, TT, BH * VD], F32, 144 * K)
        cqT = at("cqT", [P, 2, T], F32, 152 * K)
        ckvT = at("ckvT", [P, T], F32, 156 * K)
        qTA = at("qTA", [P, 4, T], F32, 158 * K)
        kTA = at("kTA", [P, T], F32, 166 * K)
        vA = at("vA", [P, TT, P], F32, 168 * K)
        gate_t = [at("gate_tanh0", [P, 4, 2, T], F32, 16 * K), at("gate_tanh1", [P, 4, 2, T], F32, 152 * K)]
        fsq = at("ffn_squares", [P, D], F32, 148 * K)
        hT_hi = at("hT_hi", [P, KD, T], F32R, 64 * K)
        hT_lo = at("hT_lo", [P, KD, T], F32R, 80 * K)
        c_hi = [at("c0_hi", [P, KD, 512], F32R, 128 * K), at("c1_hi", [P, KD, 512], F32R, 48 * K)]
        c_lo = [at("c0_lo", [P, KD, 512], F32R, 0), at("c1_lo", [P, KD, 512], F32R, 16 * K)]
        oab_hi = at("oabT_hi", [P, 2, 4, T], F32R, 112 * K)
        oab_lo = at("oabT_lo", [P, 2, 4, T], F32R, 128 * K)
        WAB = [3, 0]
        wab_hi = at("w_oab_hi", [P, 2, 2, 4, P], F32R, 188 * K)
        wab_lo = [at(f"w_oab_lo{z}", [P, 4, D], F32R, 16 * s_ * K) for z, s_ in enumerate(WAB)]
        mT_hi = [at("mergedT_hi0", [P, 4, 2, T], F32R, 16 * K), at("mergedT_hi1", [P, 4, 2, T], F32R, 152 * K)]
        WO = [4, 5]
        wo_hi = [at("w_o_hi0", [P, KD, 512], F32R, 32 * K), at("w_o_hi1", [P, KD, 512], F32R, 0)]
        wo_lo = [at(f"w_o_lo{n_}", [P, KD, 512], F32R, 16 * s_ * K) for n_, s_ in enumerate(WO)]
        xn = at("xn", [P, TT, D], F32, 170 * K)
        sq = at("sq", [P, 2, T], F32, 170 * K)
        qn = at("qn", [P, 2, T], F32, 174 * K)
        qk = at("qk_rows", [P, 2, 2 * BH, QK], F32, 170 * K)
        sq2 = at("sq2", [P, 2 * BH, QK], F32, 182 * K)
        pr = at("probs", [P, 4, T], F32, 170 * K)
        pT = at("probsT", [P, 4, T], F32, 178 * K)
        mT_lo = at("mergedT_lo", [P, KD, T], F32R, 170 * K)
        gath = at("gathered", [P, UNROLL, T], F32, 170 * K)
        xeT = at("xeT", [P, 2, 4, P], F32, 178 * K)
        gtmp = at("gu_half", [P, 2, T], F32, 182 * K)
        gsum = at("gu", [P, T], F32, 186 * K)
        gsum2 = at("gu2", [P, T], F32, 144 * K)
        gexp = at("silu_tmp", [P, 2, FE], F32, 146 * K)
        hrow = at("h_expert", [P, 2, FE], F32, 148 * K)
        heT = at("heT", [P, 2, 2, SLOTS], F32, 150 * K)
        ye = at("y_expert", [P, UNROLL, T], F32, 128 * K)
        h2 = at("h2_rows", [P, TT, D], F32, 128 * K)
        hot2 = at("hot_experts", [P, 2, TT, EXP], F32, 152 * K)
        slot_rows = at("slot_rows", [P, 2, TT, P], F32, 153 * K)
        gu_rows = [gsum, gsum2]
        bias = at("bias", [P, AH, 2 * P], F32, 188 * K)
        misc = 196 * K
        sizes = {}

        def small(name, shape, dt=F32):
            nonlocal misc
            n = 1
            for s in shape[1:]:
                n *= s
            t = at(name, shape, dt, misc)
            misc += (n * mybir.dt.size(dt) + 31) // 32 * 32
            return t

        cst = small("cst", [P, N_CONST])
        causal_bf = small("causal_bf", [P, P], BF16)
        ident_bf = small("ident_bf", [P, P], BF16)
        before_bf = small("before_bf", [P, P], BF16)
        ones_bf = small("ones_bf", [P, P], BF16)
        minus_half = small("minus_half", [P, 48])
        colrows = at("colrows", [28, P], F32, 187 * K)
        cols = small("cols", [P, 28])
        hbg = small("half_b_gate", [P, 16])
        gainA = small("gainA", [P, 2, AD])
        gainB = small("gainB", [P, 2, QK])
        nsink = small("neg_sink", [P, AH])
        rbias = small("router_bias", [P, GROUPS + EXP])
        kpe = small("kpe", [P, TT, ROPE])
        stats = small("stats", [P, 64])
        st1 = small("st1", [P, 12, 9])
        idx_g = small("idx_gather", [P, EXP + EXTRA], I32)
        idx_s = small("idx_scatter", [P, EXP + EXTRA], I32)
        cur_g = small("cur_gather", [P, UNROLL], I32)
        cur_s = small("cur_scatter", [P, UNROLL], I32)
        wts = small("weights", [P, 2, TT])
        rank = small("ranks", [P, 2, TT])
        cmax = small("count_max", [P, 1], I32)
        assert base + misc <= nc.sbuf_usable_end, (base + misc, nc.sbuf_usable_end)
        wr = at("w_router", [P, KD, GROUPS + EXP], F32, 168 * K)
        gffn = at("gain_ffn", [P, D], F32, 144 * K)
        unit = at("unit_stats", [P, 48, 8], F32, 186 * K)
        rt = at("routing", [P, 2048], F32, 178 * K)
        pre_rel = at("rel_rows", [BUCKETS + 1, AH], F32, 170 * K)
        pre_hot = at("hot_rows", [BUCKETS + 1, BIAS_W], F32, 171 * K)
        pre_bias = at("bias_sb", [AH, BIAS_W], F32, 188 * K)
        assert base + misc <= nc.sbuf_usable_end, (base + misc, nc.sbuf_usable_end)

        def C(name):
            a, n = CONST[name]
            return cst[:, a:a + n]

        ident = C("ident")
        cosv = C("cos").rearrange("p (t c) -> p t c", t=TT)
        sinv = C("sin").rearrange("p (t c) -> p t c", t=TT)

        bank = [ctx.enter_context(nc.psum_tensor(f"bank{i}", [P, 512], F32)) for i in range(8)]

        def slot(s, n=4096, off=0):
            return ring[:, s * 4096 + off:s * 4096 + off + n]

        EXP_OFF = [2 * 6144, 0, 6144, 3 * 6144]

        pre_dma, pre_c, pre_b, pre_v = (ctx.enter_context(nc.semaphore(n)) for n in
                                        ("pre_dma", "pre_consts", "pre_bias", "pre_vec"))
        x_ld, bias_st, rows_ld, c0_ld, out_st = (ctx.enter_context(nc.semaphore(n)) for n in (
            "x_loaded", "bias_stored", "colrows_loaded", "c0_loaded", "out_stored"))

        def load_first(sp, layer):
            for dst, src in ((colrows[0:8, :], attn_norm[layer].rearrange("(k p) -> k p", p=P)),
                             (colrows[8:24, :], b_gate[layer].rearrange("(k p) -> k p", p=P)),
                             (colrows[24:26, :], q_a_norm[layer].rearrange("(k p) -> k p", p=P)),
                             (colrows[26:27, :], kv_a_norm[layer].unsqueeze(0)),
                             (gainA[:, 0, :], a_q_norm[layer].unsqueeze(0).broadcast_to([P, AD])),
                             (gainA[:, 1, :], a_k_norm[layer].unsqueeze(0).broadcast_to([P, AD]))):
                sp.dma_start(dst, src).then_inc(rows_ld, 16)
            sp.dma_start(slot(0).rearrange("p (k n) -> p k n", k=KD),
                         w_in[layer].rearrange("(k p) n -> p k n", p=P)[:, :, 0:512]).then_inc(c0_ld, 16)

        with nc.Block() as block:
            @block.sync
            def _(sp):
                sp.dma_start(pre_hot[:, :], hot).then_inc(pre_dma, 16)
                sp.dma_start(pre_rel[0:BUCKETS, :], rel_bias).then_inc(pre_dma, 16)
                sp.dma_start(cst[:, :], consts).then_inc(pre_dma, 16)
                sp.dma_start(X[:, :, :], x[0].rearrange("(t p) d -> p t d", p=P)).then_inc(x_ld, 16)
                load_first(sp, FIRST)
                sp.wait_ge(pre_v, 5)
                sp.dma_start(bias_dram, pre_bias[:, :].unsqueeze(1).broadcast_to([AH, P, BIAS_W])).then_inc(bias_st, 16)

            @block.vector
            def _(dve):
                dve.memset(pre_rel[BUCKETS:BUCKETS + 1, :], 1.0).then_inc(pre_c, 1)
                dve.memset(minus_half[:, :], -0.5).then_inc(pre_c, 1)
                dve.memset(idx_g[:, :], PAD).then_inc(pre_c, 1)
                dve.memset(idx_s[:, :], PAD).then_inc(pre_c, 1)
                dve.wait_ge(pre_dma, 48)
                dve.tensor_copy(causal_bf[:, :], C("causal")).then_inc(pre_v, 1)
                dve.tensor_copy(ident_bf[:, :], ident).then_inc(pre_v, 1)
                dve.tensor_copy(before_bf[:, :], C("before")).then_inc(pre_v, 1)
                dve.tensor_copy(ones_bf[:, :], C("ones")).then_inc(pre_v, 1)
                dve.wait_ge(pre_b, 1)
                dve.tensor_copy(pre_bias[:, :], bank[0][0:AH, 0:BIAS_W]).then_inc(pre_v, 1)

            @block.tensor
            def _(pe):
                pe.wait_ge(pre_dma, 48)
                pe.wait_ge(pre_c, 1)
                pe.matmul(bank[0][0:AH, 0:BIAS_W], pre_rel[:, :], pre_hot[:, :],
                          start=True, stop=True).then_inc(pre_b, 1)

        names = []

        def sem(name):
            s = ctx.enter_context(nc.semaphore(name))
            names.append(s)
            return s

        WCH = ["c1", "c2", "woa", "wob", "g0", "g2", "g1", "g3", "wo0", "wo1"]
        w_in_dma = {n: sem(f"loaded_{n}") for n in WCH}
        small_ld = sem("small_loaded")
        late_ld = sem("late_loaded")
        x_sq, rs_x, xn_ok, hT_ps, hT_ok = (sem(n) for n in ("x_sq", "rs_x", "xn_ok", "hT_ps", "hT_ok"))
        cols_ps, cols_ok = sem("cols_ps"), sem("cols_ok")
        pj, pj_act, pj_ss, pj_rs, pj_dve, qn_ok, tpj, tp_read = (sem(n) for n in (
            "proj", "proj_act", "proj_sums", "proj_rstd", "proj_dve", "qn_ok", "proj_T", "proj_T_read"))
        p2, p2_act, p2_dve, p2_kpe, p2_sq, p2_ss, p2_rs, p2_rope, p2_tp, p2_te = (sem(n) for n in (
            "mla", "mla_act", "mla_dve", "mla_kpe", "mla_sq", "mla_sums", "mla_rstd",
            "mla_rope", "mla_T", "mla_T_read"))
        sc, mx, ex, pn, tp, te, pv, pvu, oe = (sem(n) for n in (
            "scores", "maxima", "exps", "probs_ok", "probsT_ps", "probsT_ok", "pv_group", "pv_unit", "o_read"))
        gates_ps, ge, y_ps, mg = (sem(n) for n in ("gates_ps", "gate_tanh", "y_ps", "merged"))
        hT_h, hT_l, c0_h, c0_l, c1_h, c1_l = (sem(n) for n in (
            "hT_hi_ok", "hT_lo_ok", "c0_hi_ok", "c0_lo_ok", "c1_hi_ok", "c1_lo_ok"))
        oab_h, oab_l, wab_h, wab_l = (sem(n) for n in ("oabT_hi_ok", "oabT_lo_ok", "w_oab_hi_ok", "w_oab_lo_ok"))
        wo_h, wo_l = ([sem(f"w_o_{n}{i}_ok") for i in range(2)] for n in ("hi", "lo"))
        wo_ps, xw = sem("wo_ps"), sem("x_mixed")
        f_sq, f_rs, h2_ok, h2t_ps, h2T_ok, lg_ps, h2_dma = (sem(n) for n in (
            "f_sq", "f_rstd", "h2_ok", "h2T_ps", "h2T_ok", "logits_ps", "h2_stored"))
        r_exp_in, r_exp_out, onehots, ranks_ps, counts_ok = (sem(n) for n in (
            "r_exp_in", "r_exp_out", "onehots", "ranks_ps", "counts_ok"))
        srow_ok, tbl_ps, idx_ok, round_done = (sem(n) for n in (
            "slot_rows_ok", "table_ps", "idx_ok", "round_done"))
        wload = [sem(f"expert_loaded{j}") for j in range(UNROLL)]
        gdma = [sem(f"gathered{j}") for j in range(UNROLL)]
        sdma = [sem(f"scattered{j}") for j in range(UNROLL)]
        cg, cs_, xtp, xte, gu, gcp, gsm, gex, silu2, hh, htp, hte, yp, yev = (sem(n) for n in (
            "cur_g", "cur_s", "e_xT_ps", "e_xT_ok", "e_gu_ps", "e_gu_half", "e_gu_ok", "e_tanh",
            "e_silu", "e_h", "e_hT_ps", "e_hT_ok", "e_y_ps", "e_y_ok"))
        experts_done, moe_done = sem("experts_done"), sem("moe_done")
        bias_ld = sem("bias_loaded")
        yl = [sem(f"y_loaded{i}") for i in range(TT)]
        comb = sem("combined")
        dch, ach, pch = sem("dve_chain"), sem("act_chain"), sem("pool_chain")
        gath_ok = sem("gather_cleared")
        passed = sem("pool_passed")
        pe_passed = sem("pe_passed")
        sem_range = range(names[0].num, names[-1].num + 1)
        assert len(sem_range) == len(names)

        UNITS = [("A", n, g, jj) for n in range(TT) for g in range(AKV) for jj in range(2)] + \
                [("B", h, n, 0) for h in range(BH) for n in range(TT)]
        NU = len(UNITS)
        GROUP_OF = [u // 4 if u < 16 else 4 + (u - 16) // 8 for u in range(NU)]
        LAST_OF = [u == NU - 1 or GROUP_OF[u] != GROUP_OF[u + 1] for u in range(NU)]

        def wab_tile(z, m):
            return slot(WAB[z]).rearrange("p (k n) -> p k n", k=4)[:, :, m * P:(m + 1) * P]

        def wo_tile(nh, k):
            return slot(WO[nh])[:, k * 512:(k + 1) * 512]

        MLA_JOBS = TT
        STEPS = NU + 3
        JOBS = 2 * KD
        GATE_MM = JOBS * KD
        GATES_END = STEPS - 4
        UNIT_MM = GATE_MM - MLA_JOBS * KD
        GATE_DONE = [MLA_JOBS * KD + min(UNIT_MM, -(-UNIT_MM * s_ // (GATES_END - 1))) for s_ in range(STEPS)]
        GATE_JOBS_DONE = [n_ // KD for n_ in GATE_DONE]

        def gate_job(q):
            c_, j_ = divmod(q, 4)
            z_ = c_ % 2
            b_ = bank[7] if q < MLA_JOBS else bank[6 + q % 2]
            return 2 * z_, j_ * P, gate_t[c_ // 2][:, j_, z_, :], 4 * (c_ // 2) + j_, z_, b_

        with nc.Fori(0, L) as l:
            with nc.Block() as block:
                @block.sync
                def _(sp):
                    def w_in_cols(a, n):
                        return w_in[l].rearrange("(k p) n -> p k n", p=P)[:, :, a:a + n]

                    def k_view(s, n, off=0, k=KD):
                        return slot(s, k * n, off).rearrange("p (k n) -> p k n", k=k)

                    def load(name, *pairs):
                        for dst, src in pairs:
                            sp.dma_start(dst, src).then_inc(w_in_dma[name], 16)

                    load("c1", (k_view(1, 512), w_in_cols(512, 512)))
                    load("c2", (k_view(2, 160), w_in_cols(1024, 160)),
                         (k_view(2, BH * QK, 1280, 2), w_qb[l].rearrange("(k p) n -> p k n", p=P)),
                         (slot(2, 1024, 2816), w_kvb[l]))
                    sp.wait_ge(pj, TT)
                    load("g0", (k_view(0, 512), w_in_cols(C_GATE, 512)))
                    sp.wait_ge(pj, 2 * TT)
                    oa = w_oa[l].rearrange("(g j d) n -> g d j n", g=2, j=4)
                    load("woa", *[(k_view(3, 1024, 0, 4)[g * AD:(g + 1) * AD], oa[g]) for g in range(2)])
                    sp.wait_ge(p2, TT)
                    load("g2", (k_view(2, 512), w_in_cols(C_GATE + 1024, 512)))
                    sp.wait_ge(gates_ps, 4)
                    load("g1", (k_view(0, 512), w_in_cols(C_GATE + 512, 512)))
                    sp.wait_ge(gates_ps, 8)
                    load("g3", (k_view(2, 512), w_in_cols(C_GATE + 1536, 512)))
                    sp.wait_ge(gates_ps, 12)
                    load("wob", (k_view(0, 1024, 0, 4), w_ob[l].rearrange("(k p) n -> p k n", p=P)))
                    sp.wait_ge(sc, NU)
                    wo_v = w_o[l].rearrange("(k p) n -> p k n", p=P)
                    load("wo0", (k_view(4, 512), wo_v[:, :, 0:512]))
                    load("wo1", (k_view(5, 512), wo_v[:, :, 512:1024]))
                    sp.wait_ge(mg, 1)
                    sp.dma_start(wr[:, :, 0:GROUPS], w_rg[l].rearrange("(k p) n -> p k n", p=P)).then_inc(late_ld, 16)
                    sp.dma_start(wr[:, :, GROUPS:], w_re[l].rearrange("(k p) n -> p k n", p=P)).then_inc(late_ld, 16)
                    sp.dma_start(gffn[:, :], ffn_norm[l].unsqueeze(0).broadcast_to([P, D])).then_inc(late_ld, 16)

                    def load_expert(e, j):
                        o = EXP_OFF[j]
                        for k, w in enumerate((w_gate, w_up)):
                            sp.dma_start(ring[:, o + 2048 * k:o + 2048 * (k + 1)].rearrange("p (n c) -> p n c", n=2),
                                         w[l, e].rearrange("(n p j) f -> p n (j f)", n=2, j=4)).then_inc(wload[j], 16)
                        sp.dma_start(ring[:, o + 4096:o + 6144],
                                     w_down[l, e].rearrange("(p k) n -> p (k n)", k=2)).then_inc(wload[j], 16)

                    def turns(rnd):
                        for j in range(UNROLL):
                            if rnd is FIRST:
                                if j == 0:
                                    sp.wait_ge(wo_ps, 4)
                                if j == 1:
                                    sp.wait_ge(wo_ps, 8)
                                if j == 3:
                                    sp.wait_ge(gdma[0], 16)
                            else:
                                sp.wait_ge(yp, rnd * EXP + j + 1)
                            load_expert(j, j)
                        with sp.Fori(1, TURNS) as i:
                            for j in range(UNROLL):
                                sp.wait_ge(yp, rnd * EXP + i * UNROLL + j + 1)
                                load_expert(i * UNROLL + j, j)

                    turns(FIRST)
                    sp.wait_ge(counts_ok, 1)
                    most = sp.value_load(cmax[0:1, 0:1], min_val=0, max_val=T)
                    with sp.If(most > SLOTS):
                        with sp.Fori(1, ROUNDS) as rnd:
                            with sp.If(most > rnd * SLOTS):
                                turns(rnd)
                        sp.wait_ge(experts_done, 1)
                    sp.wait_ge(yp, EXP - 1 + CREDIT)
                    with sp.Fori(1, L) as following:
                        with sp.If(following == l + 1):
                            load_first(sp, following)
                    sp.wait_ge(moe_done, 1)
                    yv = y_dram.rearrange("(t p k h) c -> t p k (h c)", p=P, k=2, h=2)
                    for tt in range(TT):
                        sp.dma_start(yld[:, tt], yv[tt]).then_inc(yl[tt], 16)
                    for tt in range(TT):
                        sp.wait_ge(yl[tt], 16)
                    with sp.If(l == L - 1):
                        for tt in range(TT):
                            sp.wait_ge(comb, tt + 1)
                            sp.dma_start(out[0, tt * P:(tt + 1) * P, :], X[:, tt, :]).then_inc(out_st, 16)
                        sp.wait_ge(out_st, 16 * TT)

                @block.scalar
                def _(act):
                    act.wait_ge(x_ld, 16)
                    for tt in range(TT):
                        act.activation(hT[:, 2 * tt:2 * tt + 2, :], X[:, tt, :].rearrange("p (a b) -> p a b", a=2),
                                       ACT.Square, accum_out=stats[:, tt:tt + 1]).then_inc(x_sq, 1)
                    def c0_hi(k):
                        act.activation(c_hi[0][:, k, :], slot(0)[:, k * 512:(k + 1) * 512], ACT.Copy).then_inc(c0_h, 1)

                    def x_hi(i):
                        tt, kh = divmod(i, 2)
                        act.wait_ge(hT_ok, i + 1)
                        act.activation(hT_hi[:, 4 * kh:4 * kh + 4, tt * P:(tt + 1) * P],
                                       hT[:, 4 * kh:4 * kh + 4, tt * P:(tt + 1) * P], ACT.Copy).then_inc(hT_h, 1)

                    x_hi(0)
                    x_hi(1)
                    act.wait_ge(c0_ld, 16 * (l + 1))
                    for k in range(KD):
                        c0_hi(k)
                    for i in range(2, 2 * TT):
                        x_hi(i)
                    for dst, src in (
                        (gainB[:, 0, :], b_q_norm[l].unsqueeze(0).broadcast_to([P, QK])),
                        (gainB[:, 1, :], b_k_norm[l].unsqueeze(0).broadcast_to([P, QK])),
                        (nsink[:, :], a_sinks[l].unsqueeze(0).broadcast_to([P, AH])),
                        (rbias[:, 0:GROUPS], b_rg[l].unsqueeze(0).broadcast_to([P, GROUPS])),
                        (rbias[:, GROUPS:], b_re[l].unsqueeze(0).broadcast_to([P, EXP])),
                    ):
                        act.dma_start(dst, src).then_inc(small_ld, 16)
                    act.wait_ge(bias_st, 16)
                    act.dma_start(bias[:, :, :], bass.AP(bias_dram.tensor, P - 1, [[BIAS_W - 1, P], [P * BIAS_W, AH], [1, 2 * P]]))\
                        .then_inc(bias_ld, 16)

                    for i in range(3 * TT):
                        c, tt = divmod(i, TT)
                        b = bank[i % 4]
                        act.wait_ge(pj, i + 1)
                        if i >= 2:
                            act.wait_ge(pj_ss, i - 1)
                        if i == 0:
                            act.wait_ge(hT_ps, 8)
                            act.wait_ge(w_in_dma["c1"], 16)
                        if i < TT:
                            for k in (2 * i, 2 * i + 1):
                                act.activation(c_hi[1][:, k, :], slot(1)[:, k * 512:(k + 1) * 512],
                                               ACT.Copy).then_inc(c1_h, 1)
                        if c == 0:
                            act.activation(sq[:, i % 2, :], b[:, :], ACT.Square).then_inc(pj_act, 1)
                        elif c == 1:
                            act.activation(sq[:, i % 2, 0:P], b[:, 0:P], ACT.Square)
                            act.activation(sq[:, i % 2, QL:2 * QL], b[:, QL:2 * QL], ACT.Square,
                                           accum_out=st1[:, i, 8:9])
                            act.activation(vA[:, tt, :], b[:, P:2 * P], ACT.Copy).then_inc(pj_act, 1)
                        else:
                            act.activation(sq[:, i % 2, 0:KVL], b[:, 0:KVL], ACT.Square,
                                           accum_out=st1[:, i, 8:9])
                            act.activation(kpe[:, tt, :], b[:, KVL:KVL + ROPE], ACT.Copy).then_inc(pj_act, 1)

                    def gate_tanh(q):
                        _, _, dst, m, z, b = gate_job(q)
                        act.wait_ge(gates_ps, q + 1)
                        if q == 2 * 4:
                            act.wait_ge(sc, 16)
                        act.activation(dst, b[:, :], ACT.Tanh, bias=hbg[:, 8 * z + m:8 * z + m + 1],
                                       scale=0.5).then_inc(ge, 1)

                    def mla_T(tt):
                        for b in range(4):
                            act.wait_ge(p2_tp, 4 * tt + b + 1)
                            act.activation(qkT[0:QK, 4 * b:4 * b + 4, tt * P:(tt + 1) * P],
                                           bank[4 + (4 * tt + b) % 3][0:QK, :].rearrange("p (h q) -> p h q", h=4),
                                           ACT.Copy).then_inc(p2_te, 1)

                    def mla_rows(tt):
                        act.wait_ge(p2, tt + 1)
                        if tt == 0:
                            act.wait_ge(tpj, 12)
                            act.wait_ge(pj_ss, 12)
                        if tt >= 2:
                            act.wait_ge(p2_tp, 4 * (tt - 1))
                        for b in range(2):
                            kv = bank[2 + b][:, :].rearrange("p (h d) -> p h d", h=4)
                            act.activation(qk[:, tt % 2, BH + 4 * b:BH + 4 * b + 4, 0:NOPE], kv[:, :, 0:NOPE], ACT.Copy)
                            ins = act.activation(vB[:, tt, 4 * b * VD:4 * (b + 1) * VD].rearrange("p (h d) -> p h d", h=4),
                                                 kv[:, :, NOPE:], ACT.Copy)
                        ins.then_inc(p2_act, 1)
                        act.activation(qk[:, tt % 2, BH:, NOPE:], kpe[:, tt, :].unsqueeze(1).broadcast_to([P, BH, ROPE]),
                                       ACT.Copy).then_inc(p2_kpe, 1)
                        act.wait_ge(p2_act, tt + 1)
                        act.wait_ge(p2_dve, tt + 1)
                        act.wait_ge(p2_kpe, tt + 1)
                        if tt >= 1:
                            act.wait_ge(p2_ss, tt)
                        act.activation(sq2[:, :, :], qk[:, tt % 2, :, :], ACT.Square).then_inc(p2_sq, 1)

                    mla_rows(0)
                    mla_rows(1)
                    gate_tanh(0)
                    mla_T(0)
                    mla_rows(2)
                    gate_tanh(1)
                    mla_T(1)
                    mla_rows(3)
                    gate_tanh(2)
                    gate_tanh(3)
                    mla_T(2)
                    mla_T(3)

                    def exp_unit(u):
                        kind, a, b_, c_ = UNITS[u]
                        act.wait_ge(mx, u + 1)
                        if kind == "A":
                            w = P if a == 0 else 2 * P
                            for hh in range(2):
                                act.activation(pr[:, u % 4, hh * w:(hh + 1) * w], pr[:, u % 4, hh * w:(hh + 1) * w],
                                               ACT.Exp, bias=unit[:, u, hh:hh + 1], accum_out=unit[:, u, 4 + hh:5 + hh])
                            act.activation(unit[:, u, 6:8], unit[:, u, 2:4], ACT.Exp).then_inc(ex, 1)
                        else:
                            w = P * (b_ + 1)
                            if u >= 4:
                                act.wait_ge(tp, u - 3)
                            act.activation(pr[:, u % 4, 0:w], bank[u % 3][:, 0:w], ACT.Exp, bias=unit[:, u, 0:1],
                                           scale=B_SCALE, accum_out=unit[:, u, 4:5]).then_inc(ex, 1)

                    def probsT(u):
                        act.wait_ge(tp, u + 1)
                        if u >= 4:
                            act.wait_ge(pvu, u - 3)
                        kind, a, b_, c_ = UNITS[u]
                        w = (2 * P if a == 0 else 4 * P) if kind == "A" else P * (b_ + 1)
                        act.activation(pT[:, u % 4, 0:w], bank[3 + u % 2][:, 0:w], ACT.Copy).then_inc(te, 1)

                    def o_out(G):
                        act.wait_ge(pv, G + 1)
                        b = bank[5]
                        if G < 4:
                            act.activation(oaT[:, :, G * P:(G + 1) * P], b[:, :].rearrange("p (j q) -> p j q", j=4),
                                           ACT.Copy).then_inc(oe, 1)
                        else:
                            act.activation(obT[:, G - 4, :], b[:, :], ACT.Copy).then_inc(oe, 1)

                    def wab_split(m):
                        if m == 0:
                            act.wait_ge(mx, 16)
                            act.wait_ge(w_in_dma["woa"], 32)
                            act.wait_ge(w_in_dma["wob"], 16)
                        if m >= 2:
                            act.wait_ge(y_ps, m - 1)
                        for z in range(2):
                            ins = act.activation(wab_hi[:, m % 2, z, :, :], wab_tile(z, m), ACT.Copy)
                        ins.then_inc(wab_h, 1)

                    oab_done = 0

                    def oab_split():
                        nonlocal oab_done
                        z, k = divmod(oab_done, 4)
                        if oab_done == 0:
                            act.wait_ge(gates_ps, JOBS)
                        act.wait_ge(oe, 4 + k + 1 if z else 4)
                        act.activation(oab_hi[:, z, k, :], oab[:, z, k, :], ACT.Copy).then_inc(oab_h, 1)
                        oab_done += 1

                    done = MLA_JOBS
                    for s in range(NU + 4):
                        if 0 <= s - 4 < NU and LAST_OF[s - 4]:
                            o_out(GROUP_OF[s - 4])
                        if s < NU:
                            exp_unit(s)
                        if 0 <= s - 2 < NU:
                            probsT(s - 2)
                        while s >= 1 and done < GATE_JOBS_DONE[min(s, STEPS) - 1]:
                            gate_tanh(done)
                            done += 1
                        if s in (NU - 6, NU - 3):
                            wab_split(0 if s == NU - 6 else 1)
                        for _ in range(2):
                            if s > GATES_END + 1 and oab_done < 7:
                                oab_split()

                    while oab_done < 8:
                        oab_split()
                    act.wait_ge(w_in_dma["wo0"], 16)
                    for m in range(KD):
                        if m >= 2:
                            wab_split(m)
                        act.activation(wo_hi[0][:, m, :], wo_tile(0, m), ACT.Copy).then_inc(wo_h[0], 1)
                    act.wait_ge(w_in_dma["wo1"], 16)
                    act.wait_ge(y_ps, KD)
                    for k in range(KD):
                        act.activation(wo_hi[1][:, k, :], wo_tile(1, k), ACT.Copy).then_inc(wo_h[1], 1)

                    for tt in range(TT):
                        act.wait_ge(xw, 5 + tt)
                        act.wait_ge(mg, 8)
                        act.activation(fsq[:, :], X[:, tt, :], ACT.Square, accum_out=stats[:, 8 + tt:9 + tt]).then_inc(f_sq, 1)
                        act.wait_ge(h2_ok, tt + 1)
                        act.dma_start(h_dram.rearrange("(t p h) c -> t p (h c)", p=P, h=2)[tt],
                                      h2[:, tt, :]).then_inc(h2_dma, 16)
                        for b in range(2):
                            act.wait_ge(h2t_ps, 2 * tt + b + 1)
                            act.activation(hT[:, 4 * b:4 * b + 4, tt * P:(tt + 1) * P],
                                           bank[2 * (tt % 2) + b][:, :].rearrange("p (k q) -> p k q", k=4),
                                           ACT.Copy).then_inc(h2T_ok, 1)
                    act.wait_ge(r_exp_in, 1)
                    act.activation(rt[:, 16:32], rt[:, 0:16], ACT.Exp).then_inc(r_exp_out, 1)
                    act.wait_ge(r_exp_in, 2)
                    act.activation(rt[:, 36:40], rt[:, 32:36], ACT.Exp).then_inc(r_exp_out, 1)

                    for s in (xte, gcp, gex, hte, yev):
                        act.sem_inc(s, CREDIT)

                    def turns(rnd):
                        def xT_out(i, j):
                            act.wait_ge(xtp, rnd * XPER + i * UNROLL + j + 1 + CREDIT)
                            act.wait_ge(gu, rnd * EXP + i * UNROLL + j + 1 + CREDIT - 2)
                            act.activation(xeT[:, j % 2, :, :], bank[j % 2][:, :].rearrange("p (k q) -> p k q", k=4),
                                           ACT.Copy).then_inc(xte, 1)

                        def gu_half(v, j):
                            act.wait_ge(gu, v + CREDIT)
                            act.wait_ge(gsm, v + CREDIT - 2)
                            act.activation(gtmp[0:SLOTS, j % 2, :], bank[2 + j % 2][SLOTS:P, :], ACT.Copy).then_inc(gcp, 1)

                        def silu_tanh(v, j):
                            act.wait_ge(gsm, v + CREDIT)
                            act.activation(gexp[0:SLOTS, j % 2, :], gu_rows[j % 2][0:SLOTS, 0:FE], ACT.Tanh,
                                           scale=0.5).then_inc(gex, 1)

                        def hT_out(v, j):
                            act.wait_ge(htp, v + CREDIT)
                            act.wait_ge(yp, v + CREDIT - 2)
                            act.activation(heT[:, j % 2, :, :],
                                           bank[4 + j % 2][:, 0:2 * P].rearrange("p (k q) -> p k q", k=2)[:, :, 0:SLOTS],
                                           ACT.Copy).then_inc(hte, 1)

                        def y_out(i, v, j):
                            act.wait_ge(yp, v + CREDIT)
                            if not (rnd is FIRST and i is FIRST):
                                act.wait_ge(sdma[j], 16 * (rnd * TURNS + i))
                            act.activation(ye[:, j, :], bank[6 + j % 2][:, :], ACT.Copy).then_inc(yev, 1)

                        def turn(i):
                            for j in range(UNROLL):
                                v = rnd * EXP + i * UNROLL + j + 1
                                last = i if j else i - 1
                                before = j > 0 or i is not FIRST
                                gu_half(v, j)
                                if before:
                                    hT_out(v - 1, (j - 1) % UNROLL)
                                xT_out(i, j + 1)
                                silu_tanh(v, j)
                                if before:
                                    y_out(last, v - 1, (j - 1) % UNROLL)

                        xT_out(0, 0)
                        turn(FIRST)
                        with act.Fori(1, TURNS) as i:
                            turn(i)
                        hT_out((rnd + 1) * EXP, UNROLL - 1)
                        y_out(TURNS - 1, (rnd + 1) * EXP, UNROLL - 1)

                    act.wait_ge(counts_ok, 1)
                    most = act.value_load(cmax[0:1, 0:1], min_val=0, max_val=T)
                    act.wait_ge(gath_ok, 2)
                    turns(FIRST)
                    with act.If(most > SLOTS):
                        with act.Fori(1, ROUNDS) as rnd:
                            with act.If(most > rnd * SLOTS):
                                turns(rnd)

                @block.tensor
                def _(pe):
                    pe.wait_ge(rows_ld, 96 * (l + 1))
                    pe.sem_inc(pe_passed, 1)
                    pe.transpose(bank[7][:, 0:27], colrows[0:27, :], ident[0:27, 0:27]).then_inc(cols_ps, 1)
                    for i in range(2 * TT):
                        tt, kh = divmod(i, 2)
                        pe.wait_ge(xn_ok, tt + 1)
                        if i == 7:
                            pe.wait_ge(cols_ok, 1)
                        for k in range(4):
                            ins = pe.transpose(bank[i][:, k * P:(k + 1) * P],
                                               xn[:, tt, (4 * kh + k) * P:(4 * kh + k + 1) * P], ident)
                        ins.then_inc(hT_ps, 1)

                    def project(i):
                        c, tt = divmod(i, TT)
                        n = 160 if c == 2 else 512
                        w = slot(c, KD * n).rearrange("p (k n) -> p k n", k=KD)
                        if c == 2 and tt == 0:
                            pe.wait_ge(w_in_dma["c2"], 48)
                        if i >= 4:
                            pe.wait_ge(pj_act, i - 3)
                            pe.wait_ge(pj_dve, i - 3)
                        ts = slice(tt * P, (tt + 1) * P)
                        if c == 2:
                            for k in range(KD):
                                ins = pe.matmul(bank[i % 4][:, 0:n], hT[:, k, ts], w[:, k, :],
                                                start=k == 0, stop=k == KD - 1)
                        else:
                            if c == 0:
                                pe.wait_ge(hT_h, 2 * (tt + 1))
                                pe.wait_ge(hT_l, 2 * (tt + 1))
                            w_h, w_l = ((c0_h, c0_l), (c1_h, c1_l))[c]
                            for k in range(KD):
                                if tt == 0:
                                    pe.wait_ge(w_h, k + 1)
                                pe.matmul(bank[i % 4][:, :], hT_hi[:, k, ts], c_hi[c][:, k, :], start=k == 0, stop=False)
                                pe.matmul(bank[i % 4][:, :], hT_lo[:, k, ts], c_hi[c][:, k, :], start=False, stop=False)
                            for k in range(KD):
                                if tt == 0:
                                    pe.wait_ge(w_l, k + 1)
                                ins = pe.matmul(bank[i % 4][:, :], hT_hi[:, k, ts], c_lo[c][:, k, :],
                                                start=False, stop=k == KD - 1)
                        ins.then_inc(pj, 1)

                    def project_T(i):
                        c, tt = divmod(i, TT)
                        pe.wait_ge(qn_ok, i + 1)
                        if i >= 2:
                            pe.wait_ge(tp_read, i - 1)
                        b = bank[4 + i % 2]
                        q = qn[:, i % 2, :]
                        for j in range((4, 3, 1)[c]):
                            ins = pe.transpose(b[:, j * P:(j + 1) * P], q[:, j * P:(j + 1) * P], ident)
                        ins.then_inc(tpj, 1)

                    for i in range(3 * TT):
                        if i == 2:
                            pe.wait_ge(hT_ok, 8)
                        project(i)
                        if i >= 2:
                            project_T(i - 2)
                    project_T(3 * TT - 2)
                    project_T(3 * TT - 1)

                    wqb = slot(2, 2 * BH * QK, 1280).rearrange("p (k n) -> p k n", k=2)
                    wkv = slot(2, 1024, 2816)

                    def mla(tt):
                        if tt == 0:
                            pe.wait_ge(tp_read, 12)
                            pe.wait_ge(pj_act, 12)
                            pe.wait_ge(pj_dve, 12)
                        else:
                            pe.wait_ge(p2_act, tt)
                            pe.wait_ge(p2_dve, tt)
                        for b in range(2):
                            for k in range(2):
                                pe.matmul(bank[b][:, 0:4 * QK], cqT[:, k, tt * P:(tt + 1) * P],
                                          wqb[:, k, b * 4 * QK:(b + 1) * 4 * QK], start=k == 0, stop=k == 1)
                        for b in range(2):
                            ins = pe.matmul(bank[2 + b][:, :], ckvT[:, tt * P:(tt + 1) * P],
                                            wkv[:, b * 512:(b + 1) * 512], start=True, stop=True)
                        ins.then_inc(p2, 1)

                    def mla_T(tt):
                        pe.wait_ge(p2_rope, tt + 1)
                        for b in range(4):
                            t = 4 * tt + b
                            if t >= 3:
                                pe.wait_ge(p2_te, t - 2)
                            for h in range(4):
                                ins = pe.transpose(bank[4 + t % 3][0:QK, h * P:(h + 1) * P],
                                                   qk[:, tt % 2, 4 * b + h, :], ident)
                            ins.then_inc(p2_tp, 1)

                    def gate_matmul(i):
                        q, k = divmod(i, KD)
                        slot_, col, _, _, _, b = gate_job(q)
                        if q % 4 == 0 and k == 0:
                            pe.wait_ge(w_in_dma[("g0", "g2", "g1", "g3")[q // 4]], 16)
                        if k == 0:
                            if q == MLA_JOBS:
                                pe.wait_ge(p2_te, 16)
                            elif q > MLA_JOBS:
                                pe.wait_ge(ge, q - 1)
                            elif q > 0:
                                pe.wait_ge(ge, q)
                        w = slot(slot_).rearrange("p (k n) -> p k n", k=KD)
                        ins = pe.matmul(b[:, :], w[:, k, col:col + P], hT[:, k, :],
                                        start=k == 0, stop=k == KD - 1)
                        if k == KD - 1:
                            ins.then_inc(gates_ps, 1)

                    def gate(q):
                        for k in range(KD):
                            gate_matmul(q * KD + k)

                    mla(0)
                    mla(1)
                    gate(0)
                    mla_T(0)
                    mla(2)
                    gate(1)
                    mla_T(1)
                    mla(3)
                    gate(2)
                    gate(3)
                    mla_T(2)
                    mla_T(3)

                    def scores(u):
                        kind, a, b_, c_ = UNITS[u]
                        if u < 3:
                            pe.wait_ge(p2_act, 4)
                            pe.wait_ge(p2_dve, 4)
                        else:
                            pe.wait_ge(ex, u - 2)
                        if u == 0:
                            pe.wait_ge(tp_read, 12)
                        b = bank[u % 3]
                        if kind == "A":
                            n, g, jj = a, b_, c_
                            w = P if n == 0 else 2 * P
                            k0 = max(n - 1, 0) * P
                            for hh in range(2):
                                ins = pe.matmul(b[:, hh * w:(hh + 1) * w],
                                                qTA[g * AD:(g + 1) * AD, 2 * jj + hh, n * P:(n + 1) * P],
                                                kTA[g * AD:(g + 1) * AD, k0:k0 + w], start=True, stop=True)
                            ins.then_inc(sc, 1)
                        else:
                            h, n = a, b_
                            if u == 16:
                                pe.wait_ge(p2_te, 16)
                            w = P * (n + 1)
                            pe.matmul(b[:, 0:w], qkT[0:QK, h, n * P:(n + 1) * P], qkT[0:QK, BH + h, 0:w],
                                      start=True, stop=False)
                            pe.matmul(b[:, n * P:w], ident_bf[:, :], causal_bf[:, :],
                                      start=False, stop=True).then_inc(sc, 1)

                    def transposes(u):
                        kind, a, b_, c_ = UNITS[u]
                        pe.wait_ge(pn, u + 1)
                        if u < 2:
                            pe.wait_ge(p2_te, 16)
                        else:
                            pe.wait_ge(te, u - 1)
                        b = bank[3 + u % 2]
                        if kind == "A":
                            nk = 1 if a == 0 else 2
                            for kb in range(nk):
                                for hh in range(2):
                                    ins = pe.transpose(b[:, (kb * 2 + hh) * P:(kb * 2 + hh + 1) * P],
                                                       pr[:, u % 4, (hh * nk + kb) * P:(hh * nk + kb + 1) * P], ident)
                        else:
                            for kb in range(b_ + 1):
                                ins = pe.transpose(b[:, kb * P:(kb + 1) * P], pr[:, u % 4, kb * P:(kb + 1) * P], ident)
                        ins.then_inc(tp, 1)

                    def values(u):
                        kind, a, b_, c_ = UNITS[u]
                        G = GROUP_OF[u]
                        pe.wait_ge(te, u + 1)
                        if (u == 0 or GROUP_OF[u - 1] != G):
                            if G >= 1:
                                pe.wait_ge(oe, G)
                            else:
                                pe.wait_ge(p2_te, 16)
                        o = bank[5]
                        if kind == "A":
                            n, g, jj = a, b_, c_
                            kbs = [n] if n == 0 else [n - 1, n]
                            for x_, kb in enumerate(kbs):
                                ins = pe.matmul(o[g * AD:(g + 1) * AD, jj * 2 * P:(jj + 1) * 2 * P],
                                                vA[:, kb, g * AD:(g + 1) * AD],
                                                pT[:, u % 4, x_ * 2 * P:(x_ + 1) * 2 * P],
                                                start=x_ == 0, stop=x_ == len(kbs) - 1)
                        else:
                            h, n = a, b_
                            for kb in range(n + 1):
                                ins = pe.matmul(o[(h % 2) * VD:(h % 2 + 1) * VD, n * P:(n + 1) * P],
                                                vB[:, kb, h * VD:(h + 1) * VD], pT[:, u % 4, kb * P:(kb + 1) * P],
                                                start=kb == 0, stop=kb == n)
                        ins.then_inc(pvu, 1)
                        if LAST_OF[u]:
                            pe.wait_ge(pvu, u + 1)
                            pe.sem_inc(pv, 1)

                    done = MLA_JOBS * KD
                    for s in range(STEPS):
                        for part in range(3):
                            if part == 0 and s < NU:
                                scores(s)
                            if part == 1 and 0 <= s - 2 < NU:
                                transposes(s - 2)
                            if part == 2 and 0 <= s - 3 < NU:
                                values(s - 3)
                            before = GATE_DONE[s - 1] if s else 0
                            until = before + -(-(GATE_DONE[s] - before) * (part + 1) // 3)
                            while done < until:
                                gate_matmul(done)
                                done += 1

                    def three_passes(out_, w_hi, w_lo, x_hi, x_lo, first, last):
                        pe.matmul(out_, w_hi, x_hi, start=first, stop=False)
                        pe.matmul(out_, w_hi, x_lo, start=False, stop=False)
                        return pe.matmul(out_, w_lo, x_hi, start=False, stop=last)

                    for m in range(KD):
                        if m == 0:
                            pe.wait_ge(te, NU)
                            pe.wait_ge(oe, 8)
                            pe.wait_ge(ge, JOBS)
                        if m >= 2:
                            pe.wait_ge(mg, m - 1)
                        pe.wait_ge(wab_h, m + 1)
                        pe.wait_ge(wab_l, m + 1)
                        for z in range(2):
                            for k in range(4):
                                if m == 0:
                                    pe.wait_ge(oab_h, 4 * z + k + 1)
                                    pe.wait_ge(oab_l, 4 * z + k + 1)
                                ins = three_passes(bank[4 + 2 * (m % 2) + z][:, :],
                                                   wab_hi[:, m % 2, z, k, :], wab_lo[z][:, k, m * P:(m + 1) * P],
                                                   oab_hi[:, z, k, :], oab_lo[:, z, k, :], k == 0, k == 3)
                        ins.then_inc(y_ps, 1)

                    def mixed(i):
                        nh, tt = divmod(i, TT)
                        if i == 0:
                            pe.wait_ge(ex, NU)
                        ts = slice(tt * P, (tt + 1) * P)
                        for k in range(KD):
                            if i == 0:
                                pe.wait_ge(mg, k + 1)
                            if tt == 0:
                                pe.wait_ge(wo_h[nh], k + 1)
                                pe.wait_ge(wo_l[nh], k + 1)
                            ins = three_passes(bank[i][:, :], mT_hi[k // 4][:, k % 4, 0, ts], mT_lo[:, k, ts],
                                               wo_hi[nh][:, k, :], wo_lo[nh][:, k, :], k == 0, k == KD - 1)
                        ins.then_inc(wo_ps, 1)

                    def h2_T(tt):
                        pe.wait_ge(h2_ok, tt + 1)
                        for b in range(2):
                            if tt >= 2:
                                pe.wait_ge(h2T_ok, 2 * (tt - 2) + b + 1)
                            for k in range(4):
                                ins = pe.transpose(bank[2 * (tt % 2) + b][:, k * P:(k + 1) * P],
                                                   h2[:, tt, (4 * b + k) * P:(4 * b + k + 1) * P], ident)
                            ins.then_inc(h2t_ps, 1)

                    def logits(tt):
                        if tt == 0:
                            pe.wait_ge(late_ld, 48)
                            pe.wait_ge(xw, 5)
                        pe.wait_ge(h2T_ok, 2 * tt + 2)
                        for k in range(KD):
                            ins = pe.matmul(bank[4][:, tt * 36:(tt + 1) * 36], hT[:, k, tt * P:(tt + 1) * P],
                                            wr[:, k, :], start=k == 0, stop=k == KD - 1)
                        ins.then_inc(lg_ps, 1)

                    for i in range(TT + 2):
                        mixed(i)
                    h2_T(0)
                    mixed(TT + 2)
                    logits(0)
                    h2_T(1)
                    mixed(TT + 3)
                    logits(1)
                    for tt in range(2, TT):
                        h2_T(tt)
                        logits(tt)

                    pe.wait_ge(onehots, 1)
                    cnt = rt[:, 1024:1024 + TT * EXP // 2].bitcast(BF16)
                    pe.matmul(bank[7][:, 0:TT * EXP], before_bf[:, :], cnt, start=True, stop=False, skip_group_check=True)
                    for s in range(1, TT):
                        pe.matmul(bank[7][:, s * EXP:TT * EXP], ones_bf[:, :], cnt[:, 0:(TT - s) * EXP],
                                  start=False, stop=s == TT - 1, skip_group_check=True)
                    for s in range(TT):
                        ins = pe.matmul(bank[5][:, 0:EXP], ones_bf[:, :], cnt[:, s * EXP:(s + 1) * EXP],
                                        start=s == 0, stop=s == TT - 1)
                    ins.then_inc(ranks_ps, 1)

                    for s in (xtp, gu, htp, yp):
                        pe.sem_inc(s, CREDIT)
                    pe.wait_ge(counts_ok, 1)

                    def slot_table(rnd):
                        pe.wait_ge(srow_ok, 2 * TT * (rnd + 1))
                        if rnd is not FIRST:
                            pe.wait_ge(yev, rnd * EXP + CREDIT)
                        for c in range(2 * TT):
                            k, tt = divmod(c, TT)
                            ins = pe.matmul(bank[6][:, 0:EXP], slot_rows[:, k, tt, :], hot2[:, k, tt, :],
                                            start=c == 0, stop=c == 2 * TT - 1)
                        ins.then_inc(tbl_ps, 1)

                    def turns(rnd):
                        def x_T(i, j):
                            v = rnd * XPER + i * UNROLL + j + 1
                            pe.wait_ge(gdma[j % UNROLL], 16 * (rnd * (TURNS + 1) + i + j // UNROLL + 1))
                            pe.wait_ge(xte, v + CREDIT - (1 if i is FIRST and j == 0 else 2))
                            g = gath[:, j % UNROLL, :].rearrange("s (p c) -> s c p", c=4)
                            for c in range(4):
                                ins = pe.transpose(bank[j % 2][:, c * P:(c + 1) * P], g[:, c, :], ident)
                            ins.then_inc(xtp, 1)

                        def gate_up(i, j):
                            v = rnd * EXP + i * UNROLL + j + 1
                            pe.wait_ge(wload[j], 48 * (rnd * TURNS + i + 1))
                            pe.wait_ge(xte, rnd * XPER + i * UNROLL + j + 1 + CREDIT)
                            pe.wait_ge(gsm, v + CREDIT - 2)
                            w = ring[:, EXP_OFF[j]:EXP_OFF[j] + 4096].rearrange("p (z k f) -> p k z f", z=2, k=8)
                            for c in range(4):
                                for n in range(2):
                                    ins = pe.matmul(bank[2 + j % 2][n * SLOTS:(n + 1) * SLOTS, :],
                                                    xeT[:, j % 2, c, n * SLOTS:(n + 1) * SLOTS], w[:, n * 4 + c],
                                                    start=c == 0, stop=c == 3)
                            ins.then_inc(gu, 1)

                        def h_T(v, j):
                            pe.wait_ge(hh, v + CREDIT)
                            pe.wait_ge(hte, v + CREDIT - 2)
                            hv = hrow[:, j % 2, :].rearrange("s (p k) -> s k p", k=2)
                            for k in range(2):
                                ins = pe.transpose(bank[4 + j % 2][:, k * P:(k + 1) * P], hv[:, k, :], ident)
                            ins.then_inc(htp, 1)

                        def down(v, j):
                            pe.wait_ge(hte, v + CREDIT)
                            pe.wait_ge(yev, v + CREDIT - 2)
                            w = ring[:, EXP_OFF[j] + 4096:EXP_OFF[j] + 6144].rearrange("p (k n) -> p k n", k=2)
                            for k in range(2):
                                for n in range(2):
                                    ins = pe.matmul(bank[6 + j % 2][n * SLOTS:(n + 1) * SLOTS, :],
                                                    heT[:, j % 2, k, :], w[:, k, n * 512:(n + 1) * 512],
                                                    start=k == 0, stop=k == 1)
                            ins.then_inc(yp, 1)

                        def turn(i):
                            for j in range(UNROLL):
                                before = rnd * EXP + i * UNROLL + j
                                some = j > 0 or i is not FIRST
                                gate_up(i, j)
                                if some:
                                    h_T(before, (j - 1) % UNROLL)
                                x_T(i, j + 1)
                                if some:
                                    down(before, (j - 1) % UNROLL)

                        x_T(FIRST, 0)
                        turn(FIRST)
                        with pe.Fori(1, TURNS) as i:
                            turn(i)
                        h_T((rnd + 1) * EXP, UNROLL - 1)
                        down((rnd + 1) * EXP, UNROLL - 1)

                    most = pe.value_load(cmax[0:1, 0:1], min_val=0, max_val=T)
                    slot_table(FIRST)
                    turns(FIRST)
                    with pe.If(most > SLOTS):
                        with pe.Fori(1, ROUNDS) as rnd:
                            with pe.If(most > rnd * SLOTS):
                                slot_table(rnd)
                                turns(rnd)
                    pe.sem_inc(experts_done, 1)

                @block.vector
                def _(dve):
                    ch = Chain(dve, dch)
                    dve.wait_ge(cols_ps, 1)
                    ch.step(dve.tensor_copy(cols[:, 0:27], bank[7][:, 0:27]))
                    dve.tensor_scalar(hbg[:, :], cols[:, 8:24], 0.5, None, ALU.mult).then_inc(cols_ok, 1)

                    def x_norm(tt):
                        dve.wait_ge(rs_x, tt + 1)
                        dve.tensor_scalar(xn[:, tt, :], X[:, tt, :], stats[:, 4 + tt:5 + tt], None,
                                          ALU.mult).then_inc(xn_ok, 1)

                    def x_T(i):
                        tt, kh = divmod(i, 2)
                        dve.wait_ge(hT_ps, i + 1)
                        if i == 0:
                            dve.wait_ge(x_sq, 4)
                        dve.tensor_tensor(hT[:, 4 * kh:4 * kh + 4, tt * P:(tt + 1) * P],
                                          bank[i][:, :].rearrange("p (k q) -> p k q", k=4),
                                          cols[:, 4 * kh:4 * kh + 4].unsqueeze(2).broadcast_to([P, 4, P]),
                                          ALU.mult).then_inc(hT_ok, 1)

                    def x_lo(i):
                        tt, kh = divmod(i, 2)
                        v = slice(4 * kh, 4 * kh + 4), slice(tt * P, (tt + 1) * P)
                        dve.wait_ge(hT_h, i + 1)
                        dve.tensor_tensor(hT_lo[:, v[0], v[1]], hT[:, v[0], v[1]], hT_hi[:, v[0], v[1]].bitcast(F32),
                                          ALU.subtract).then_inc(hT_l, 1)

                    for tt in range(TT + 2):
                        if tt < TT:
                            x_norm(tt)
                        if 1 <= tt <= TT:
                            x_T(2 * tt - 2)
                            x_T(2 * tt - 1)
                        if tt >= 2:
                            x_lo(2 * tt - 4)
                            x_lo(2 * tt - 3)
                    def proj_norm(i):
                        c, tt = divmod(i, TT)
                        b, q = bank[i % 4], qn[:, i % 2, :]
                        dve.wait_ge(pj_act, i + 1)
                        if c < 2:
                            nh = AH if c == 0 else AKV
                            dve.tensor_reduce(st1[:, i, 0:nh], sq[:, i % 2, 0:nh * AD].rearrange("p (h d) -> p h d", h=nh),
                                              AX, ALU.add).then_inc(pj_ss, 1)
                        else:
                            dve.engine_nop().then_inc(pj_ss, 1)
                        dve.wait_ge(pj_rs, i + 1)
                        if i >= 2:
                            dve.wait_ge(tpj, i - 1)
                        r = st1[:, i, :]
                        if c == 0:
                            ch.step(dve.tensor_tensor(
                                q.rearrange("p (j g d) -> p g j d", g=2, d=AD),
                                b[:, :].rearrange("p (g j d) -> p g j d", g=2, d=AD),
                                r[:, 0:AH].rearrange("p (g j) -> p g j", g=2).unsqueeze(3).broadcast_to([P, 2, 4, AD]),
                                ALU.mult))
                            dve.sem_inc(pj_dve, 1)
                            qv = q.rearrange("p (h d) -> p h d", h=AH)
                            dve.tensor_tensor(qv, qv, gainA[:, 0, :].unsqueeze(1).broadcast_to([P, AH, AD]),
                                              ALU.mult).then_inc(qn_ok, 1)
                        elif c == 1:
                            ch.step(dve.tensor_tensor(
                                q[:, 0:P].rearrange("p (g d) -> p g d", g=AKV), b[:, 0:P].rearrange("p (g d) -> p g d", g=AKV),
                                r[:, 0:AKV].unsqueeze(2).broadcast_to([P, AKV, AD]), ALU.mult))
                            ch.step(dve.tensor_scalar(q[:, P:P + QL], b[:, 2 * P:2 * P + QL], r[:, 8:9], None, ALU.mult))
                            dve.sem_inc(pj_dve, 1)
                            kv = q[:, 0:P].rearrange("p (g d) -> p g d", g=AKV)
                            dve.tensor_tensor(kv, kv, gainA[:, 1, :].unsqueeze(1).broadcast_to([P, AKV, AD]),
                                              ALU.mult).then_inc(qn_ok, 1)
                        else:
                            ch.step(dve.tensor_scalar(q[:, 0:KVL], b[:, 0:KVL], r[:, 8:9], None, ALU.mult))
                            dve.sem_inc(pj_dve, 1)
                            dve.sem_inc(qn_ok, 1)

                    def proj_T(i):
                        c, tt = divmod(i, TT)
                        b = bank[4 + i % 2]
                        ts = slice(tt * P, (tt + 1) * P)
                        dve.wait_ge(tpj, i + 1)
                        if c == 0:
                            dve.tensor_copy(qTA[:, :, ts], b[:, :].rearrange("p (j q) -> p j q", j=4)).then_inc(tp_read, 1)
                        elif c == 1:
                            dve.tensor_copy(kTA[:, ts], b[:, 0:P])
                            ch.step(dve.tensor_tensor(cqT[:, :, ts], b[:, P:3 * P].rearrange("p (k q) -> p k q", k=2),
                                                      cols[:, 24:26].unsqueeze(2).broadcast_to([P, 2, P]), ALU.mult))
                            dve.sem_inc(tp_read, 1)
                        else:
                            dve.tensor_scalar(ckvT[:, ts], b[:, 0:P], cols[:, 26:27], None, ALU.mult).then_inc(tp_read, 1)

                    for i in range(3 * TT):
                        proj_norm(i)
                        if i >= 2:
                            proj_T(i - 2)
                    proj_T(3 * TT - 2)
                    proj_T(3 * TT - 1)

                    def q_rows(tt):
                        dve.wait_ge(p2, tt + 1)
                        if tt >= 2:
                            dve.wait_ge(p2_tp, 4 * (tt - 1))
                        for b in range(2):
                            ins = dve.tensor_copy(qk[:, tt % 2, 4 * b:4 * b + 4, :],
                                                  bank[b][:, 0:4 * QK].rearrange("p (h d) -> p h d", h=4))
                        ins.then_inc(p2_dve, 1)

                    def qk_sums(tt):
                        dve.wait_ge(p2_sq, tt + 1)
                        dve.tensor_reduce(st2(tt), sq2[:, :, :], AX,
                                          ALU.add).then_inc(p2_ss, 1)

                    def qk_norm(tt):
                        dve.wait_ge(p2_rs, tt + 1)
                        v = qk[:, tt % 2, :, :]
                        ch.step(dve.tensor_tensor(v, v, st2(tt).unsqueeze(2).broadcast_to([P, 2 * BH, QK]), ALU.mult))
                        v4 = v.rearrange("p (z h) d -> p z h d", z=2)
                        ch.step(dve.tensor_tensor(v4, v4, gainB[:, :, :].unsqueeze(2).broadcast_to([P, 2, BH, QK]),
                                                  ALU.mult))
                        hf = ROPE // 2
                        x1, x2 = v[:, :, NOPE:NOPE + hf], v[:, :, NOPE + hf:]
                        cb = cosv[:, tt, :].unsqueeze(1).broadcast_to([P, 2 * BH, hf])
                        sb = sinv[:, tt, :].unsqueeze(1).broadcast_to([P, 2 * BH, hf])
                        dve.tensor_tensor(rope_t[:, 0], x1, cb, ALU.mult)
                        dve.tensor_tensor(rope_t[:, 1], x2, sb, ALU.mult)
                        dve.tensor_tensor(rope_t[:, 2], x1, sb, ALU.mult)
                        ch.step(dve.tensor_tensor(rope_t[:, 3], x2, cb, ALU.mult))
                        dve.tensor_tensor(x1, rope_t[:, 0], rope_t[:, 1], ALU.subtract)
                        dve.tensor_tensor(x2, rope_t[:, 2], rope_t[:, 3], ALU.add).then_inc(p2_rope, 1)

                    def st2(tt):
                        return st1[:, :, :].rearrange("p a b -> p (a b)")[:, 16 * tt:16 * tt + 16]

                    dve.wait_ge(small_ld, 16 * 5)
                    ch.step(dve.tensor_scalar(nsink[:, :], nsink[:, :], -1.0, None, ALU.mult))
                    q_rows(0)
                    qk_sums(0)
                    q_rows(1)
                    qk_norm(0)
                    qk_sums(1)
                    qk_norm(1)
                    q_rows(2)
                    qk_sums(2)
                    q_rows(3)
                    qk_norm(2)
                    qk_sums(3)
                    qk_norm(3)

                    def maxima(u):
                        kind, a, b_, c_ = UNITS[u]
                        dve.wait_ge(sc, u + 1)
                        if kind == "A":
                            n, g, jj = a, b_, c_
                            if u == 0:
                                dve.wait_ge(p2_tp, 16)
                                dve.wait_ge(bias_ld, 16)
                            if u >= 4:
                                dve.wait_ge(tp, u - 3)
                            w = P if n == 0 else 2 * P
                            h0 = 4 * g + 2 * jj
                            s = pr[:, u % 4, 0:2 * w].rearrange("p (h k) -> p h k", h=2)
                            ch.step(dve.scalar_tensor_tensor(s, bank[u % 3][:, 0:2 * w].rearrange("p (h k) -> p h k", h=2),
                                                             A_SCALE, bias[:, h0:h0 + 2, 2 * P - w:2 * P], ALU.mult, ALU.add))
                            ch.step(dve.tensor_reduce(unit[:, u, 4:6], s, AX, ALU.max))
                            ch.step(dve.scalar_tensor_tensor(unit[:, u, 0:2], unit[:, u, 4:6], -1.0, nsink[:, h0:h0 + 2],
                                                             ALU.mult, ALU.min))
                            dve.tensor_tensor(unit[:, u, 2:4], unit[:, u, 0:2], nsink[:, h0:h0 + 2],
                                              ALU.subtract).then_inc(mx, 1)
                        else:
                            w = P * (b_ + 1)
                            ch.step(dve.tensor_reduce(unit[:, u, 1:2], bank[u % 3][:, 0:w], AX, ALU.max))
                            dve.tensor_scalar(unit[:, u, 0:1], unit[:, u, 1:2], -B_SCALE, None, ALU.mult).then_inc(mx, 1)

                    def normalise(u):
                        kind, a, b_, c_ = UNITS[u]
                        dve.wait_ge(ex, u + 1)
                        if kind == "A":
                            w = P if a == 0 else 2 * P
                            ch.step(dve.tensor_tensor(unit[:, u, 4:6], unit[:, u, 4:6], unit[:, u, 6:8], ALU.add))
                            ch.step(dve.reciprocal(unit[:, u, 2:4], unit[:, u, 4:6]))
                            s = pr[:, u % 4, 0:2 * w].rearrange("p (h k) -> p h k", h=2)
                            dve.tensor_tensor(s, s, unit[:, u, 2:4].unsqueeze(2).broadcast_to([P, 2, w]),
                                              ALU.mult).then_inc(pn, 1)
                        else:
                            w = P * (b_ + 1)
                            ch.step(dve.reciprocal(unit[:, u, 2:3], unit[:, u, 4:5]))
                            dve.tensor_scalar(pr[:, u % 4, 0:w], pr[:, u % 4, 0:w], unit[:, u, 2:3], None,
                                              ALU.mult).then_inc(pn, 1)

                    oab_done = 0

                    def oab_rest():
                        nonlocal oab_done
                        z, k = divmod(oab_done, 4)
                        dve.wait_ge(oab_h, oab_done + 1)
                        dve.tensor_tensor(oab_lo[:, z, k, :], oab[:, z, k, :], oab_hi[:, z, k, :].bitcast(F32),
                                          ALU.subtract).then_inc(oab_l, 1)
                        oab_done += 1

                    for s in range(STEPS + 1):
                        if s < NU:
                            maxima(s)
                        if 1 <= s <= NU:
                            normalise(s - 1)
                        for _ in range(2):
                            if s > GATES_END + 2 and oab_done < 7:
                                oab_rest()
                    while oab_done < 8:
                        oab_rest()

                    for m in range(KD):
                        s = gate_t[m // 4][:, m % 4, :, :]
                        b0 = 4 + 2 * (m % 2)
                        if m % 4 == 0:
                            dve.wait_ge(ge, JOBS if m else JOBS // 2)
                        dve.wait_ge(y_ps, m + 1)
                        for z in range(2):
                            ins = dve.scalar_tensor_tensor(s[:, z], s[:, z], 1.0, bank[b0 + z][:, :], ALU.add, ALU.mult)
                        ch.step(ins)
                        if m == 0:
                            dve.wait_ge(pvu, NU)
                        hi = mT_hi[m // 4][:, m % 4, 0, :]
                        ch.step(dve.tensor_tensor(s[:, 1], s[:, 0], s[:, 1], ALU.add))
                        ch.step(dve.tensor_scalar(hi, s[:, 1], 0.5, None, ALU.mult))
                        dve.scalar_tensor_tensor(mT_lo[:, m, :], s[:, 1], 0.5, hi.bitcast(F32), ALU.mult,
                                                 ALU.subtract).then_inc(mg, 1)
                    def xmix(i):
                        nh, tt = divmod(i, TT)
                        dve.wait_ge(wo_ps, i + 1)
                        xv = X[:, tt, nh * 512:(nh + 1) * 512]
                        dve.tensor_tensor(xv, bank[i][:, :], xv, ALU.add).then_inc(xw, 1)

                    def h_norm(tt):
                        dve.wait_ge(f_rs, tt + 1)
                        dve.scalar_tensor_tensor(h2[:, tt, :], X[:, tt, :], stats[:, 12 + tt:13 + tt], gffn[:, :],
                                                 ALU.mult, ALU.mult).then_inc(h2_ok, 1)

                    for i in range(TT):
                        xmix(i)
                    dve.wait_ge(late_ld, 48)
                    for tt in range(TT):
                        xmix(TT + tt)
                        if tt >= 1:
                            h_norm(tt - 1)
                    h_norm(TT - 1)
                    dve.wait_ge(wo_ps, 8)
                    dve.memset(gath[:, :, :], 0.0).then_inc(gath_ok, 1)
                    dve.memset(hrow[SLOTS:P, :, :], 0.0).then_inc(gath_ok, 1)
                    dve.wait_ge(lg_ps, TT)

                    used = [40]

                    def tmp(*shape):
                        n = 1
                        for d_ in shape:
                            n *= d_
                        a = used[0]
                        used[0] += n
                        assert used[0] <= 1024
                        v = rt[:, a:a + n]
                        if len(shape) == 2:
                            v = v.rearrange("p (a b) -> p a b", b=shape[1])
                        if len(shape) == 3:
                            v = v.rearrange("p (a b c) -> p a b c", b=shape[1], c=shape[2])
                        return v

                    def bc(v, *shape):
                        return v.broadcast_to([P, *shape])

                    lg = tmp(TT, GROUPS + EXP)
                    ch.step(dve.tensor_tensor(lg, bank[4][:, 0:TT * 36].rearrange("p (t c) -> p t c", t=TT),
                                              bc(rbias[:, :].unsqueeze(1), TT, 36), ALU.add))

                    def argmax(v, n, iota, d):
                        m = tmp(TT, 1)
                        ch.step(dve.tensor_reduce(m[:, :, 0], v, AX, ALU.max))
                        ch.step(dve.tensor_tensor(d, v, bc(m, TT, n), ALU.subtract))
                        t = tmp(TT, n)
                        ch.step(dve.tensor_scalar(t, d, 0.0, -64.0, ALU.is_ge, ALU.mult))
                        ch.step(dve.tensor_tensor(t, t, bc(iota.unsqueeze(1), TT, n), ALU.add))
                        first = tmp(TT, 1)
                        ch.step(dve.tensor_reduce(first[:, :, 0], t, AX, ALU.min))
                        one = tmp(TT, n)
                        ch.step(dve.tensor_tensor(one, t, bc(first, TT, n), ALU.is_equal))
                        return m, one

                    gd = rt[:, 0:16].rearrange("p (t c) -> p t c", t=TT)
                    _, og = argmax(lg[:, :, 0:GROUPS], GROUPS, C("iota4"), gd)
                    dve.engine_nop().then_inc(r_exp_in, 1)
                    pick = tmp(TT, EXP)
                    pick4 = pick.rearrange("p t (g e) -> p t g e", g=GROUPS)
                    el = tmp(TT, PER_GROUP)
                    ch.step(dve.tensor_tensor(pick4, lg[:, :, GROUPS:].rearrange("p t (g e) -> p t g e", g=GROUPS),
                                              bc(og.unsqueeze(3), TT, GROUPS, PER_GROUP), ALU.mult))
                    ch.step(dve.tensor_reduce(el, pick4.rearrange("p t g e -> p t e g"), AX, ALU.add))
                    e1d, e2d = tmp(TT, PER_GROUP), tmp(TT, PER_GROUP)
                    m1, o1 = argmax(el, PER_GROUP, C("iota8"), e1d)
                    ch.step(dve.scalar_tensor_tensor(el, o1, NEG, el, ALU.mult, ALU.add))
                    m2, o2 = argmax(el, PER_GROUP, C("iota8"), e2d)
                    dm = rt[:, 32:36]
                    dve.tensor_tensor(dm, m2[:, :, 0], m1[:, :, 0], ALU.subtract).then_inc(r_exp_in, 1)
                    for k_, o_ in enumerate((o1, o2)):
                        ins = dve.tensor_tensor(hot2[:, k_].rearrange("p t (g e) -> p t g e", g=GROUPS),
                                                bc(og.unsqueeze(3), TT, GROUPS, PER_GROUP),
                                                bc(o_.unsqueeze(2), TT, GROUPS, PER_GROUP), ALU.mult)
                    ch.step(ins)
                    cnt = rt[:, 1024:1024 + TT * EXP // 2].bitcast(BF16).rearrange("p (t e) -> p t e", t=TT)
                    dve.tensor_tensor(cnt, hot2[:, 0], hot2[:, 1], ALU.add).then_inc(onehots, 1)
                    dve.wait_ge(r_exp_out, 2)
                    gsum_, gp, den = tmp(TT), tmp(TT), tmp(TT)
                    ch.step(dve.tensor_reduce(gsum_, rt[:, 16:32].rearrange("p (t c) -> p t c", t=TT), AX, ALU.add))
                    ch.step(dve.reciprocal(gp, gsum_))
                    ch.step(dve.tensor_scalar(den, rt[:, 36:40], 1.0, None, ALU.add))
                    ch.step(dve.reciprocal(den, den))
                    ch.step(dve.tensor_tensor(wts[:, 0, :], gp, den, ALU.mult))
                    dve.tensor_tensor(wts[:, 1, :], wts[:, 0, :], rt[:, 36:40], ALU.mult)
                    dve.wait_ge(ranks_ps, 1)
                    mxc = tmp(1)
                    ch.step(dve.tensor_reduce(mxc, bank[5][:, 0:EXP], AX, ALU.max))
                    dve.tensor_copy(cmax[:, :], mxc).then_inc(counts_ok, 1)
                    mine = tmp(2, TT * EXP)
                    ch.step(dve.tensor_tensor(mine, hot2[:, :, :, :].rearrange("p k t e -> p k (t e)"),
                                              bc(bank[7][:, 0:TT * EXP].unsqueeze(1), 2, TT * EXP), ALU.mult))
                    ch.step(dve.tensor_reduce(rank[:, :, :], mine.rearrange("p k (t e) -> p k t e", t=TT), AX, ALU.add))

                    for s in (gsm, silu2, hh):
                        dve.sem_inc(s, CREDIT)

                    def indices(rnd):
                        steps = rnd * 5
                        if rnd is FIRST:
                            dve.sem_inc(idx_ok, 1)
                        else:
                            dve.wait_ge(round_done, rnd)
                            dve.tensor_scalar(rank[:, :, :], rank[:, :, :], float(-SLOTS), None, ALU.add).then_inc(idx_ok, 1)
                            dve.wait_ge(idx_ok, steps + 1)
                        for k in range(2):
                            for tt in range(TT):
                                r = CONST["rowid"][0] + 2 * tt + k
                                dve.tensor_scalar(slot_rows[:, k, tt, :], C("iota_slot"), rank[:, k, tt:tt + 1],
                                                  cst[:, r:r + 1], ALU.is_equal, ALU.mult).then_inc(srow_ok, 1)
                        g, s = idx_g[:, 0:EXP], idx_s[:, 0:EXP]
                        dve.wait_ge(tbl_ps, rnd + 1)
                        dve.tensor_scalar(s, bank[6][:, 0:EXP], float(PAD), None, ALU.add).then_inc(idx_ok, 1)
                        dve.wait_ge(idx_ok, steps + 2)
                        dve.tensor_scalar(g, s, -2, None, ALU.bitwise_and).then_inc(idx_ok, 1)
                        dve.wait_ge(idx_ok, steps + 3)
                        dve.tensor_scalar(g, g, C("half"), None, ALU.add).then_inc(idx_ok, 1)
                        dve.tensor_scalar(s, s, 2.0, C("half"), ALU.mult, ALU.add).then_inc(idx_ok, 1)

                    def turns(rnd):
                        with dve.Fori(0, TURNS) as i:
                            for j in range(UNROLL):
                                v = rnd * EXP + i * UNROLL + j + 1
                                r = gu_rows[j % 2]
                                e, h = gexp[0:SLOTS, j % 2, :], hrow[0:SLOTS, j % 2, :]
                                dve.wait_ge(gcp, v + CREDIT)
                                dve.wait_ge(hh, v + CREDIT - 2)
                                dve.tensor_tensor(r[0:SLOTS, :], bank[2 + j % 2][0:SLOTS, :], gtmp[0:SLOTS, j % 2, :],
                                                  ALU.add).then_inc(gsm, 1)
                                dve.wait_ge(gex, v + CREDIT)
                                dve.scalar_tensor_tensor(e, e, 1.0, r[0:SLOTS, 0:FE], ALU.add, ALU.mult).then_inc(silu2, 1)
                                dve.wait_ge(silu2, v + CREDIT)
                                dve.wait_ge(htp, v + CREDIT - 2)
                                dve.scalar_tensor_tensor(h, e, 0.5, r[0:SLOTS, FE:2 * FE], ALU.mult,
                                                         ALU.mult).then_inc(hh, 1)

                    indices(0)
                    most = dve.value_load(cmax[0:1, 0:1], min_val=0, max_val=T)
                    turns(0)
                    with dve.If(most > SLOTS):
                        with dve.Fori(1, ROUNDS) as rnd:
                            with dve.If(most > rnd * SLOTS):
                                indices(rnd)
                                turns(rnd)

                    for tt in range(TT):
                        dve.wait_ge(yl[tt], 16)
                        yv = yld[:, tt]
                        ch.step(dve.scalar_tensor_tensor(X[:, tt, :], yv[:, 0, :], wts[:, 0, tt:tt + 1], X[:, tt, :],
                                                         ALU.mult, ALU.add))
                        dve.scalar_tensor_tensor(X[:, tt, :], yv[:, 1, :], wts[:, 1, tt:tt + 1], X[:, tt, :],
                                                 ALU.mult, ALU.add).then_inc(comb, 1)

                @block.gpsimd
                def _(pool):
                    ch = Chain(pool, pch)

                    def rstd(dst, src, n, width):
                        ch.step(pool.tensor_scalar(dst, src, 1.0 / width, EPS, ALU.mult, ALU.add))
                        return pool.tensor_tensor(dst, dst, minus_half[:, 0:n], ALU.pow)

                    for tt in range(TT):
                        pool.wait_ge(x_sq, tt + 1)
                        rstd(stats[:, 4 + tt:5 + tt], stats[:, tt:tt + 1], 1, D).then_inc(rs_x, 1)
                    def chunk_lo(c, k):
                        pool.wait_ge((c0_h, c1_h)[c], k + 1)
                        pool.tensor_tensor(c_lo[c][:, k, :], slot(c)[:, k * 512:(k + 1) * 512],
                                           c_hi[c][:, k, :].bitcast(F32), ALU.subtract).then_inc((c0_l, c1_l)[c], 1)

                    for k in range(KD):
                        chunk_lo(0, k)
                    for i in range(3 * TT):
                        c = i // TT
                        if i < TT:
                            chunk_lo(1, 2 * i)
                            chunk_lo(1, 2 * i + 1)
                        pool.wait_ge(pj_act, i + 1)
                        pool.wait_ge(pj_ss, i + 1)
                        r = st1[:, i, :]
                        if c == 0:
                            rstd(r[:, 0:8], r[:, 0:8], 8, AD).then_inc(pj_rs, 1)
                        elif c == 1:
                            rstd(r[:, 0:2], r[:, 0:2], 2, AD)
                            rstd(r[:, 8:9], r[:, 8:9], 1, QL).then_inc(pj_rs, 1)
                        else:
                            rstd(r[:, 8:9], r[:, 8:9], 1, KVL).then_inc(pj_rs, 1)
                    for tt in range(TT):
                        pool.wait_ge(p2_ss, tt + 1)
                        r = st1[:, :, :].rearrange("p a b -> p (a b)")[:, 16 * tt:16 * tt + 16]
                        rstd(r, r, 16, QK).then_inc(p2_rs, 1)

                    for m in range(KD):
                        pool.wait_ge(wab_h, m + 1)
                        for z in range(2):
                            ins = pool.tensor_tensor(wab_lo[z][:, :, m * P:(m + 1) * P], wab_tile(z, m),
                                                     wab_hi[:, m % 2, z, :, :].bitcast(F32), ALU.subtract)
                        ins.then_inc(wab_l, 1)
                        pool.wait_ge(wo_h[0], m + 1)
                        pool.tensor_tensor(wo_lo[0][:, m, :], wo_tile(0, m), wo_hi[0][:, m, :].bitcast(F32),
                                           ALU.subtract).then_inc(wo_l[0], 1)
                    for k in range(KD):
                        pool.wait_ge(wo_h[1], k + 1)
                        pool.tensor_tensor(wo_lo[1][:, k, :], wo_tile(1, k), wo_hi[1][:, k, :].bitcast(F32),
                                           ALU.subtract).then_inc(wo_l[1], 1)
                    for tt in range(TT):
                        pool.wait_ge(f_sq, tt + 1)
                        rstd(stats[:, 12 + tt:13 + tt], stats[:, 8 + tt:9 + tt], 1, D).then_inc(f_rs, 1)
                    def gather(e, j, use):
                        pool.tensor_copy(cur_g[:, j:j + 1], idx_g[:, bass.ds(e, 1)]).then_inc(cg, 1)
                        pool.wait_ge(cg, use)
                        pool.sem_inc(passed, 1)
                        pool.indirect_dma_start(gath[:, j, :], None, h_dram,
                                                bass.IndirectOffsetOnAxis(cur_g[:, j:j + 1], 0),
                                                bounds_check=2 * T - 1, oob_is_err=False).then_inc(gdma[j], 16)

                    def scatter(e, j, use):
                        pool.tensor_copy(cur_s[:, j:j + 1], idx_s[:, bass.ds(e, 1)]).then_inc(cs_, 1)
                        pool.wait_ge(cs_, use)
                        pool.sem_inc(passed, 1)
                        pool.indirect_dma_start(y_dram, bass.IndirectOffsetOnAxis(cur_s[:, j:j + 1], 0),
                                                ye[:, j, :], None, bounds_check=4 * T - 1,
                                                oob_is_err=False).then_inc(sdma[j], 16)

                    def turns(rnd):
                        first = rnd * (EXP + UNROLL)
                        if rnd is not FIRST:
                            pool.wait_ge(xtp, rnd * XPER + CREDIT)
                            pool.sem_inc(passed, 1)
                        for j in range(UNROLL):
                            gather(j, j, first + j + 1)

                        def ahead(i, j):
                            pool.wait_ge(xtp, rnd * XPER + i * UNROLL + j + 1 + CREDIT)
                            pool.sem_inc(passed, 1)
                            gather(i * UNROLL + j + UNROLL, j, first + UNROLL + i * UNROLL + j + 1)

                        def store(i, j):
                            pool.wait_ge(yev, rnd * EXP + i * UNROLL + j + 1 + CREDIT)
                            pool.sem_inc(passed, 1)
                            scatter(i * UNROLL + j, j, rnd * EXP + i * UNROLL + j + 1)

                        def turn(i):
                            for j in range(UNROLL):
                                ahead(i, j)
                                if j > 0:
                                    store(i, j - 1)
                                elif i is not FIRST:
                                    store(i - 1, UNROLL - 1)

                        turn(FIRST)
                        with pool.Fori(1, TURNS) as i:
                            turn(i)
                        store(TURNS - 1, UNROLL - 1)
                        for j in range(UNROLL):
                            pool.wait_ge(gdma[j], 16 * (rnd + 1) * (TURNS + 1))
                            pool.wait_ge(sdma[j], 16 * (rnd + 1) * TURNS)
                        pool.sem_inc(round_done, 1)

                    pool.wait_ge(counts_ok, 1)
                    most = pool.value_load(cmax[0:1, 0:1], min_val=0, max_val=T)
                    pool.wait_ge(idx_ok, 5)
                    pool.wait_ge(gath_ok, 2)
                    pool.wait_ge(h2_dma, 16 * TT)
                    turns(FIRST)
                    with pool.If(most > SLOTS):
                        with pool.Fori(1, ROUNDS) as rnd:
                            with pool.If(most > rnd * SLOTS):
                                pool.wait_ge(idx_ok, rnd * 5 + 5)
                                pool.sem_inc(passed, 1)
                                turns(rnd)
                    pool.sem_inc(moe_done, 1)
                    pool.dma_reset(sem_range)

            nc.all_engine_barrier(sems_to_clear=sem_range)


_INS = ["x", "attn_norm", "w_in", "b_gate", "a_q_norm", "a_k_norm", "a_sinks", "rel_bias", "w_oa",
        "q_a_norm", "w_qb", "kv_a_norm", "w_kvb", "b_q_norm", "b_k_norm", "w_ob", "w_o", "ffn_norm",
        "w_router_group", "b_router_group", "w_router_expert", "b_router_expert", "w_exp_gate",
        "w_exp_up", "w_exp_down"]


def kernel(**inputs):
    import concourse.bacc as bacc
    from concourse.bass_utils import run_bass_kernel_spmd

    nc = bacc.Bacc("TRN2", target_bir_lowering=False, num_devices=1)
    arrays = {name: np.ascontiguousarray(inputs[name]) for name in _INS}
    arrays["consts"], arrays["hot"] = constants()
    args = [nc.dram_tensor(f"{n}_dram", a.shape, mybir.dt.from_np(a.dtype), kind="ExternalInput").ap()
            for n, a in arrays.items()]
    out = nc.dram_tensor("out_dram", (1, T, D), F32, kind="ExternalOutput").ap()
    trunk(nc, *args, out)
    r = run_bass_kernel_spmd(nc, [{f"{n}_dram": a for n, a in arrays.items()}], core_ids=[0])
    return r.results[0]["out_dram"]
```
